# Optimizing a Trainium2 kernel written in Bass

```python
import math
import jax, jax.numpy as jnp
from jax import lax
import numpy as np

D_MODEL = 1024
BATCH = 1
SEQ = 1024
DEPTH = 1

N_MEM = 256
RET_HEADS = 4
RET_DV = D_MODEL // 2 // RET_HEADS
RET_DK = RET_DV // 2
RET_QK_W = RET_HEADS * RET_DK
RET_V_W = RET_HEADS * RET_DV
DIFF_HEADS = 4
DIFF_DH = D_MODEL // 2 // DIFF_HEADS // 2
DIFF_DV = 2 * DIFF_DH
DIFF_QK_W = DIFF_HEADS * 2 * DIFF_DH
DIFF_V_W = DIFF_HEADS * DIFF_DV
MIX_W = RET_V_W + DIFF_V_W
IN_COLS = 2 * RET_QK_W + 2 * RET_V_W + 2 * DIFF_QK_W + DIFF_V_W
XATTN_HEADS = 4
XATTN_DH = D_MODEL // XATTN_HEADS
D_FF = ((8 * D_MODEL // 3 + 127) // 128) * 128
RET_CHUNK = 128
Q_BLOCK = 128
ROPE_BASE = 10000.0
EPS = 1e-6


def rmsnorm(x, g):
    xf = x.astype(jnp.float32)
    y = xf * lax.rsqrt(jnp.mean(xf * xf, axis=-1, keepdims=True) + EPS)
    return (y * g.astype(jnp.float32)).astype(x.dtype)

def swiglu(h, w_gate, w_up, w_down):
    return (jax.nn.silu(h @ w_gate) * (h @ w_up)) @ w_down

def rotary(t, pos):
    d = t.shape[-1]
    inv = 1.0 / (ROPE_BASE ** (jnp.arange(0, d, 2, dtype=jnp.float32) / d))
    ang = pos.astype(jnp.float32)[:, None] * inv[None, :]
    cos = jnp.cos(ang)[None, :, None, :].astype(t.dtype)
    sin = jnp.sin(ang)[None, :, None, :].astype(t.dtype)
    t1, t2 = t[..., : d // 2], t[..., d // 2:]
    return jnp.concatenate([t1 * cos - t2 * sin, t1 * sin + t2 * cos], axis=-1)

def retention_chunkwise(q, k, v):
    B, S, H, dk = q.shape
    dv = v.shape[-1]
    C = RET_CHUNK
    NC = S // C
    log_g = jnp.log(1.0 - 2.0 ** (-5.0 - jnp.arange(H, dtype=jnp.float32)))
    n = jnp.arange(C, dtype=jnp.float32)
    rel = n[:, None] - n[None, :]
    decay = jnp.where(rel[None] >= 0, jnp.exp(jnp.maximum(rel, 0.0)[None] * log_g[:, None, None]), 0.0)
    xi = jnp.exp((n[None, :] + 1.0) * log_g[:, None])
    zeta = jnp.exp((C - 1.0 - n[None, :]) * log_g[:, None])
    g_chunk = jnp.exp(C * log_g)

    def to_chunks(t):
        return t.astype(jnp.float32).reshape(B, NC, C, H, t.shape[-1]).transpose(1, 0, 3, 2, 4)

    qc, kc, vc = to_chunks(q), to_chunks(k), to_chunks(v)

    def step(R, inp):
        qi, ki, vi = inp
        inner = jnp.einsum('bhnd,bhmd->bhnm', qi, ki) * decay[None]
        o = jnp.einsum('bhnm,bhme->bhne', inner, vi)
        o = o + jnp.einsum('bhnd,bhde->bhne', qi, R) * xi[None, :, :, None]
        R = g_chunk[None, :, None, None] * R + jnp.einsum('bhmd,bhme->bhde', ki * zeta[None, :, :, None], vi)
        return R, o

    R0 = jnp.zeros((B, H, dk, dv), jnp.float32)
    _, out = lax.scan(step, R0, (qc, kc, vc))
    return out.transpose(1, 0, 3, 2, 4).reshape(B, S, H, dv)

def diff_attention(q, k, v, lam):
    B, S, H, _, dh = q.shape
    NB = S // Q_BLOCK
    scale = 1.0 / math.sqrt(dh)
    qb = q.reshape(B, NB, Q_BLOCK, H, 2, dh).transpose(1, 0, 2, 3, 4, 5)
    kpos = jnp.arange(S)

    def block(args):
        qi, i = args
        s = jnp.einsum('bqhcd,bkhcd->bhcqk', qi, k).astype(jnp.float32) * scale
        qpos = i * Q_BLOCK + jnp.arange(Q_BLOCK)
        mask = kpos[None, :] <= qpos[:, None]
        s = jnp.where(mask[None, None, None], s, -jnp.inf)
        p = jax.nn.softmax(s, axis=-1)
        a = p[:, :, 0] - lam * p[:, :, 1]
        return jnp.einsum('bhqk,bkhe->bqhe', a.astype(v.dtype), v)

    out = lax.map(block, (qb, jnp.arange(NB)))
    return out.transpose(1, 0, 2, 3, 4).reshape(B, S, H, v.shape[-1])

def memory_cross_attention(h, m, wq, wkv, wo):
    B, S, _ = h.shape
    M = m.shape[1]
    q = (h @ wq).reshape(B, S, XATTN_HEADS, XATTN_DH)
    kv = m @ wkv
    k = kv[..., :D_MODEL].reshape(B, M, XATTN_HEADS, XATTN_DH)
    v = kv[..., D_MODEL:].reshape(B, M, XATTN_HEADS, XATTN_DH)
    s = jnp.einsum('bshd,bmhd->bhsm', q, k).astype(jnp.float32) / math.sqrt(XATTN_DH)
    p = jax.nn.softmax(s, axis=-1).astype(v.dtype)
    o = jnp.einsum('bhsm,bmhd->bshd', p, v).reshape(B, S, D_MODEL)
    return o @ wo

def first_inputs(seed: int = 0) -> dict:
    key = jax.random.key(seed)
    ks = jax.random.split(key, 32)
    f32 = jnp.float32

    def w(k, shape, fan_in):
        return jax.random.normal(k, shape, f32) * (fan_in ** -0.5)

    def gain(k, shape):
        return 1.0 + 0.02 * jax.random.normal(k, shape, f32)

    L = DEPTH
    return {
        "x": jax.random.normal(ks[0], (BATCH, SEQ, D_MODEL), f32),
        "mem": jax.random.normal(ks[1], (BATCH, N_MEM, D_MODEL), f32),
        "ffn1_norm": gain(ks[2], (L, D_MODEL)),
        "ffn1_w_gate": w(ks[3], (L, D_MODEL, D_FF), D_MODEL),
        "ffn1_w_up": w(ks[4], (L, D_MODEL, D_FF), D_MODEL),
        "ffn1_w_down": w(ks[5], (L, D_FF, D_MODEL), D_FF),
        "mix_norm": gain(ks[6], (L, D_MODEL)),
        "w_in": w(ks[7], (L, D_MODEL, IN_COLS), D_MODEL),
        "ret_out_norm": gain(ks[8], (L, RET_HEADS, RET_DV)),
        "diff_lq1": 0.1 * jax.random.normal(ks[9], (L, DIFF_DH), f32),
        "diff_lk1": 0.1 * jax.random.normal(ks[10], (L, DIFF_DH), f32),
        "diff_lq2": 0.1 * jax.random.normal(ks[11], (L, DIFF_DH), f32),
        "diff_lk2": 0.1 * jax.random.normal(ks[12], (L, DIFF_DH), f32),
        "diff_out_norm": gain(ks[13], (L, DIFF_HEADS, DIFF_DV)),
        "w_out": w(ks[14], (L, MIX_W, D_MODEL), MIX_W),
        "xattn_norm": gain(ks[15], (L, D_MODEL)),
        "mem_norm": gain(ks[16], (L, D_MODEL)),
        "xattn_wq": w(ks[17], (L, D_MODEL, D_MODEL), D_MODEL),
        "xattn_wkv": w(ks[18], (L, D_MODEL, 2 * D_MODEL), D_MODEL),
        "xattn_wo": w(ks[19], (L, D_MODEL, D_MODEL), D_MODEL),
        "ffn2_norm": gain(ks[20], (L, D_MODEL)),
        "ffn2_w_gate": w(ks[21], (L, D_MODEL, D_FF), D_MODEL),
        "ffn2_w_up": w(ks[22], (L, D_MODEL, D_FF), D_MODEL),
        "ffn2_w_down": w(ks[23], (L, D_FF, D_MODEL), D_FF),
        "final_norm": gain(ks[24], (D_MODEL,)),
    }

def first_block(x, mem, ffn1_norm, ffn1_w_gate, ffn1_w_up, ffn1_w_down, mix_norm, w_in,
              ret_out_norm, diff_lq1, diff_lk1, diff_lq2, diff_lk2, diff_out_norm, w_out,
              xattn_norm, mem_norm, xattn_wq, xattn_wkv, xattn_wo,
              ffn2_norm, ffn2_w_gate, ffn2_w_up, ffn2_w_down, final_norm):
    B, S, _ = x.shape
    pos = jnp.arange(S)
    split_at = np.cumsum([RET_QK_W, RET_QK_W, RET_V_W, RET_V_W, DIFF_QK_W, DIFF_QK_W]).tolist()
    for l in range(DEPTH):
        x = x + 0.5 * swiglu(rmsnorm(x, ffn1_norm[l]), ffn1_w_gate[l], ffn1_w_up[l], ffn1_w_down[l])

        h = rmsnorm(x, mix_norm[l])
        p = h @ w_in[l]
        rq, rk, rv, rg, dq, dk, dv = jnp.split(p, split_at, axis=-1)

        rq = rotary(rq.reshape(B, S, RET_HEADS, RET_DK), pos)
        rk = rotary(rk.reshape(B, S, RET_HEADS, RET_DK), pos) * (RET_DK ** -0.5)
        rv = rv.reshape(B, S, RET_HEADS, RET_DV)
        y_ret = retention_chunkwise(rq, rk, rv).astype(x.dtype)
        y_ret = rmsnorm(y_ret, ret_out_norm[l]).reshape(B, S, RET_V_W) * jax.nn.silu(rg)

        lambda_init = 0.8 - 0.6 * math.exp(-0.3 * l)
        lam = (jnp.exp(jnp.sum(diff_lq1[l].astype(jnp.float32) * diff_lk1[l].astype(jnp.float32)))
               - jnp.exp(jnp.sum(diff_lq2[l].astype(jnp.float32) * diff_lk2[l].astype(jnp.float32)))
               + lambda_init)
        dq = dq.reshape(B, S, DIFF_HEADS, 2, DIFF_DH)
        dk = dk.reshape(B, S, DIFF_HEADS, 2, DIFF_DH)
        dv = dv.reshape(B, S, DIFF_HEADS, DIFF_DV)
        y_diff = diff_attention(dq, dk, dv, lam)
        y_diff = (rmsnorm(y_diff, diff_out_norm[l]) * (1.0 - lambda_init)).reshape(B, S, DIFF_V_W)

        x = x + jnp.concatenate([y_ret, y_diff], axis=-1) @ w_out[l]

        x = x + memory_cross_attention(rmsnorm(x, xattn_norm[l]), rmsnorm(mem, mem_norm[l]),
                                       xattn_wq[l], xattn_wkv[l], xattn_wo[l])

        x = x + 0.5 * swiglu(rmsnorm(x, ffn2_norm[l]), ffn2_w_gate[l], ffn2_w_up[l], ffn2_w_down[l])
    return rmsnorm(x, final_norm)


CHUNK = 64
N_MIXERS = 2
N_POOL_LAYERS = (DEPTH + N_MIXERS - 1) // N_MIXERS
N_GLA_LAYERS = DEPTH // N_MIXERS

POOL_WIDTH = D_MODEL
POOL_WINDOWS = (2, 4, 8, 16)
POOL_GROUPS = len(POOL_WINDOWS)
POOL_GROUP_DIM = POOL_WIDTH // POOL_GROUPS

GLA_HEADS = 4
GLA_KEY_WIDTH = D_MODEL // 2
GLA_VALUE_WIDTH = D_MODEL
GLA_HEAD_K = GLA_KEY_WIDTH // GLA_HEADS
GLA_HEAD_V = GLA_VALUE_WIDTH // GLA_HEADS
GLA_GATE_RANK = 16
GLA_GATE_NORMALIZER = 16.0
GLA_IN_WIDTH = 2 * GLA_KEY_WIDTH + 2 * GLA_VALUE_WIDTH + GLA_GATE_RANK

RMS_EPS = 1e-6


def rms_norm(x, w):
    xf = x.astype(jnp.float32)
    y = xf * lax.rsqrt(jnp.mean(xf * xf, axis=-1, keepdims=True) + RMS_EPS)
    return (y * w.astype(jnp.float32)).astype(x.dtype)

def trailing_mean(u, window):
    seq = u.shape[1]
    cs = jnp.cumsum(u.astype(jnp.float32), axis=1)
    lagged = jnp.pad(cs, ((0, 0), (window, 0), (0, 0)))[:, :seq]
    count = jnp.minimum(jnp.arange(1, seq + 1), window).astype(jnp.float32)
    return ((cs - lagged) / count[None, :, None]).astype(u.dtype)

def pool_mixer(h, in_w, group_w, group_b, scale, out_w):
    b, s, _ = h.shape
    u, gate = jnp.split(h @ in_w, 2, axis=-1)
    ug = u.reshape(b, s, POOL_GROUPS, POOL_GROUP_DIM)
    pooled = jnp.stack([trailing_mean(ug[:, :, g], w) for g, w in enumerate(POOL_WINDOWS)],
                       axis=2) - ug
    mixed = jnp.einsum('bsgc,gcd->bsgd', pooled, group_w) + group_b
    y = mixed.reshape(b, s, POOL_WIDTH) * scale * jax.nn.silu(gate)
    return y @ out_w

def gla_mixer(h, in_w, gk_w, gk_b, head_norm_w, out_w):
    b, s, _ = h.shape
    n_chunks = s // CHUNK
    f32 = jnp.float32
    proj = h @ in_w
    q, k, v, gate, gk_low = jnp.split(
        proj, [GLA_KEY_WIDTH, 2 * GLA_KEY_WIDTH, 2 * GLA_KEY_WIDTH + GLA_VALUE_WIDTH,
               2 * GLA_KEY_WIDTH + 2 * GLA_VALUE_WIDTH], axis=-1)
    log_g = jax.nn.log_sigmoid((gk_low @ gk_w + gk_b).astype(f32)) / GLA_GATE_NORMALIZER

    def to_chunks(t, d):
        return t.astype(f32).reshape(b, n_chunks, CHUNK, GLA_HEADS, d)

    qc = to_chunks(q, GLA_HEAD_K) * (GLA_HEAD_K ** -0.5)
    kc = to_chunks(k, GLA_HEAD_K)
    vc = to_chunks(v, GLA_HEAD_V)
    cum = jnp.cumsum(to_chunks(log_g, GLA_HEAD_K), axis=2)
    cum_last = cum[:, :, -1:]
    e_pos, e_neg = jnp.exp(cum), jnp.exp(-cum)

    fwd = jnp.einsum('bnthk,bnshk->bnhts', qc * e_pos, kc * e_neg)
    bwd = jnp.einsum('bnthk,bnshk->bnhts', qc * e_neg, kc * e_pos)
    idx = jnp.arange(CHUNK)
    lower = idx[:, None] >= idx[None, :]
    scores = jnp.where(lower, fwd, bwd)
    o_intra = jnp.einsum('bnhts,bnshv->bnthv', scores, vc)

    q_dec = qc * e_pos
    k_dec = kc * jnp.exp(cum_last - cum)
    chunk_decay = jnp.exp(cum_last[:, :, 0])

    def step(state, inp):
        q_n, k_n, v_n, d_n = inp
        o_n = jnp.einsum('bthk,bhkv->bthv', q_n, state)
        state = state * d_n[..., None] + jnp.einsum('bthk,bthv->bhkv', k_n, v_n)
        return state, o_n

    xs = (jnp.moveaxis(q_dec, 1, 0), jnp.moveaxis(k_dec, 1, 0),
          jnp.moveaxis(vc, 1, 0), jnp.moveaxis(chunk_decay, 1, 0))
    state0 = jnp.zeros((b, GLA_HEADS, GLA_HEAD_K, GLA_HEAD_V), f32)
    _, o_inter = lax.scan(step, state0, xs)
    o = (o_intra + jnp.moveaxis(o_inter, 0, 1)).reshape(b, s, GLA_HEADS, GLA_HEAD_V)

    o = o * lax.rsqrt(jnp.mean(o * o, axis=-1, keepdims=True) + RMS_EPS) * head_norm_w.astype(f32)
    y = o.reshape(b, s, GLA_VALUE_WIDTH).astype(h.dtype) * jax.nn.silu(gate)
    return y @ out_w

def second_inputs(seed: int = 0) -> dict:
    key = jax.random.key(seed)
    ks = jax.random.split(key, 16)
    nrm = jax.random.normal
    f32 = jnp.float32
    NP, NG = N_POOL_LAYERS, N_GLA_LAYERS
    return {
        "x": nrm(ks[0], (BATCH, SEQ, D_MODEL), f32),
        "norm_w": 1.0 + 0.02 * nrm(ks[1], (DEPTH, D_MODEL), f32),
        "pool_in_w": nrm(ks[2], (NP, D_MODEL, 2 * POOL_WIDTH), f32) * D_MODEL ** -0.5,
        "pool_group_w": nrm(ks[3], (NP, POOL_GROUPS, POOL_GROUP_DIM, POOL_GROUP_DIM), f32) * POOL_GROUP_DIM ** -0.5,
        "pool_group_b": 0.02 * nrm(ks[4], (NP, POOL_GROUPS, POOL_GROUP_DIM), f32),
        "pool_scale": 1.0 + 0.1 * nrm(ks[5], (NP, POOL_WIDTH), f32),
        "pool_out_w": nrm(ks[6], (NP, POOL_WIDTH, D_MODEL), f32) * POOL_WIDTH ** -0.5,
        "gla_in_w": nrm(ks[7], (NG, D_MODEL, GLA_IN_WIDTH), f32) * D_MODEL ** -0.5,
        "gla_gk_w": nrm(ks[8], (NG, GLA_GATE_RANK, GLA_KEY_WIDTH), f32) * GLA_GATE_RANK ** -0.5,
        "gla_gk_b": 0.02 * nrm(ks[9], (NG, GLA_KEY_WIDTH), f32),
        "gla_head_norm_w": 1.0 + 0.02 * nrm(ks[10], (NG, GLA_HEAD_V), f32),
        "gla_out_w": nrm(ks[11], (NG, GLA_VALUE_WIDTH, D_MODEL), f32) * GLA_VALUE_WIDTH ** -0.5,
        "final_norm_w": 1.0 + 0.02 * nrm(ks[12], (D_MODEL,), f32),
    }

def second_block(x, norm_w, pool_in_w, pool_group_w, pool_group_b, pool_scale, pool_out_w,
              gla_in_w, gla_gk_w, gla_gk_b, gla_head_norm_w, gla_out_w, final_norm_w):
    h = x
    for i in range(DEPTH):
        normed = rms_norm(h, norm_w[i])
        j = i // N_MIXERS
        if i % N_MIXERS == 0:
            h = h + pool_mixer(normed, pool_in_w[j], pool_group_w[j], pool_group_b[j],
                               pool_scale[j], pool_out_w[j])
        else:
            h = h + gla_mixer(normed, gla_in_w[j], gla_gk_w[j], gla_gk_b[j],
                              gla_head_norm_w[j], gla_out_w[j])
    return rms_norm(h, final_norm_w)


def setup_inputs(seed=0):
    out = dict(first_inputs(seed))
    for name, value in second_inputs(seed + 1).items():
        if name != "x":
            out[name + "_2"] = value
    return out


def reference(
    x, mem, ffn1_norm, ffn1_w_gate, ffn1_w_up, ffn1_w_down, mix_norm, w_in, ret_out_norm,
    diff_lq1, diff_lk1, diff_lq2, diff_lk2, diff_out_norm, w_out, xattn_norm, mem_norm,
    xattn_wq, xattn_wkv, xattn_wo, ffn2_norm, ffn2_w_gate, ffn2_w_up, ffn2_w_down, final_norm,
    norm_w_2, pool_in_w_2, pool_group_w_2, pool_group_b_2, pool_scale_2, pool_out_w_2,
    gla_in_w_2, gla_gk_w_2, gla_gk_b_2, gla_head_norm_w_2, gla_out_w_2, final_norm_w_2,
):
    x = first_block(
        x, mem, ffn1_norm, ffn1_w_gate, ffn1_w_up, ffn1_w_down, mix_norm, w_in, ret_out_norm,
        diff_lq1, diff_lk1, diff_lq2, diff_lk2, diff_out_norm, w_out, xattn_norm, mem_norm,
        xattn_wq, xattn_wkv, xattn_wo, ffn2_norm, ffn2_w_gate, ffn2_w_up, ffn2_w_down,
        final_norm,
    )
    return second_block(
        x, norm_w_2, pool_in_w_2, pool_group_w_2, pool_group_b_2, pool_scale_2, pool_out_w_2,
        gla_in_w_2, gla_gk_w_2, gla_gk_b_2, gla_head_norm_w_2, gla_out_w_2, final_norm_w_2,
    )


_drawn_inputs = setup_inputs


def setup_inputs(seed=0):
    import zlib

    import numpy as np

    out = dict(_drawn_inputs(seed))
    spreads = {}
    factors = {'ffn1_norm': 4.518,
     'ret_out_norm': 7.858,
     'diff_lq1': 7.277,
     'diff_lk1': 8.0,
     'diff_out_norm': 5.625,
     'xattn_norm': 8.0,
     'mem_norm': 8.0,
     'ffn2_norm': 7.998,
     'norm_w_2': 4.281,
     'pool_group_b_2': 5.313,
     'final_norm_w_2': 7.99,
     'diff_lq2': 8.0,
     'diff_lk2': 8.0}
    for name, (base, spread) in spreads.items():
        noise = np.random.default_rng([zlib.crc32(name.encode()), seed]).standard_normal(out[name].shape)
        drawn = base * np.exp(spread * noise) if base else spread * noise
        out[name] = __import__('jax').numpy.asarray(drawn.astype(out[name].dtype))
    for name, factor in factors.items():
        out[name] = (out[name] * factor).astype(out[name].dtype)
    return out
```

```python
from contextlib import ExitStack

import numpy as np
import concourse.bass as bass
from concourse import mybir

ALU = mybir.AluOpType
ACT = mybir.ActivationFunctionType
AX = mybir.AxisListType
F32 = mybir.dt.float32
F32R = mybir.dt.float32r

P = 128
S = 1024
D = 1024
KT = D // P
TT = S // P
FF = 2816
FT = FF // P
CHUNKS = ((0, 8), (8, 8), (16, 6))
M = 256
MT = M // P
H = 4
EPS = 1e-6
LAMBDA_INIT = 0.2
DIFF_SCALE = 0.125
XATTN_SCALE = 0.0625
HALVES = ((0, 512), (512, 1024))

G_FFN1, G_MIX, G_X, G_MEM, G_FFN2, G_FIN, G_NORM2, G_PB, G_PS, G_RET, G_DIFF, G_ROWS = (
    0, 8, 16, 24, 32, 40, 48, 56, 64, 72, 76, 80)

C_ID, C_MASK, C_ONES, C_DECAY, C_ZETA, C_XI, C_XI2, C_GCH, C_INV, C_COLS = (
    0, 128, 256, 384, 896, 1024, 1028, 1032, 1033, 1033 + 64)


def constants():
    c = np.zeros((P, C_COLS), np.float32)
    n = np.arange(P)
    c[:, C_ID:C_ID + P] = np.eye(P)
    c[:, C_MASK:C_MASK + P] = np.where(n[None, :] <= n[:, None], 0.0, -2.0 ** 100)
    c[:, C_ONES:C_ONES + P] = 1.0
    log_g = np.log(1.0 - 2.0 ** (-5.0 - np.arange(H)))
    for h in range(H):
        c[:, C_DECAY + h * P:C_DECAY + (h + 1) * P] = np.where(
            n[:, None] <= n[None, :], np.exp(-(n[:, None] + 1.0) * log_g[h]), 0.0)
        c[:, C_ZETA + 32 * h:C_ZETA + 32 * (h + 1)] = np.exp((P - 1.0 - n) * log_g[h])[:, None]
        xi = np.exp((n + 1.0) * log_g[h]) / 8.0
        c[:, C_XI + h] = xi
        c[:, C_XI2 + h] = xi * xi / P
        c[32 * h:32 * h + 32, C_GCH] = np.exp(P * log_g[h])
    for g in range(4):
        c[:, C_INV + 16 * g:C_INV + 16 * (g + 1)] = 1.0 / np.minimum(np.arange(1, 17), 2 << g)
    return c


def rotary_tables():
    inv = (1.0 / (np.float32(10000.0) ** (np.arange(0, 64, 2, dtype=np.float32) / np.float32(64)))).astype(np.float32)
    ang = (np.arange(S, dtype=np.float32)[None, :] * inv[:, None]).astype(np.float32)
    t = np.stack([np.cos(ang), np.sin(ang)], 1).astype(np.float32)
    return np.ascontiguousarray(np.tile(t, (H, 1, 1)))


def plan():
    at, n, u = {}, 0, 0
    order = [("gains", 1, 0), ("xt", KT, 0)]
    for f in ("ffn1", "ffn2"):
        stages = [(f + "_stat", 1, 0)]
        for c, (_, k) in enumerate(CHUNKS):
            stages += [(f"{f}_up{c}", 2 * k, 2 * k), (f"{f}_down{c}", KT, KT)]
        if f == "ffn1":
            order += stages
            order += [("win_stat", 1, 0), ("win", 24, 24), ("wout", KT, KT), ("wq_stat", 1, 0), ("wq", KT, KT),
                      ("memt", 2, 0), ("wkv", 2 * KT, 2 * KT), ("vt", MT, 0), ("wo", KT, KT)]
        else:
            order += stages
    order += [("pool_stat", 2, 0), ("pool_u", KT, KT), ("pool_g", 2 * KT, 2 * KT), ("fgain", 1, 0), ("pool_out", KT, KT),
              ("final", TT, 0)]
    for name, dn, du in order:
        at[name] = (n, u)
        n += dn
        u += du
    at["end"] = (n, u)
    return at


def build(nc, a, consts, rot, spill, out):
    at = plan()
    N = {k: v[0] for k, v in at.items()}
    U = {k: v[1] for k, v in at.items()}
    UNITS = U["end"]
    R_XT, R_FFN1, R_WOUT, R_WO, R_FFN2 = 0, 8, 16, 24, 32

    with ExitStack() as ctx:
        sem = lambda name: ctx.enter_context(nc.semaphore(name))
        base = [(nc.sbuf_base + 63) // 64 * 64]

        def here(name, shape, dt=F32):
            t = nc.alloc_sbuf_tensor_at(name, shape, dt, offset=base[0])
            base[0] += (int(np.prod(shape[1:])) * 4 + 31) // 32 * 32
            return t

        def over(name, shape, dt, offset):
            return nc.alloc_sbuf_tensor_at(name, shape, dt, offset=offset)

        K1 = 1024
        a_xt = base[0]
        xt = here("xt", [P, KT, S])
        a_r0 = base[0]
        r0h, r0l = here("r0h", [P, KT, S], F32R), here("r0l", [P, KT, S], F32R)
        a_r1 = base[0]
        r1h, r1l = here("r1h", [P, KT, S], F32R), here("r1l", [P, KT, S], F32R)
        raw = here("raw", [P, 2, KT, P])
        w_hi, w_lo = here("w_hi", [P, 2, KT, P], F32R), here("w_lo", [P, 2, KT, P], F32R)
        PAD = 16
        t1, t2, t3 = (here(f"t{i}", [P, PAD + S]) for i in (1, 2, 3))
        T1, T2, T3 = (t[:, PAD:PAD + S] for t in (t1, t2, t3))
        acc, rstd, acc2, rfin = here("acc", [P, S]), here("rstd", [P, S]), here("acc2", [P, S]), here("rfin", [P, S])
        cst = here("cst", [P, C_COLS])
        gain = here("gain", [P, G_ROWS])
        ygain, gain2 = here("ygain", [P, 8]), here("gain2", [P, KT])
        ident_r, mask_r = here("ident_r", [P, P], F32R), here("mask_r", [P, P], F32R)
        lamv = here("lamv", [P, 2])
        small = here("small", [P, 64])
        assert base[0] <= nc.sbuf_usable_end, (base[0], nc.sbuf_usable_end)
        ident, ones = cst[:, C_ID:C_ID + P], cst[:, C_ONES:C_ONES + P]

        xin = over("xin", [P, TT, D], F32, a_r1)
        grow = over("grow", [P, P], F32, a_r1 + 32 * K1)
        lrow = over("lrow", [P, 4, 64], F32, a_r1 + 33 * K1)
        pa = over("pa", [P, 16, S], F32, a_r1)
        pb = over("pb", [P, 8, S], F32, a_xt)
        pa_f, pb_f = pa[:].rearrange("p t n -> p (t n)"), pb[:].rearrange("p t n -> p (t n)")
        y = over("y", [P, 8, S], F32, a_r0)
        y_f = y[:].rearrange("p t n -> p (t n)")
        w0 = a_r0 + 32 * K1
        rott = over("rott", [P, 2, S], F32, w0)
        qk = over("qk", [P, 4, P], F32, w0 + 8 * K1)
        qkh, qkl = over("qkh", [P, 4, P], F32R, w0 + 10 * K1), over("qkl", [P, 4, P], F32R, w0 + 12 * K1)
        vc = over("vc", [P, 4, P], F32, w0 + 14 * K1)
        rvh, rvl = over("rvh", [P, 4, P], F32R, w0 + 16 * K1), over("rvl", [P, 4, P], F32R, w0 + 18 * K1)
        kz = over("kz", [P, 2, P], F32, w0 + 20 * K1)
        kzh, kzl = over("kzh", [P, 2, P], F32R, w0 + 21 * K1), over("kzl", [P, 2, P], F32R, w0 + 22 * K1)
        inh, inl = over("inh", [P, 4, P], F32R, w0 + 23 * K1), over("inl", [P, 4, P], F32R, w0 + 25 * K1)
        rs = over("rs", [P, 2, P], F32, w0 + 27 * K1)
        rsh, rsl = over("rsh", [P, 2, P], F32R, w0 + 28 * K1), over("rsl", [P, 2, P], F32R, w0 + 29 * K1)
        rtmp_a = over("rtmp_a", [P, 2, 2, P], F32, w0 + 30 * K1)
        rtmp = [rtmp_a[:, 0], rtmp_a[:, 1]] + [T3[:, c:c + 2 * P].rearrange("p (c n) -> p c n", c=2) for c in (4 * P, 6 * P)]
        inf = T1[:, 0:512].rearrange("p (h n) -> p h n", h=4)
        rsq = T2[:, 0:512].rearrange("p (h n) -> p h n", h=4)
        on = T3[:, 0:512].rearrange("p (h n) -> p h n", h=4)
        dqh, dql, dkh, dkl = (over(nm, [P, S], F32R, w0 + 4 * K1 * i) for i, nm in enumerate(("dqh", "dql", "dkh", "dkl")))
        dvh, dvl = (over(nm, [P, TT, P], F32R, w0 + 4 * K1 * (4 + i)) for i, nm in enumerate(("dvh", "dvl")))
        pth, ptl = (over(nm, [P, TT, P], F32R, w0 + 4 * K1 * (6 + i)) for i, nm in enumerate(("pth", "ptl")))
        e = ((T1, T2), (acc[:], rstd[:]))
        qx = over("qx", [P, KT, S], F32, a_r1)
        y2 = over("y2", [P, KT, S], F32, a_r1 + 32 * K1)
        memh, meml, kxh, kxl = (over(nm, [P, KT, M], F32R, a_r0 + 8 * K1 * i) for i, nm in enumerate(("memh", "meml", "kxh", "kxl")))
        vxh, vxl = (over(nm, [P, MT, D], F32R, w0 + 8 * K1 * i) for i, nm in enumerate(("vxh", "vxl")))
        vf = over("vf", [P, KT, M], F32, w0 + 16 * K1)
        memr = over("memr", [P, MT, D], F32, w0 + 24 * K1)
        qsh, qsl = (over(nm, [P, KT, P], F32R, w0 + 16 * K1 + 4 * K1 * i) for i, nm in enumerate(("qsh", "qsl")))
        pxh, pxl = (over(nm, [P, KT, P], F32R, w0 + 24 * K1 + 4 * K1 * i) for i, nm in enumerate(("pxh", "pxl")))
        outrow = (T1, T2)
        fgain, frow = acc, acc2

        ps = ctx.enter_context(nc.psum_tensor("ps", [P, 4, S], F32))
        bank = lambda b: ps[:, b // 2, (b % 2) * 512:(b % 2) * 512 + 512]

        s_cst, s_vec, s_lrow, s_x, s_rot, s_mem, s_frow = map(sem, ("s_cst", "s_vec", "s_lrow", "s_x", "s_rot", "s_mem", "s_frow"))
        s_raw = [sem("s_raw0"), sem("s_raw1")]
        s_whi, s_wlo = sem("s_whi"), sem("s_wlo")
        s_mm, s_evac = sem("s_mm"), sem("s_evac")
        s_setup_act, s_setup_dve, s_lam = sem("s_setup_act"), sem("s_setup_dve"), sem("s_lam")
        s_sqrt, s_rstd, s_sq2, s_acc2 = map(sem, ("s_sqrt", "s_rstd", "s_sq2", "s_acc2"))
        s_ahi, s_alo, s_sq, s_acc = sem("s_ahi"), sem("s_alo"), sem("s_sq"), sem("s_acc")
        s_silu, s_h, s_hhi, s_hlo = sem("s_silu"), sem("s_h"), sem("s_hhi"), sem("s_hlo")
        s_spill, s_reload = sem("s_spill"), sem("s_reload")
        s_dve, s_pool = sem("s_dve"), sem("s_pool")
        s_out = [sem("s_out0"), sem("s_out1")]

        (s_sg, s_rotd, s_qkh, s_qkl, s_vtr, s_ktr, s_vh, s_vl, s_kz, s_kzh, s_kzl, s_inner, s_inf, s_inh,
         s_inl, s_kv, s_r, s_rh, s_rl, s_o, s_rsq, s_rms, s_rroot, s_on, s_ytr, s_y) = map(sem, (
             "s_sg", "s_rotd", "s_qkh", "s_qkl", "s_vtr", "s_ktr", "s_vh", "s_vl", "s_kz", "s_kzh", "s_kzl",
             "s_inner", "s_inf", "s_inh", "s_inl", "s_kv", "s_r", "s_rh", "s_rl", "s_o", "s_rsq", "s_rms",
             "s_rroot", "s_on", "s_ytr", "s_y"))
        (s_dqh, s_dql, s_vt, s_dvtr, s_dvh, s_dvl, s_s, s_nm, s_exp, s_a, s_t, s_pth, s_ptl, s_pv, s_dsq,
         s_dms, s_droot, s_don, s_dytr, s_dy) = map(sem, (
             "s_dqh", "s_dql", "s_vt", "s_dvtr", "s_dvh", "s_dvl", "s_s", "s_nm", "s_exp", "s_a", "s_t",
             "s_pth", "s_ptl", "s_pv", "s_dsq", "s_dms", "s_droot", "s_don", "s_dytr", "s_dy"))
        s_rtile, s_ms2, s_ra, s_mx, s_da, s_dn, s_xa = map(sem, ("s_rtile", "s_ms2", "s_ra", "s_mx", "s_da", "s_dn", "s_xa"))
        s_yhi, s_ylo = sem("s_yhi"), sem("s_ylo")
        (s_msq, s_mms, s_mroot, s_mn, s_mhi, s_mlo, s_khi, s_klo, s_vf, s_vxh, s_vxl, s_qh, s_ql, s_xs, s_xnm,
         s_xe, s_xn, s_xt, s_xph, s_xpl, s_xpv, s_xy) = map(sem, (
             "s_msq", "s_mms", "s_mroot", "s_mn", "s_mhi", "s_mlo", "s_khi", "s_klo", "s_vf", "s_vxh", "s_vxl",
             "s_qh", "s_ql", "s_xs", "s_xnm", "s_xe", "s_xn", "s_xt", "s_xph", "s_xpl", "s_xpv", "s_xy"))
        s_pd, s_phi, s_plo, s_psilu, s_pq, s_yy, s_fsq, s_fms, s_froot, s_fo = map(sem, (
            "s_pd", "s_phi", "s_plo", "s_psilu", "s_pq", "s_yy", "s_fsq", "s_fms", "s_froot", "s_fo"))

        def weights(name):
            return a[name].rearrange("l (k p) n -> p (l k) n", p=P)

        def landed(u):
            rotary = max(0, min(2, (u - U["win"]) // 2 + 1))
            return 16 * (u // 2 + 1 + (H - 1) * rotary)

        block = ctx.enter_context(nc.Block())

        @block.sync
        def _(sp):
            sp.dma_start(cst[:], consts).then_inc(s_cst, 16)
            xv = a["x"].rearrange("b (t p) d -> p (b t) d", p=P)
            for t in range(0, TT, 2):
                sp.dma_start(xin[:, t:t + 2], xv[:, t:t + 2]).then_inc(s_x, 16)
            vectors = (("ffn1_norm", G_FFN1), ("mix_norm", G_MIX), ("xattn_norm", G_X), ("mem_norm", G_MEM),
                       ("ffn2_norm", G_FFN2), ("norm_w_2", G_NORM2), ("pool_scale_2", G_PS))
            for name, row in vectors:
                sp.dma_start(grow[row:row + KT, :], a[name].rearrange("l (k p) -> (l k) p", p=P)).then_inc(s_vec, 16)
            sp.dma_start(grow[G_FIN:G_FIN + KT, :], a["final_norm"].rearrange("(k p) -> k p", p=P)).then_inc(s_vec, 16)
            sp.dma_start(grow[G_PB:G_PB + KT, :], a["pool_group_b_2"].rearrange("l g (k p) -> (l g k) p", p=P)).then_inc(s_vec, 16)
            sp.dma_start(grow[G_RET:G_RET + H, :], a["ret_out_norm"].rearrange("l h p -> (l h) p")).then_inc(s_vec, 16)
            sp.dma_start(grow[G_DIFF:G_DIFF + H, :], a["diff_out_norm"].rearrange("l h p -> (l h) p")).then_inc(s_vec, 16)
            for i, name in enumerate(("diff_lq1", "diff_lk1", "diff_lq2", "diff_lk2")):
                sp.dma_start(lrow[0:1, i, :], a[name]).then_inc(s_lrow, 16)

            def load(u, j, src, kn=KT, first=False):
                if not first:
                    sp.wait_ge(s_wlo, u - 1)
                sp.dma_start(raw[:, j, 0:kn], src).then_inc(s_raw[j], 16)

            def ffn(f, first):
                wg, wu = weights(f + "_w_gate"), weights(f + "_w_up")
                wd = weights(f + "_w_down")
                for c, (t0, k) in enumerate(CHUNKS):
                    u = U[f"{f}_up{c}"]
                    peel = 1 if first and c == 0 else 0
                    for j in range(4 * peel):
                        w = (wg, wu)[j % 2]
                        load(u + j, j % 2, w[:, :, (j // 2) * P:(j // 2 + 1) * P], first=(j < 2))
                    with sp.Fori(peel, k // 2) as i:
                        for j in range(4):
                            w = (wg, wu)[j % 2]
                            load(u + 4 * i + j, j % 2, w[:, :, bass.ds(i * (2 * P) + (t0 + j // 2) * P, P)])
                    u = U[f"{f}_down{c}"]
                    with sp.Fori(0, 2) as i:
                        for j in range(4):
                            load(u + 4 * i + j, j % 2, wd[:, t0:t0 + k, bass.ds(i * (4 * P) + j * P, P)], k)

            def project(u, w, count, col0=0):
                with sp.Fori(0, count // 4) as i:
                    for j in range(4):
                        load(u + 4 * i + j, j % 2, w[:, :, bass.ds(i * (4 * P) + (col0 + j * P), P)])

            ffn("ffn1", True)
            win = weights("w_in")
            for j in range(4):
                sp.wait_ge(s_wlo, U["win"] + j - 1)
                for h in range(H):
                    col = (j // 2) * 256 + 64 * h + 32 * (j % 2)
                    sp.dma_start(raw[:, j % 2, :, 32 * h:32 * h + 32], win[:, :, col:col + 32]).then_inc(s_raw[j % 2], 16)
            sp.wait_ge(s_acc, R_FFN1 + KT)
            sp.dma_start(spill, xt[:]).then_inc(s_spill, 16)
            project(U["win"] + 4, win, 20, 4 * P)

            def project_units(name, w, js):
                for j in js:
                    load(U[name] + j, j % 2, w[:, :, j * P:(j + 1) * P])

            project_units("wout", weights("w_out"), (0, 1))
            sp.wait_ge(s_mm, N["win"] + 24)
            sp.dma_start(rott[:], rot).then_inc(s_rot, 16)
            sp.wait_ge(s_dy, H + 1)
            sp.dma_start(xt[:], spill).then_inc(s_reload, 16)
            project_units("wout", weights("w_out"), range(2, KT))
            project(U["wq"], weights("xattn_wq"), KT)
            project_units("wkv", weights("xattn_wkv"), (0, 1))
            sp.wait_ge(s_mm, N["wq"] + KT)
            sp.dma_start(memr[:], a["mem"].rearrange("b (t p) d -> p (b t) d", p=P)).then_inc(s_mem, 16)
            project_units("wkv", weights("xattn_wkv"), range(2, 4))
            project(U["wkv"] + 4, weights("xattn_wkv"), 12, 4 * P)
            project(U["wo"], weights("xattn_wo"), KT)
            ffn("ffn2", False)
            win2 = weights("pool_in_w_2")
            project(U["pool_u"], win2, KT)
            wg2 = a["pool_group_w_2"].rearrange("l g (k p) n -> p (l g) k n", p=P)
            for g in range(4):
                u = U["pool_g"] + 4 * g
                for j in range(2):
                    load(u + j, j, win2[:, :, (KT + 2 * g + j) * P:(KT + 2 * g + j + 1) * P])
                for j in range(2):
                    load(u + 2 + j, j, wg2[:, g, :, j * P:(j + 1) * P], 2)
                if g == 0:
                    sp.wait_ge(s_mm, N["pool_stat"] + 2)
                    sp.dma_start(frow[0:1, :], a["final_norm_w_2"].rearrange("(o d) -> o d", o=1)).then_inc(s_frow, 16)
            project(U["pool_out"], weights("pool_out_w_2"), KT)
            for t in range(TT):
                sp.wait_ge(s_evac, N["final"] + t + 1)
                sp.dma_start(out[0, t * P:(t + 1) * P, :], outrow[t % 2]).then_inc(s_out[t % 2], 16)
            for j in range(2):
                sp.wait_ge(s_out[j], 16 * TT // 2)

        @block.tensor
        def _(pe):
            def slot_free(n):
                if isinstance(n, int) and n < 4:
                    return
                pe.wait_ge(s_evac, n - 3)

            def product(out_ap, pairs, first=True, last=True):
                for i, (lhs, rhs) in enumerate(pairs):
                    mm = pe.matmul(out_ap, lhs, rhs, start=first and i == 0, stop=last and i == len(pairs) - 1,
                                   skip_group_check=True)
                return mm

            def unit(n, u, j, slot, rh, rl, kts=range(KT), cols=S, ready=None):
                slot_free(n)
                pe.wait_ge(s_wlo, u + 1)
                for i, k in enumerate(kts):
                    if ready:
                        pe.wait_ge(ready[0], ready[1] + i + 1)
                    for p, (w, x) in enumerate(((w_hi, rh), (w_hi, rl), (w_lo, rh))):
                        for c0, c1 in HALVES:
                            if c0 >= cols:
                                continue
                            c1 = min(c1, cols)
                            mm = pe.matmul(ps[:, slot, c0:c1], w[:, j, i, :], x[:, k, c0:c1],
                                           start=(i == 0 and p == 0), stop=(i == len(kts) - 1 and p == 2))
                mm.then_inc(s_mm, 1)

            def units(stage, count, rh, rl, kts=range(KT), cols=S, ready=None):
                n0, u0 = N[stage], U[stage]
                with pe.Fori(0, count // 4) as i:
                    for j in range(4):
                        unit(n0 + j + 4 * i, u0 + j + 4 * i, j % 2, (n0 + j) % 4, rh, rl, kts, cols,
                             ready if j == 0 else None)

            def stat(stage, tiles):
                for i, (src, s_done, count) in enumerate(tiles):
                    n = N[stage] + i
                    slot_free(n)
                    pe.wait_ge(s_done, count)
                    for c0, c1 in HALVES:
                        mm = pe.matmul(ps[:, n % 4, c0:c1], ones, src[:, c0:c1], start=True, stop=True)
                    mm.then_inc(s_mm, 1)

            def ffn(f, rh, rl, hh, hl, r, pairs0):
                stat(f + "_stat", [(acc, s_acc, r + KT)])
                pairs = pairs0
                for c, (t0, k) in enumerate(CHUNKS):
                    units(f"{f}_up{c}", 2 * k, rh, rl, ready=(s_alo, r) if c == 0 else None)
                    units(f"{f}_down{c}", KT, hh, hl, kts=range(k), ready=(s_hlo, pairs))
                    pairs += k

            pe.wait_ge(s_cst, 16)
            pe.wait_ge(s_vec, 11 * 16)
            pe.transpose(ps[:, 0, 0:G_ROWS], grow[0:G_ROWS, :], cst[0:G_ROWS, C_ID:C_ID + G_ROWS])
            pe.wait_ge(s_lam, 1)
            pe.matmul(ps[:, 0, 512:514], cst[0:1, C_ONES:C_ONES + P], small[0:1, 4:6], start=True, stop=True).then_inc(s_mm, 1)
            for m in range(KT):
                n = N["xt"] + m
                slot_free(n)
                for t in range(TT):
                    if m == 0 and t == 0:
                        pe.wait_ge(s_x, 16 * TT // 2)
                    mm = pe.transpose(ps[:, n % 4, t * P:(t + 1) * P], xin[:, t, m * P:(m + 1) * P], ident)
                mm.then_inc(s_mm, 1)
            ffn("ffn1", r0h, r0l, r1h, r1l, R_XT, 0)
            stat("win_stat", [(acc, s_acc, R_FFN1 + KT)])
            units("win", 24, r0h, r0l, ready=(s_alo, R_FFN1))

            bv, bk, bo, bkv = bank(4), bank(5), bank(6), bank(7)
            pe.wait_ge(s_evac, N["win"] + 24)

            def retention_chunk(i, first):
                pe.wait_ge(s_rotd, i + 1)
                if not first:
                    pe.wait_ge(s_y, i)
                for h in range(H):
                    mm = pe.transpose(bv[:, h * P:(h + 1) * P], vc[:, h], ident)
                mm.then_inc(s_vtr, 1)
                for c in range(2):
                    if not first and c == 0:
                        pe.wait_ge(s_r, i)
                    mm = pe.transpose(bk[:, c * P:(c + 1) * P], qk[:, 2 + c], ident)
                mm.then_inc(s_ktr, 1)
                pe.wait_ge(s_qkl, i + 1)
                if not first:
                    pe.wait_ge(s_inf, i)
                for h in range(H):
                    rows = slice(32 * h, 32 * h + 32)
                    pairs = [(kk[rows, 2 + c], qq[rows, c]) for c in range(2) for kk, qq in ((qkh, qkh), (qkh, qkl), (qkl, qkh))]
                    mm = product(bank(h)[:, 0:P], pairs)
                mm.then_inc(s_inner, 1)
                pe.wait_ge(s_kzl, i + 1)
                pe.wait_ge(s_vl, i + 1)
                vh, vl = rvh[:].rearrange("p h n -> p (h n)"), rvl[:].rearrange("p h n -> p (h n)")
                product(bkv, [(kzh[:, 0], vh), (kzh[:, 0], vl), (kzl[:, 0], vh)])
                product(bk, [(kzh[:, 1], vh), (kzh[:, 1], vl), (kzl[:, 1], vh)]).then_inc(s_kv, 1)
                pe.wait_ge(s_inl, i + 1)
                if not first:
                    pe.wait_ge(s_rl, i)
                for h in range(H):
                    rows = slice(32 * h, 32 * h + 32)
                    o = bo[:, h * P:(h + 1) * P]
                    mm = product(o, [(inh[:, h], rvh[:, h]), (inh[:, h], rvl[:, h]), (inl[:, h], rvh[:, h])], last=first)
                    if not first:
                        if h > 0:
                            pe.wait_ge(s_rtile, 3 * (i - 1) + h)
                        mm = product(o, [(qq[rows, c], rr[rows, c]) for c in range(2)
                                         for qq, rr in ((qkh, rsh), (qkh, rsl), (qkl, rsh))], first=False)
                        if h < H - 1:
                            mm.then_inc(s_rtile, 1)
                mm.then_inc(s_o, 1)
                pe.wait_ge(s_on, i + 1)
                for h in range(H):
                    mm = pe.transpose(bv[:, h * P:(h + 1) * P], on[:, h], ident)
                mm.then_inc(s_ytr, 1)

            retention_chunk(0, True)
            with pe.Fori(1, TT) as i:
                retention_chunk(i, False)

            pe.wait_ge(s_y, TT)
            pe.sem_inc(s_s, 1)
            pe.sem_inc(s_t, 2)
            pe.sem_inc(s_pv, 1)

            def scores(i, t):
                g = 8 * i + t
                w = (t + 1) * P
                if t == 0:
                    pe.wait_ge(s_dql, i + 1)
                for c in range(2):
                    rows = slice(64 * c, 64 * c + 64)
                    pe.wait_ge(s_exp, 2 * g + c + 1)
                    for c0 in range(0, w, 512):
                        c1 = min(c0 + 512, w)
                        product(ps[:, c, c0:c1], [(qq[rows, t * P:w], kk[rows, c0:c1])
                                                  for qq, kk in ((dqh, dkh), (dqh, dkl), (dql, dkh))], last=False)
                    mm = pe.matmul(ps[:, c, t * P:w], ident_r[:], mask_r[:], start=False, stop=True, skip_group_check=True)
                    mm.then_inc(s_s, 1)

            with pe.Fori(0, H) as i:
                pe.wait_ge(s_vt, i + 1)
                pe.wait_ge(s_dy, i + 1)
                for t in range(TT):
                    mm = pe.transpose(ps[:, 2, t * P:(t + 1) * P], T3[:, t * P:(t + 1) * P], ident)
                mm.then_inc(s_dvtr, 1)
                scores(i, 0)
                for t in range(TT):
                    g = 8 * i + t
                    if t + 1 < TT:
                        scores(i, t + 1)
                    pe.wait_ge(s_a, g + 1)
                    if t == 0:
                        pe.wait_ge(s_dvl, i + 1)
                    else:
                        pe.wait_ge(s_ptl, g)
                    for b in range(t + 1):
                        mm = pe.transpose(ps[:, 2, b * P:(b + 1) * P], e[t % 2][1][:, b * P:(b + 1) * P], ident)
                    mm.then_inc(s_t, 1)
                    pe.wait_ge(s_ptl, g + 1)
                    for b in range(t + 1):
                        mm = product(ps[:, 3, t * P:(t + 1) * P], [(pp[:, b], vv[:, b]) for pp, vv in (
                            (pth, dvh), (pth, dvl), (ptl, dvh))], first=(b == 0), last=(b == t))
                    mm.then_inc(s_pv, 1)
                pe.wait_ge(s_don, i + 1)
                for t in range(TT):
                    mm = pe.transpose(ps[:, 2, t * P:(t + 1) * P], rfin[:, t * P:(t + 1) * P], ident)
                mm.then_inc(s_dytr, 1)

            pe.wait_ge(s_dy, H + 1)
            units("wout", KT, r1h, r1l, ready=(s_ylo, 0))
            stat("wq_stat", [(acc, s_acc, R_WOUT + KT)])
            units("wq", KT, r0h, r0l, ready=(s_alo, R_WOUT))

            pe.wait_ge(s_mn, 1)
            for q in range(2):
                n = N["memt"] + q
                slot_free(n)
                for k in range(4):
                    for t in range(MT):
                        c = k * M + t * P
                        mm = pe.transpose(ps[:, n % 4, c:c + P], memr[:, t, (4 * q + k) * P:(4 * q + k + 1) * P], ident)
                mm.then_inc(s_mm, 1)
            pe.wait_ge(s_evac, N["memt"] + 2)
            units("wkv", 2 * KT, memh, meml, cols=M)
            for t in range(MT):
                n = N["vt"] + t
                slot_free(n)
                pe.wait_ge(s_evac, N["wkv"] + 2 * KT)
                for k in range(KT):
                    mm = pe.transpose(ps[:, n % 4, k * P:(k + 1) * P], vf[:, k, t * P:(t + 1) * P], ident)
                mm.then_inc(s_mm, 1)

            def xscores(i, first):
                pe.wait_ge(s_ql, i + 1)
                if not first:
                    pe.wait_ge(s_xe, i)
                for h in range(H):
                    mm = product(ps[:, 0, h * M:(h + 1) * M], [(qq[:, 2 * h + c], kk[:, 2 * h + c]) for c in range(2)
                                                               for qq, kk in ((qsh, kxh), (qsh, kxl), (qsl, kxh))])
                mm.then_inc(s_xs, 1)

            def xvalues(i, first):
                pe.wait_ge(s_xn, i + 1)
                if not first:
                    pe.wait_ge(s_xpl, i)
                for h in range(H):
                    for t in range(MT):
                        b = h * MT + t
                        mm = pe.transpose(ps[:, 1, b * P:(b + 1) * P], T1[:, b * P:(b + 1) * P], ident)
                mm.then_inc(s_xt, 1)
                pe.wait_ge(s_xpl, i + 1)
                if not first:
                    pe.wait_ge(s_xy, i)
                for f in range(KT):
                    h = f // 2
                    mm = product(ps[:, 2, f * P:(f + 1) * P], [(vv[:, t, f * P:(f + 1) * P], pp[:, h * MT + t])
                                                               for t in range(MT) for vv, pp in ((vxh, pxh), (vxl, pxh), (vxh, pxl))])
                mm.then_inc(s_xpv, 1)

            pe.wait_ge(s_evac, N["vt"] + MT)
            xscores(0, True)
            xscores(1, False)
            xvalues(0, True)
            with pe.Fori(1, TT - 1) as i:
                xscores(i + 1, False)
                xvalues(i, False)
            xvalues(TT - 1, False)

            pe.wait_ge(s_xy, TT)
            units("wo", KT, r0h, r0l, ready=(s_ylo, KT))
            ffn("ffn2", r1h, r1l, r0h, r0l, R_WO, FT)
            stat("pool_stat", [(acc, s_acc, R_FFN2 + KT), (acc2, s_acc2, KT)])
            units("pool_u", KT, r1h, r1l, ready=(s_alo, R_FFN2))
            for g in range(4):
                n, u = N["pool_g"] + 4 * g, U["pool_g"] + 4 * g
                for j in range(2):
                    unit(n + j, u + j, j, (n + j) % 4, r1h, r1l)
                for j in range(2, 4):
                    unit(n + j, u + j, j % 2, (n + j) % 4, r0h, r0l, kts=range(2 * g, 2 * g + 2), ready=(s_plo, 2 * g))
            n = N["fgain"]
            slot_free(n)
            pe.wait_ge(s_frow, 16)
            for c0, c1 in HALVES:
                mm = pe.matmul(ps[:, n % 4, c0:c1], cst[0:1, C_ONES:C_ONES + P], frow[0:1, c0:c1], start=True, stop=True)
            mm.then_inc(s_mm, 1)
            units("pool_out", KT, r0h, r0l, ready=(s_plo, KT))
            for t in range(TT):
                n = N["final"] + t
                slot_free(n)
                for m in range(KT):
                    pe.wait_ge(s_evac, N["pool_out"] + m + 1)
                    mm = pe.transpose(ps[:, n % 4, m * P:(m + 1) * P], xt[:, m, t * P:(t + 1) * P], ident)
                mm.then_inc(s_mm, 1)

        @block.scalar
        def _(act):
            def step(n, u, j):
                act.wait_ge(s_mm, n + 1)
                if u + 2 < UNITS:
                    act.wait_ge(s_raw[j], landed(u + 2))
                    act.activation(w_hi[:, j], raw[:, j], ACT.Copy).then_inc(s_whi, 1)

            def loop_step(n0, u0, i, j):
                act.wait_ge(s_mm, 4 * i + (n0 + j + 1))
                act.wait_ge(s_raw[j % 2], 32 * i + landed(u0 + j + 2))
                act.activation(w_hi[:, j % 2], raw[:, j % 2], ACT.Copy).then_inc(s_whi, 1)

            def split_residual(n, r, m, xh, g, g_sq2=None):
                act.wait_ge(s_evac, n + 1)
                act.activation(xh[:, m], xt[:, m], ACT.Copy, scale=g[:, m:m + 1]).then_inc(s_ahi, 1)
                if r + m > 0:
                    act.wait_ge(s_acc, r + m)
                act.activation(T2, xt[:, m], ACT.Square).then_inc(s_sq, 1)
                if g_sq2 is not None:
                    if m > 0:
                        act.wait_ge(s_acc2, m)
                    act.activation(T3, xt[:, m], ACT.Square, scale=g_sq2[:, m:m + 1]).then_inc(s_sq2, 1)

            roots = [0]

            def root(n):
                act.wait_ge(s_evac, n + 1)
                act.activation(T2, T1, ACT.Sqrt).then_inc(s_sqrt, 1)
                roots[0] += 1

            def ffn(f, hh, pairs0, residual):
                pairs = pairs0
                hh_f = hh[:].rearrange("p t n -> p (t n)")
                root(N[f + "_stat"])
                for c, (t0, k) in enumerate(CHUNKS):
                    n0, u0 = N[f"{f}_up{c}"], U[f"{f}_up{c}"]
                    with act.Fori(0, k // 2) as i:
                        for q in range(2):
                            loop_step(n0, u0, i, 2 * q)
                            act.wait_ge(s_evac, 4 * i + (n0 + 2 * q + 1))
                            act.activation(T2, T1, ACT.Silu).then_inc(s_silu, 1)
                            loop_step(n0, u0, i, 2 * q + 1)
                            act.wait_ge(s_h, 2 * i + (pairs + q + 1))
                            act.wait_ge(s_rstd, 1)
                            act.activation(hh_f[:, bass.ds(i * (2 * S) + q * S, S)], T1, ACT.Copy).then_inc(s_hhi, 1)
                    pairs += k
                    n0, u0 = N[f"{f}_down{c}"], U[f"{f}_down{c}"]
                    if c < len(CHUNKS) - 1:
                        with act.Fori(0, 2) as i:
                            for j in range(4):
                                loop_step(n0, u0, i, j)
                    else:
                        for m in range(KT):
                            step(n0 + m, u0 + m, m % 2)
                            residual(n0 + m, m)

            act.wait_ge(s_cst, 16)
            act.activation(ident_r[:], ident, ACT.Copy)
            act.activation(mask_r[:], cst[:, C_MASK:C_MASK + P], ACT.Copy).then_inc(s_setup_act, 1)
            act.wait_ge(s_dve, 2)
            act.activation(small[0:1, 2:4], small[0:1, 0:2], ACT.Exp).then_inc(s_setup_act, 1)
            for m in range(KT):
                split_residual(N["xt"] + m, R_XT, m, r0h, gain[:, G_FFN1:G_FFN1 + KT])
            for u in range(2):
                act.wait_ge(s_raw[u], 16)
                act.activation(w_hi[:, u], raw[:, u], ACT.Copy).then_inc(s_whi, 1)
            ffn("ffn1", r1h, 0, lambda n, m: split_residual(n, R_FFN1, m, r0h, gain[:, G_MIX:G_MIX + KT]))
            root(N["win_stat"])
            for j in range(4):
                step(N["win"] + j, U["win"] + j, j % 2)
            with act.Fori(0, 5) as i:
                for j in range(4):
                    loop_step(N["win"] + 4, U["win"] + 4, i, j)

            act.wait_ge(s_evac, N["win"] + 24)
            act.activation(pa[:, 8:12], pa[:, 8:12], ACT.Silu).then_inc(s_sg, 1)

            def retention_chunk(i, first):
                act.wait_ge(s_rotd, i + 1)
                if not first:
                    act.wait_ge(s_o, i)
                act.activation(qkh[:], qk[:], ACT.Copy).then_inc(s_qkh, 1)
                act.wait_ge(s_vtr, i + 1)
                act.activation(rvh[:], bank(4).rearrange("p (h n) -> p h n", h=4), ACT.Copy).then_inc(s_vh, 1)
                act.wait_ge(s_kz, i + 1)
                act.activation(kzh[:], kz[:], ACT.Copy).then_inc(s_kzh, 1)
                act.wait_ge(s_inf, i + 1)
                act.activation(inh[:], inf, ACT.Copy).then_inc(s_inh, 1)
                act.wait_ge(s_o, i + 1)
                if not first:
                    act.wait_ge(s_rms, i)
                act.activation(rsq, bank(6).rearrange("p (h n) -> p h n", h=4), ACT.Square).then_inc(s_rsq, 1)
                act.wait_ge(s_rms, i + 1)
                act.activation(small[:, 8:12], small[:, 4:8], ACT.Sqrt).then_inc(s_rroot, 1)
                act.wait_ge(s_r, i + 1)
                act.activation(rsh[:], rs[:], ACT.Copy).then_inc(s_rh, 1)

            retention_chunk(0, True)
            with act.Fori(1, TT) as i:
                retention_chunk(i, False)

            act.wait_ge(s_y, TT)
            act.sem_inc(s_exp, 2)

            with act.Fori(0, H) as i:
                act.wait_ge(s_s, 16 * i + 1)
                act.wait_ge(s_y, TT)
                act.activation(dqh[:], pa_f[:, bass.ds(i * S + 12 * S, S)], ACT.Copy).then_inc(s_dqh, 1)
                act.activation(dkh[:], pb_f[:, bass.ds(i * S, S)], ACT.Copy).then_inc(s_dqh, 1)
                act.wait_ge(s_dvtr, i + 1)
                act.activation(dvh[:].rearrange("p t n -> p (t n)"), ps[:, 2], ACT.Copy).then_inc(s_dvh, 1)

                def exps(t):
                    w = (t + 1) * P
                    for c in range(2):
                        act.wait_ge(s_nm, 2 * (8 * i + t) + c + 1)
                        act.wait_ge(s_t, 8 * i + t + 1)
                        act.activation(e[t % 2][c][:, 0:w], ps[:, c, 0:w], ACT.Exp, bias=small[:, 16 + 2 * (t % 2) + c:17 + 2 * (t % 2) + c],
                                       scale=DIFF_SCALE, accum_out=small[:, 20 + 2 * (t % 2) + c:21 + 2 * (t % 2) + c]).then_inc(s_exp, 1)
                exps(0)
                for t in range(TT):
                    g = 8 * i + t
                    w = (t + 1) * P
                    if t + 1 < TT:
                        exps(t + 1)
                    act.wait_ge(s_t, g + 3)
                    act.wait_ge(s_pv, g + 1)
                    act.activation(pth[:, 0:t + 1].rearrange("p t n -> p (t n)"), ps[:, 2, 0:w], ACT.Copy).then_inc(s_pth, 1)
                act.wait_ge(s_pv, 8 * i + TT + 1)
                act.activation(T3, ps[:, 3], ACT.Square).then_inc(s_dsq, 1)
                act.wait_ge(s_dms, i + 1)
                act.activation(small[:, 32:40], small[:, 24:32], ACT.Sqrt).then_inc(s_droot, 1)

            def split_output(count, src, xh, g=None):
                for k in range(KT):
                    scale = g[:, k:k + 1] if g is not None else 1.0
                    act.activation(xh[:, k], src[:, k], ACT.Copy, scale=scale).then_inc(s_yhi, 1)

            act.wait_ge(s_dy, H + 1)
            split_output(0, y, r1h, ygain)
            for m in range(KT):
                step(N["wout"] + m, U["wout"] + m, m % 2)
                split_residual(N["wout"] + m, R_WOUT, m, r0h, gain[:, G_X:G_X + KT])
            root(N["wq_stat"])
            with act.Fori(0, 2) as i:
                for j in range(4):
                    loop_step(N["wq"], U["wq"], i, j)

            act.wait_ge(s_mem, 16)
            for t in range(MT):
                act.activation((T3, T2)[t], memr[:, t], ACT.Square, accum_out=small[:, t:t + 1]).then_inc(s_msq, 1)
            act.wait_ge(s_mms, 1)
            act.activation(small[:, 4:6], small[:, 2:4], ACT.Sqrt).then_inc(s_mroot, 1)
            for q in range(2):
                n = N["memt"] + q
                act.wait_ge(s_mm, n + 1)
                for k in range(4):
                    act.activation(memh[:, 4 * q + k], ps[:, n % 4, k * M:(k + 1) * M], ACT.Copy,
                                   scale=gain[:, G_MEM + 4 * q + k:G_MEM + 4 * q + k + 1]).then_inc(s_mhi, 1)
            for m in range(2 * KT):
                n = N["wkv"] + m
                step(n, U["wkv"] + m, m % 2)
                if m < KT:
                    act.activation(kxh[:, m], ps[:, n % 4, 0:M], ACT.Copy).then_inc(s_khi, 1)
            for t in range(MT):
                n = N["vt"] + t
                act.wait_ge(s_mm, n + 1)
                act.activation(vxh[:, t], ps[:, n % 4], ACT.Copy).then_inc(s_vxh, 1)

            def xquery(i):
                act.activation(qsh[:], qx[:, :, bass.ds(i * P, P)], ACT.Copy).then_inc(s_qh, 1)

            def xstep(i, first, last):
                act.wait_ge(s_xnm, i + 1)
                if not first:
                    act.wait_ge(s_xt, i)
                for h in range(H):
                    ins = act.activation(T1[:, h * M:(h + 1) * M], ps[:, 0, h * M:(h + 1) * M], ACT.Exp, scale=XATTN_SCALE,
                                         bias=small[:, 16 + h:17 + h], accum_out=small[:, 20 + h:21 + h])
                ins.then_inc(s_xe, 1)
                if not last:
                    act.wait_ge(s_xs, i + 1)
                    act.wait_ge(s_mem, 16)
                    xquery(i + 1)
                act.wait_ge(s_xt, i + 1)
                if not first:
                    act.wait_ge(s_xpv, i)
                act.activation(pxh[:].rearrange("p k n -> p (k n)"), ps[:, 1], ACT.Copy).then_inc(s_xph, 1)

            act.wait_ge(s_evac, N["vt"] + MT)
            xquery(0)
            xstep(0, True, False)
            with act.Fori(1, TT - 1) as i:
                xstep(i, False, False)
            xstep(TT - 1, False, True)
            act.wait_ge(s_xy, TT)
            split_output(KT, y2, r0h)
            for m in range(KT):
                step(N["wo"] + m, U["wo"] + m, m % 2)
                split_residual(N["wo"] + m, R_WO, m, r1h, gain[:, G_FFN2:G_FFN2 + KT])
            ffn("ffn2", r0h, FT, lambda n, m: split_residual(n, R_FFN2, m, r1h, gain2, gain[:, G_FIN:G_FIN + KT]))

            root(N["pool_stat"])
            act.wait_ge(s_ms2, 1)
            act.activation(T2, T1, ACT.Sqrt).then_inc(s_sqrt, 1)
            for t in range(KT):
                step(N["pool_u"] + t, U["pool_u"] + t, t % 2)
                act.wait_ge(s_pd, t + 1)
                act.activation(r0h[:, t], (T3, T2)[t // 2 % 2], ACT.Copy).then_inc(s_phi, 1)
            for g in range(4):
                n, u = N["pool_g"] + 4 * g, U["pool_g"] + 4 * g
                for j in range(2):
                    step(n + j, u + j, j)
                    act.wait_ge(s_evac, n + j + 1)
                    act.activation((T1, T2)[j], (T1, T2)[j], ACT.Silu).then_inc(s_psilu, 1)
                for j in range(2):
                    step(n + 2 + j, u + 2 + j, j)
                    act.wait_ge(s_yy, 2 * g + j + 1)
                    act.wait_ge(s_mm, n + 4)
                    act.activation(r0h[:, 2 * g + j], T3, ACT.Copy).then_inc(s_phi, 1)
            for m in range(KT):
                step(N["pool_out"] + m, U["pool_out"] + m, m % 2)
            for t in range(TT):
                n = N["final"] + t
                act.wait_ge(s_mm, n + 1)
                act.activation(T3, ps[:, n % 4], ACT.Square, accum_out=small[:, t:t + 1]).then_inc(s_fsq, 1)
                act.wait_ge(s_fms, t + 1)
                act.activation(small[:, 16 + t:17 + t], small[:, 8 + t:9 + t], ACT.Sqrt).then_inc(s_froot, 1)

        @block.vector
        def _(dve):
            chain = [0]

            def link(ins):
                chain[0] += 1
                ins.then_inc(s_dve, 1)
                dve.wait_ge(s_dve, chain[0])

            def step(n, u, j):
                if u + 2 < UNITS:
                    dve.wait_ge(s_whi, u + 3)
                    dve.tensor_tensor(w_lo[:, j], raw[:, j], w_hi[:, j].bitcast(F32), ALU.subtract).then_inc(s_wlo, 1)
                    dve.wait_ge(s_wlo, u + 3)
                dve.wait_ge(s_mm, n + 1)

            def loop_step(n0, u0, i, j):
                dve.wait_ge(s_whi, 4 * i + (u0 + j + 3))
                dve.tensor_tensor(w_lo[:, j % 2], raw[:, j % 2], w_hi[:, j % 2].bitcast(F32), ALU.subtract).then_inc(s_wlo, 1)
                dve.wait_ge(s_wlo, 4 * i + (u0 + j + 3))
                dve.wait_ge(s_mm, 4 * i + (n0 + j + 1))

            def split_residual(r, m, xh, xl, g, two=False):
                dve.wait_ge(s_ahi, r + m + 1)
                dve.scalar_tensor_tensor(out=xl[:, m], in0=xt[:, m], scalar=g[:, m:m + 1], in1=xh[:, m].bitcast(F32),
                                         op0=ALU.mult, op1=ALU.subtract).then_inc(s_alo, 1)
                for total, part, done, own, r0 in ((acc, T2, s_sq, s_acc, r),) + (((acc2, T3, s_sq2, s_acc2, 0),) if two else ()):
                    dve.wait_ge(done, r0 + m + 1)
                    if m == 0:
                        dve.tensor_copy(total[:], part).then_inc(own, 1)
                    else:
                        dve.wait_ge(own, r0 + m)
                        dve.tensor_tensor(total[:], total[:], part, ALU.add).then_inc(own, 1)

            roots = [0]

            def factors(n, dst):
                dve.wait_ge(s_mm, n + 1)
                dve.tensor_scalar(T1, ps[:, n % 4], 1.0 / D, EPS, ALU.mult, ALU.add).then_inc(s_evac, 1)
                inverse(dst)

            def inverse(dst):
                roots[0] += 1
                dve.wait_ge(s_sqrt, roots[0])
                dve.reciprocal(dst[:], T2).then_inc(s_rstd, 1)
                dve.wait_ge(s_rstd, roots[0])

            def residual_add(n, m, scale):
                dve.wait_ge(s_evac, n)
                dve.scalar_tensor_tensor(out=xt[:, m], in0=ps[:, n % 4], scalar=scale, in1=xt[:, m],
                                         op0=ALU.mult, op1=ALU.add).then_inc(s_evac, 1)

            def ffn(f, hh, hl, pairs0, split):
                pairs = pairs0
                hh_f, hl_f = (t[:].rearrange("p t n -> p (t n)") for t in (hh, hl))
                xt_f = xt[:].rearrange("p t n -> p (t n)")
                factors(N[f + "_stat"], rstd)
                for c, (t0, k) in enumerate(CHUNKS):
                    n0, u0 = N[f"{f}_up{c}"], U[f"{f}_up{c}"]
                    with dve.Fori(0, k // 2) as i:
                        for q in range(2):
                            loop_step(n0, u0, i, 2 * q)
                            dve.tensor_tensor(T1, ps[:, (n0 + 2 * q) % 4], rstd[:], ALU.mult).then_inc(s_evac, 1)
                            loop_step(n0, u0, i, 2 * q + 1)
                            dve.tensor_tensor(T3, ps[:, (n0 + 2 * q + 1) % 4], rstd[:], ALU.mult).then_inc(s_evac, 1)
                            dve.wait_ge(s_silu, 2 * i + (pairs + q + 1))
                            dve.wait_ge(s_evac, 4 * i + (n0 + 2 * q + 2))
                            dve.tensor_tensor(T1, T2, T3, ALU.mult).then_inc(s_h, 1)
                            dve.wait_ge(s_hhi, 2 * i + (pairs + q + 1))
                            at_t = bass.ds(i * (2 * S) + q * S, S)
                            dve.tensor_tensor(hl_f[:, at_t], T1, hh_f[:, at_t].bitcast(F32), ALU.subtract).then_inc(s_hlo, 1)
                    pairs += k
                    n0, u0 = N[f"{f}_down{c}"], U[f"{f}_down{c}"]
                    if c < len(CHUNKS) - 1:
                        with dve.Fori(0, 2) as i:
                            for j in range(4):
                                loop_step(n0, u0, i, j)
                                at_m = bass.ds(i * (4 * S) + j * S, S)
                                dve.wait_ge(s_evac, 4 * i + (n0 + j))
                                dve.scalar_tensor_tensor(out=xt_f[:, at_m], in0=ps[:, (n0 + j) % 4], scalar=0.5, in1=xt_f[:, at_m],
                                                         op0=ALU.mult, op1=ALU.add).then_inc(s_evac, 1)
                    else:
                        for m in range(KT):
                            step(n0 + m, u0 + m, m % 2)
                            residual_add(n0 + m, m, 0.5)
                            split(m)

            for t in (t1, t2, t3):
                dve.memset(t[:, 0:PAD], 0.0)
            dve.memset(lamv[:, 0:1], 1.0)
            dve.wait_ge(s_lrow, 64)
            prod = T3[0:1, 0:128].rearrange("p (a n) -> p a n", a=2)
            link(dve.tensor_tensor(prod, lrow[0:1, 0::2, :], lrow[0:1, 1::2, :], ALU.mult))
            link(dve.tensor_reduce(small[0:1, 0:2], prod, AX.X, ALU.add))
            dve.wait_ge(s_setup_act, 2)
            link(dve.tensor_tensor(small[0:1, 6:7], small[0:1, 3:4], small[0:1, 2:3], ALU.subtract))
            for c in (4, 5):
                ins = dve.tensor_scalar(small[0:1, c:c + 1], small[0:1, 6:7], -LAMBDA_INIT, None, ALU.add)
                if c == 4:
                    link(ins)
            ins.then_inc(s_lam, 1)
            dve.wait_ge(s_mm, 1)
            link(dve.tensor_copy(gain[:], ps[:, 0, 0:G_ROWS]))
            link(dve.tensor_tensor(gain2[:], gain[:, G_FIN:G_FIN + KT], gain[:, G_NORM2:G_NORM2 + KT], ALU.mult))
            dve.tensor_copy(ygain[:, 0:4], gain[:, G_RET:G_RET + 4])
            dve.tensor_scalar(ygain[:, 4:8], gain[:, G_DIFF:G_DIFF + 4], 1.0 - LAMBDA_INIT, None, ALU.mult)
            dve.tensor_copy(lamv[:, 1:2], ps[:, 0, 512:513]).then_inc(s_evac, 1)
            for m in range(KT):
                n = N["xt"] + m
                dve.wait_ge(s_mm, n + 1)
                dve.tensor_copy(xt[:, m], ps[:, n % 4]).then_inc(s_evac, 1)
                split_residual(R_XT, m, r0h, r0l, gain[:, G_FFN1:G_FFN1 + KT])
            for u in range(2):
                dve.wait_ge(s_whi, u + 1)
                dve.tensor_tensor(w_lo[:, u], raw[:, u], w_hi[:, u].bitcast(F32), ALU.subtract).then_inc(s_wlo, 1)
            ffn("ffn1", r1h, r1l, 0, lambda m: split_residual(R_FFN1, m, r0h, r0l, gain[:, G_MIX:G_MIX + KT]))

            factors(N["win_stat"], rstd)
            for dst, count, first in ((pa_f, 16, 0), (pb_f, 8, 16)):
                if first == 16:
                    dve.wait_ge(s_spill, 16)
                with dve.Fori(0, count // 4) as i:
                    for j in range(4):
                        loop_step(N["win"] + first, U["win"] + first, i, j)
                        dve.tensor_tensor(dst[:, bass.ds(i * (4 * S) + j * S, S)], ps[:, (N["win"] + first + j) % 4], rstd[:],
                                          ALU.mult).then_inc(s_evac, 1)

            zeta = cst[:, C_ZETA:C_ZETA + P].unsqueeze(1).to_broadcast([P, 2, P])
            decay = cst[:, C_DECAY:C_DECAY + 4 * P].rearrange("p (h n) -> p h n", h=4)

            def retention_chunk(i, first):
                dve.wait_ge(s_vh, i + 1)
                dve.tensor_tensor(rvl[:], bank(4).rearrange("p (h n) -> p h n", h=4), rvh[:].bitcast(F32), ALU.subtract).then_inc(s_vl, 1)
                dve.wait_ge(s_qkh, i + 1)
                dve.tensor_tensor(qkl[:], qk[:], qkh[:].bitcast(F32), ALU.subtract).then_inc(s_qkl, 1)
                dve.wait_ge(s_ktr, i + 1)
                dve.tensor_tensor(kz[:], bank(5)[:, 0:2 * P].rearrange("p (c n) -> p c n", c=2), zeta, ALU.mult).then_inc(s_kz, 1)
                dve.wait_ge(s_inner, i + 1)
                dve.tensor_tensor(inf, ps[:, 0:2].rearrange("p a (b n) -> p (a b) n", b=2)[:, :, 0:P], decay, ALU.mult).then_inc(s_inf, 1)
                dve.wait_ge(s_kzh, i + 1)
                dve.tensor_tensor(kzl[:], kz[:], kzh[:].bitcast(F32), ALU.subtract).then_inc(s_kzl, 1)
                dve.wait_ge(s_inh, i + 1)
                dve.tensor_tensor(inl[:], inf, inh[:].bitcast(F32), ALU.subtract).then_inc(s_inl, 1)
                dve.wait_ge(s_kv, i + 1)
                if not first:
                    dve.wait_ge(s_rl, i)
                for c, b in ((0, bank(7)), (1, bank(5))):
                    for h in range(H):
                        rows, kv = slice(32 * h, 32 * h + 32), b[32 * h:32 * h + 32, h * P:(h + 1) * P]
                        if first:
                            ins = dve.tensor_copy(rs[rows, c], kv)
                        else:
                            ins = dve.scalar_tensor_tensor(out=rs[rows, c], in0=rs[rows, c], scalar=cst[rows, C_GCH:C_GCH + 1],
                                                           in1=kv, op0=ALU.mult, op1=ALU.add)
                ins.then_inc(s_r, 1)
                dve.wait_ge(s_rsq, i + 1)
                dve.tensor_reduce(small[:, 12:16], rsq, AX.X, ALU.add).then_inc(s_ra, 1)
                dve.wait_ge(s_ra, 4 * i + 1)
                dve.tensor_tensor(small[:, 56:60], small[:, 12:16], cst[:, C_XI2:C_XI2 + 4], ALU.mult).then_inc(s_ra, 1)
                dve.wait_ge(s_ra, 4 * i + 2)
                dve.tensor_scalar(small[:, 4:8], small[:, 56:60], EPS, None, ALU.add).then_inc(s_rms, 1)
                dve.wait_ge(s_rroot, i + 1)
                dve.reciprocal(small[:, 12:16], small[:, 8:12]).then_inc(s_ra, 1)
                dve.wait_ge(s_ra, 4 * i + 3)
                dve.tensor_tensor(small[:, 60:64], small[:, 12:16], cst[:, C_XI:C_XI + 4], ALU.mult).then_inc(s_ra, 1)
                dve.wait_ge(s_ra, 4 * i + 4)
                dve.tensor_tensor(on, bank(6).rearrange("p (h n) -> p h n", h=4),
                                  small[:, 60:64].unsqueeze(2).to_broadcast([P, 4, P]), ALU.mult).then_inc(s_on, 1)
                dve.wait_ge(s_rh, i + 1)
                dve.tensor_tensor(rsl[:], rs[:], rsh[:].bitcast(F32), ALU.subtract).then_inc(s_rl, 1)
                dve.wait_ge(s_ytr, i + 1)
                dve.tensor_tensor(y[:, 0:4, bass.ds(i * P, P)], bank(4).rearrange("p (h n) -> p h n", h=4),
                                  pa[:, 8:12, bass.ds(i * P, P)], ALU.mult).then_inc(s_y, 1)

            dve.wait_ge(s_sg, 1)
            retention_chunk(0, True)
            with dve.Fori(1, TT) as i:
                retention_chunk(i, False)

            dve.sem_inc(s_dy, 1)
            with dve.Fori(0, H) as i:
                dve.wait_ge(s_dy, i + 1)
                dve.tensor_copy(T3, pb_f[:, bass.ds(i * S + 4 * S, S)]).then_inc(s_vt, 1)
                dve.wait_ge(s_dqh, 2 * i + 1)
                dve.tensor_tensor(dql[:], pa_f[:, bass.ds(i * S + 12 * S, S)], dqh[:].bitcast(F32), ALU.subtract)
                dve.wait_ge(s_dqh, 2 * i + 2)
                dve.tensor_tensor(dkl[:], pb_f[:, bass.ds(i * S, S)], dkh[:].bitcast(F32), ALU.subtract).then_inc(s_dql, 1)
                dve.wait_ge(s_dvh, i + 1)
                dve.tensor_tensor(dvl[:].rearrange("p t n -> p (t n)"), ps[:, 2], dvh[:].rearrange("p t n -> p (t n)").bitcast(F32),
                                  ALU.subtract).then_inc(s_dvl, 1)

                def maxima(t):
                    for c in range(2):
                        k = 2 * (8 * i + t) + c
                        col = 2 * (t % 2) + c
                        dve.wait_ge(s_s, k + 2)
                        dve.tensor_reduce(small[:, 52 + c:53 + c], ps[:, c, 0:(t + 1) * P], AX.X, ALU.max).then_inc(s_mx, 1)
                        dve.wait_ge(s_mx, k + 1)
                        dve.tensor_scalar(small[:, 16 + col:17 + col], small[:, 52 + c:53 + c], -DIFF_SCALE, None, ALU.mult).then_inc(s_nm, 1)

                maxima(0)
                for t in range(TT):
                    g = 8 * i + t
                    w = (t + 1) * P
                    e0, e1 = (x[:, 0:w] for x in e[t % 2])
                    dve.wait_ge(s_exp, 2 * g + 4)
                    dve.reciprocal(small[:, 48:50], small[:, 20 + 2 * (t % 2):22 + 2 * (t % 2)]).then_inc(s_da, 1)
                    dve.wait_ge(s_da, 3 * g + 1)
                    dve.tensor_tensor(small[:, 50:52], small[:, 48:50], lamv[:], ALU.mult).then_inc(s_da, 1)
                    dve.wait_ge(s_da, 3 * g + 2)
                    dve.tensor_scalar(e0, e0, small[:, 50:51], None, ALU.mult).then_inc(s_da, 1)
                    dve.wait_ge(s_da, 3 * g + 3)
                    dve.scalar_tensor_tensor(out=e1, in0=e1, scalar=small[:, 51:52], in1=e0, op0=ALU.mult, op1=ALU.add).then_inc(s_a, 1)
                    if t + 1 < TT:
                        maxima(t + 1)
                    dve.wait_ge(s_pth, g + 1)
                    dve.tensor_tensor(ptl[:, 0:t + 1].rearrange("p t n -> p (t n)"), ps[:, 2, 0:w],
                                      pth[:, 0:t + 1].rearrange("p t n -> p (t n)").bitcast(F32), ALU.subtract).then_inc(s_ptl, 1)
                dve.wait_ge(s_dsq, i + 1)
                dve.tensor_reduce(small[:, 40:48], T3.rearrange("p (t n) -> p t n", t=TT), AX.X, ALU.add).then_inc(s_dn, 1)
                dve.wait_ge(s_dn, 2 * i + 1)
                dve.tensor_scalar(small[:, 24:32], small[:, 40:48], 1.0 / P, EPS, ALU.mult, ALU.add).then_inc(s_dms, 1)
                dve.wait_ge(s_droot, i + 1)
                dve.reciprocal(small[:, 40:48], small[:, 32:40]).then_inc(s_dn, 1)
                dve.wait_ge(s_dn, 2 * i + 2)
                dve.tensor_tensor(rfin[:].rearrange("p (t n) -> p t n", t=TT), ps[:, 3].rearrange("p (t n) -> p t n", t=TT),
                                  small[:, 40:48].unsqueeze(2).to_broadcast([P, TT, P]), ALU.mult).then_inc(s_don, 1)
                dve.wait_ge(s_dytr, i + 1)
                dve.tensor_copy(y_f[:, bass.ds(i * S + 4 * S, S)], ps[:, 2]).then_inc(s_dy, 1)

            def split_output(count, src, xh, xl, g=None):
                for k in range(KT):
                    dve.wait_ge(s_yhi, count + k + 1)
                    dve.scalar_tensor_tensor(out=xl[:, k], in0=src[:, k], scalar=1.0 if g is None else g[:, k:k + 1],
                                             in1=xh[:, k].bitcast(F32), op0=ALU.mult, op1=ALU.subtract).then_inc(s_ylo, 1)

            split_output(0, y, r1h, r1l, ygain)
            dve.wait_ge(s_reload, 16)
            for m in range(KT):
                step(N["wout"] + m, U["wout"] + m, m % 2)
                residual_add(N["wout"] + m, m, 1.0)
                split_residual(R_WOUT, m, r0h, r0l, gain[:, G_X:G_X + KT])
            factors(N["wq_stat"], rstd)
            qx_f = qx[:].rearrange("p t n -> p (t n)")
            with dve.Fori(0, 2) as i:
                for j in range(4):
                    loop_step(N["wq"], U["wq"], i, j)
                    dve.tensor_tensor(qx_f[:, bass.ds(i * (4 * S) + j * S, S)], ps[:, (N["wq"] + j) % 4], rstd[:],
                                      ALU.mult).then_inc(s_evac, 1)

            dve.wait_ge(s_msq, MT)
            dve.tensor_scalar(small[:, 2:4], small[:, 0:2], 1.0 / D, EPS, ALU.mult, ALU.add).then_inc(s_mms, 1)
            dve.wait_ge(s_mroot, 1)
            link(dve.reciprocal(small[:, 6:8], small[:, 4:6]))
            for t in range(MT):
                ins = dve.tensor_scalar(memr[:, t], memr[:, t], small[:, 6 + t:7 + t], None, ALU.mult)
            ins.then_inc(s_mn, 1)
            for q in range(2):
                n = N["memt"] + q
                for k in range(4):
                    f = 4 * q + k
                    dve.wait_ge(s_mhi, 4 * q + 4)
                    ins = dve.scalar_tensor_tensor(out=meml[:, f], in0=ps[:, n % 4, k * M:(k + 1) * M], scalar=gain[:, G_MEM + f:G_MEM + f + 1],
                                                   in1=memh[:, f].bitcast(F32), op0=ALU.mult, op1=ALU.subtract)
                ins.then_inc(s_evac, 1)
            for m in range(2 * KT):
                n = N["wkv"] + m
                step(n, U["wkv"] + m, m % 2)
                if m < KT:
                    dve.wait_ge(s_khi, m + 1)
                    dve.tensor_tensor(kxl[:, m], ps[:, n % 4, 0:M], kxh[:, m].bitcast(F32), ALU.subtract).then_inc(s_evac, 1)
                else:
                    dve.tensor_copy(vf[:, m - KT], ps[:, n % 4, 0:M]).then_inc(s_evac, 1)
            for t in range(MT):
                dve.wait_ge(s_vxh, t + 1)
                dve.tensor_tensor(vxl[:, t], ps[:, (N["vt"] + t) % 4], vxh[:, t].bitcast(F32), ALU.subtract).then_inc(s_evac, 1)

            def xquery(i):
                dve.wait_ge(s_qh, i + 1)
                dve.tensor_tensor(qsl[:], qx[:, :, bass.ds(i * P, P)], qsh[:].bitcast(F32), ALU.subtract).then_inc(s_ql, 1)

            def xout(i):
                dve.wait_ge(s_xpv, i + 1)
                dve.tensor_copy(y2[:, :, bass.ds(i * P, P)], ps[:, 2].rearrange("p (k n) -> p k n", k=KT)).then_inc(s_xy, 1)

            def xstep(i, first, last):
                dve.wait_ge(s_xs, i + 1)
                dve.tensor_reduce(small[:, 52:56], ps[:, 0].rearrange("p (h n) -> p h n", h=H), AX.X, ALU.max).then_inc(s_xa, 1)
                dve.wait_ge(s_xa, 2 * i + 1)
                dve.tensor_scalar(small[:, 16:20], small[:, 52:56], -XATTN_SCALE, None, ALU.mult).then_inc(s_xnm, 1)
                if not first:
                    xout(i - 1)
                if not last:
                    xquery(i + 1)
                dve.wait_ge(s_xe, i + 1)
                dve.reciprocal(small[:, 48:52], small[:, 20:24]).then_inc(s_xa, 1)
                dve.wait_ge(s_xa, 2 * i + 2)
                v = T1.rearrange("p (h n) -> p h n", h=H)
                dve.tensor_tensor(v, v, small[:, 48:52].unsqueeze(2).to_broadcast([P, H, M]), ALU.mult).then_inc(s_xn, 1)
                dve.wait_ge(s_xph, i + 1)
                dve.tensor_tensor(pxl[:].rearrange("p k n -> p (k n)"), ps[:, 1], pxh[:].rearrange("p k n -> p (k n)").bitcast(F32),
                                  ALU.subtract).then_inc(s_xpl, 1)

            xquery(0)
            xstep(0, True, False)
            with dve.Fori(1, TT - 1) as i:
                xstep(i, False, False)
            xstep(TT - 1, False, True)
            xout(TT - 1)
            split_output(KT, y2, r0h, r0l)
            for m in range(KT):
                step(N["wo"] + m, U["wo"] + m, m % 2)
                residual_add(N["wo"] + m, m, 1.0)
                split_residual(R_WO, m, r1h, r1l, gain[:, G_FFN2:G_FFN2 + KT])
            ffn("ffn2", r0h, r0l, FT, lambda m: split_residual(R_FFN2, m, r1h, r1l, gain2, True))

            factors(N["pool_stat"], rfin)
            n = N["pool_stat"] + 1
            dve.wait_ge(s_mm, n + 1)
            dve.tensor_tensor(T1, ps[:, n % 4], rfin[:], ALU.mult).then_inc(s_evac, 1)
            dve.wait_ge(s_evac, n + 1)
            link(dve.tensor_tensor(T3, T1, rfin[:], ALU.mult))
            dve.tensor_scalar(T1, T3, 1.0 / D, EPS, ALU.mult, ALU.add).then_inc(s_ms2, 1)
            inverse(rstd)
            link(dve.tensor_tensor(rstd[:], rstd[:], rfin[:], ALU.mult))
            for t in range(KT):
                n = N["pool_u"] + t
                g = t // 2
                window = 2 << g
                step(n, U["pool_u"] + t, t % 2)
                dve.tensor_tensor(T1, ps[:, n % 4], rstd[:], ALU.mult).then_inc(s_evac, 1)
                dve.wait_ge(s_evac, n + 1)
                src, dst, other = t1, t2, t3
                for k in range(g + 1):
                    sh = 1 << k
                    link(dve.tensor_tensor(dst[:, PAD:], src[:, PAD:], src[:, PAD - sh:PAD - sh + S], ALU.add))
                    src, dst, other = dst, (t3 if dst is t2 else t2), None
                head = slice(PAD, 2 * PAD)
                rest = slice(2 * PAD, PAD + S)
                dve.scalar_tensor_tensor(out=dst[:, rest], in0=src[:, rest], scalar=1.0 / window, in1=t1[:, rest],
                                         op0=ALU.mult, op1=ALU.subtract)
                link(dve.tensor_tensor(small[:, 0:PAD], src[:, head], cst[:, C_INV + 16 * g:C_INV + 16 * (g + 1)], ALU.mult))
                dve.tensor_tensor(dst[:, head], small[:, 0:PAD], t1[:, head], ALU.subtract).then_inc(s_pd, 1)
                dve.wait_ge(s_phi, t + 1)
                dve.tensor_tensor(r0l[:, t], dst[:, PAD:], r0h[:, t].bitcast(F32), ALU.subtract).then_inc(s_plo, 1)
            for g in range(4):
                n, u = N["pool_g"] + 4 * g, U["pool_g"] + 4 * g
                for j in range(2):
                    step(n + j, u + j, j)
                    dve.tensor_tensor((T1, T2)[j], ps[:, (n + j) % 4], rstd[:], ALU.mult).then_inc(s_evac, 1)
                for j in range(2):
                    f = 2 * g + j
                    step(n + 2 + j, u + 2 + j, j)
                    dve.tensor_scalar(T3, ps[:, (n + 2 + j) % 4], gain[:, G_PB + f:G_PB + f + 1], gain[:, G_PS + f:G_PS + f + 1],
                                      ALU.add, ALU.mult).then_inc(s_evac, 1)
                    dve.wait_ge(s_evac, n + 3 + j)
                    dve.wait_ge(s_psilu, f + 1)
                    dve.tensor_tensor(T3, T3, (T1, T2)[j], ALU.mult).then_inc(s_yy, 1)
                    dve.wait_ge(s_phi, KT + f + 1)
                    dve.tensor_tensor(r0l[:, f], T3, r0h[:, f].bitcast(F32), ALU.subtract).then_inc(s_plo, 1)
            n = N["fgain"]
            dve.wait_ge(s_mm, n + 1)
            dve.tensor_copy(fgain[:], ps[:, n % 4]).then_inc(s_evac, 1)
            for m in range(KT):
                n = N["pool_out"] + m
                x1 = (T1, T3)[m % 2]
                link(dve.scalar_tensor_tensor(out=x1, in0=xt[:, m], scalar=gain[:, G_FIN + m:G_FIN + m + 1], in1=rfin[:],
                                              op0=ALU.mult, op1=ALU.mult))
                step(n, U["pool_out"] + m, m % 2)
                dve.tensor_tensor(xt[:, m], x1, ps[:, n % 4], ALU.add).then_inc(s_evac, 1)
            for t in range(TT):
                n = N["final"] + t
                dve.wait_ge(s_fsq, t + 1)
                dve.tensor_scalar(small[:, 8 + t:9 + t], small[:, t:t + 1], 1.0 / D, EPS, ALU.mult, ALU.add).then_inc(s_fms, 1)
                dve.wait_ge(s_froot, t + 1)
                link(dve.reciprocal(small[:, 24 + t:25 + t], small[:, 16 + t:17 + t]))
                if t >= 2:
                    dve.wait_ge(s_out[t % 2], 16 * (t // 2))
                dve.scalar_tensor_tensor(out=outrow[t % 2], in0=ps[:, n % 4], scalar=small[:, 24 + t:25 + t], in1=fgain[:],
                                         op0=ALU.mult, op1=ALU.mult).then_inc(s_evac, 1)

        @block.gpsimd
        def _(pool):
            cos, sin = (lambda i, k=k: rott[:, k:k + 1, bass.ds(i * P, P)].to_broadcast([P, 2, P]) for k in range(2))

            def retention_chunk(i, first):
                at_i = bass.ds(i * P, P)
                left, right = pa[:, 0:4:2, at_i], pa[:, 1:4:2, at_i]
                if not first:
                    pool.wait_ge(s_qkl, i)
                    pool.wait_ge(s_ktr, i)
                for k, (half, table) in enumerate(((left, cos), (right, sin), (left, sin), (right, cos))):
                    pool.tensor_tensor(rtmp[k], half, table(i), ALU.mult).then_inc(s_pool, 1)
                pool.wait_ge(s_pool, 4 * i + 4)
                pool.tensor_tensor(qk[:, 0:4:2], rtmp[0], rtmp[1], ALU.subtract)
                pool.tensor_tensor(qk[:, 1:4:2], rtmp[2], rtmp[3], ALU.add)
                pool.tensor_copy(vc[:], pa[:, 4:8, at_i]).then_inc(s_rotd, 1)

            pool.wait_ge(s_rot, 16)
            retention_chunk(0, True)
            with pool.Fori(1, TT) as i:
                retention_chunk(i, False)


_INS = ["x", "mem", "ffn1_norm", "ffn1_w_gate", "ffn1_w_up", "ffn1_w_down", "mix_norm", "w_in", "ret_out_norm",
        "diff_lq1", "diff_lk1", "diff_lq2", "diff_lk2", "diff_out_norm", "w_out", "xattn_norm", "mem_norm",
        "xattn_wq", "xattn_wkv", "xattn_wo", "ffn2_norm", "ffn2_w_gate", "ffn2_w_up", "ffn2_w_down", "final_norm",
        "norm_w_2", "pool_in_w_2", "pool_group_w_2", "pool_group_b_2", "pool_scale_2", "pool_out_w_2", "final_norm_w_2"]


def kernel(**inputs):
    import concourse.bacc as bacc
    from concourse.bass_utils import run_bass_kernel_spmd

    nc = bacc.Bacc("TRN2", target_bir_lowering=False, num_devices=1, dynamic_dma_scratch_size=1024)
    arrays = {name: np.ascontiguousarray(inputs[name]) for name in _INS}
    arrays["constants"] = constants()
    arrays["rotary"] = rotary_tables()
    aps = {name: nc.dram_tensor("in_" + name, v.shape, mybir.dt.from_np(v.dtype), kind="ExternalInput").ap()
           for name, v in arrays.items()}
    spill = nc.dram_tensor("spill", (P, KT, S), F32, kind="Internal").ap()
    out = nc.dram_tensor("out_0", (1, S, D), F32, kind="ExternalOutput").ap()
    build(nc, aps, aps["constants"], aps["rotary"], spill, out)
    r = run_bass_kernel_spmd(nc, [{"in_" + k: v for k, v in arrays.items()}], core_ids=[0])
    return r.results[0]["out_0"]
```

```python
from contextlib import ExitStack

import numpy as np
import concourse.bass as bass
from concourse import mybir

ALU = mybir.AluOpType
ACT = mybir.ActivationFunctionType
AX = mybir.AxisListType
F32 = mybir.dt.float32
F32R = mybir.dt.float32r

P = 128
S = 1024
D = 1024
KT = D // P
TT = S // P
FF = 2816
FT = FF // P
CHUNKS = ((0, 8), (8, 8), (16, 6))
M = 256
MT = M // P
H = 4
EPS = 1e-6
LAMBDA_INIT = 0.2
DIFF_SCALE = 0.125
XATTN_SCALE = 0.0625
HALVES = ((0, 512), (512, 1024))

G_FFN1, G_MIX, G_X, G_MEM, G_FFN2, G_FIN, G_NORM2, G_PB, G_PS, G_RET, G_DIFF, G_ROWS = (
    0, 8, 16, 24, 32, 40, 48, 56, 64, 72, 76, 80)

C_ID, C_MASK, C_ONES, C_DECAY, C_ZETA, C_XI, C_XI2, C_GCH, C_INV, C_COLS = (
    0, 128, 256, 384, 896, 1024, 1028, 1032, 1033, 1033 + 64)


def constants():
    c = np.zeros((P, C_COLS), np.float32)
    n = np.arange(P)
    c[:, C_ID:C_ID + P] = np.eye(P)
    c[:, C_MASK:C_MASK + P] = np.where(n[None, :] <= n[:, None], 0.0, -2.0 ** 100)
    c[:, C_ONES:C_ONES + P] = 1.0
    log_g = np.log(1.0 - 2.0 ** (-5.0 - np.arange(H)))
    for h in range(H):
        c[:, C_DECAY + h * P:C_DECAY + (h + 1) * P] = np.where(
            n[:, None] <= n[None, :], np.exp(-(n[:, None] + 1.0) * log_g[h]), 0.0)
        c[:, C_ZETA + 32 * h:C_ZETA + 32 * (h + 1)] = np.exp((P - 1.0 - n) * log_g[h])[:, None]
        xi = np.exp((n + 1.0) * log_g[h]) / 8.0
        c[:, C_XI + h] = xi
        c[:, C_XI2 + h] = xi * xi / P
        c[32 * h:32 * h + 32, C_GCH] = np.exp(P * log_g[h])
    for g in range(4):
        c[:, C_INV + 16 * g:C_INV + 16 * (g + 1)] = 1.0 / np.minimum(np.arange(1, 17), 2 << g)
    return c


def rotary_tables():
    inv = (1.0 / (np.float32(10000.0) ** (np.arange(0, 64, 2, dtype=np.float32) / np.float32(64)))).astype(np.float32)
    ang = (np.arange(S, dtype=np.float32)[None, :] * inv[:, None]).astype(np.float32)
    t = np.stack([np.cos(ang), np.sin(ang)], 1).astype(np.float32)
    return np.ascontiguousarray(np.tile(t, (H, 1, 1)))


def plan():
    at, n, u = {}, 0, 0
    order = [("gains", 1, 0), ("xt", KT, 0)]
    for f in ("ffn1", "ffn2"):
        stages = [(f + "_stat", 1, 0)]
        for c, (_, k) in enumerate(CHUNKS):
            stages += [(f"{f}_up{c}", 2 * k, 2 * k), (f"{f}_down{c}", KT, KT)]
        if f == "ffn1":
            order += stages
            order += [("win_stat", 1, 0), ("win", 24, 24), ("wout", KT, KT), ("wq_stat", 1, 0), ("wq", KT, KT),
                      ("memt", 2, 0), ("wkv", 2 * KT, 2 * KT), ("vt", MT, 0), ("wo", KT, KT)]
        else:
            order += stages
    order += [("pool_stat", 2, 0), ("pool_u", KT, KT), ("pool_g", 2 * KT, 2 * KT), ("fgain", 1, 0), ("pool_out", KT, KT),
              ("final", TT, 0)]
    for name, dn, du in order:
        at[name] = (n, u)
        n += dn
        u += du
    at["end"] = (n, u)
    return at


def build(nc, a, consts, rot, spill, out):
    at = plan()
    N = {k: v[0] for k, v in at.items()}
    U = {k: v[1] for k, v in at.items()}
    UNITS = U["end"]
    R_XT, R_FFN1, R_WOUT, R_WO, R_FFN2 = 0, 8, 16, 24, 32

    with ExitStack() as ctx:
        sem = lambda name: ctx.enter_context(nc.semaphore(name))
        base = [(nc.sbuf_base + 63) // 64 * 64]

        def here(name, shape, dt=F32):
            t = nc.alloc_sbuf_tensor_at(name, shape, dt, offset=base[0])
            base[0] += (int(np.prod(shape[1:])) * 4 + 31) // 32 * 32
            return t

        def over(name, shape, dt, offset):
            return nc.alloc_sbuf_tensor_at(name, shape, dt, offset=offset)

        K1 = 1024
        a_xt = base[0]
        xt = here("xt", [P, KT, S])
        a_r0 = base[0]
        r0h, r0l = here("r0h", [P, KT, S], F32R), here("r0l", [P, KT, S], F32R)
        a_r1 = base[0]
        r1h, r1l = here("r1h", [P, KT, S], F32R), here("r1l", [P, KT, S], F32R)
        raw = here("raw", [P, 2, KT, P])
        w_hi, w_lo = here("w_hi", [P, 2, KT, P], F32R), here("w_lo", [P, 2, KT, P], F32R)
        PAD = 16
        t1, t2, t3 = (here(f"t{i}", [P, PAD + S]) for i in (1, 2, 3))
        T1, T2, T3 = (t[:, PAD:PAD + S] for t in (t1, t2, t3))
        a_acc = base[0]
        acc, rstd, acc2, rfin = here("acc", [P, S]), here("rstd", [P, S]), here("acc2", [P, S]), here("rfin", [P, S])
        cst = here("cst", [P, C_COLS])
        gain = here("gain", [P, G_ROWS])
        ygain, gain2 = here("ygain", [P, 8]), here("gain2", [P, KT])
        ident_r, mask_r = here("ident_r", [P, P], F32R), here("mask_r", [P, P], F32R)
        lamv = here("lamv", [P, 2])
        small = here("small", [P, 64])
        assert base[0] <= nc.sbuf_usable_end, (base[0], nc.sbuf_usable_end)
        ident, ones = cst[:, C_ID:C_ID + P], cst[:, C_ONES:C_ONES + P]

        xin = over("xin", [P, TT, D], F32, a_r1)
        grow = over("grow", [P, P], F32, a_r1 + 32 * K1)
        lrow = over("lrow", [P, 4, 64], F32, a_r1 + 33 * K1)
        pa = over("pa", [P, 16, S], F32, a_r1)
        pb = over("pb", [P, 8, S], F32, a_xt)
        pa_f, pb_f = pa[:].rearrange("p t n -> p (t n)"), pb[:].rearrange("p t n -> p (t n)")
        y = over("y", [P, 8, S], F32, a_r0)
        y_f = y[:].rearrange("p t n -> p (t n)")
        w0 = a_r0 + 32 * K1
        rott = over("rott", [P, 2, S], F32, a_acc)
        qk = over("qk", [P, 4, P], F32, w0 + 8 * K1)
        qkh, qkl = over("qkh", [P, 4, P], F32R, w0 + 10 * K1), over("qkl", [P, 4, P], F32R, w0 + 12 * K1)
        vc = over("vc", [P, 4, P], F32, w0 + 14 * K1)
        rvh, rvl = over("rvh", [P, 4, P], F32R, w0 + 16 * K1), over("rvl", [P, 4, P], F32R, w0 + 18 * K1)
        kz = over("kz", [P, 2, P], F32, w0 + 20 * K1)
        kzh, kzl = over("kzh", [P, 2, P], F32R, w0 + 21 * K1), over("kzl", [P, 2, P], F32R, w0 + 22 * K1)
        inh, inl = over("inh", [P, 4, P], F32R, w0 + 23 * K1), over("inl", [P, 4, P], F32R, w0 + 25 * K1)
        rs = over("rs", [P, 2, P], F32, w0 + 27 * K1)
        rsh, rsl = over("rsh", [P, 2, P], F32R, w0 + 28 * K1), over("rsl", [P, 2, P], F32R, w0 + 29 * K1)
        rtmp_a = over("rtmp_a", [P, 2, 2, P], F32, w0 + 30 * K1)
        rtmp = [rtmp_a[:, 0], rtmp_a[:, 1]] + [T3[:, c:c + 2 * P].rearrange("p (c n) -> p c n", c=2) for c in (4 * P, 6 * P)]
        inf = T1[:, 0:512].rearrange("p (h n) -> p h n", h=4)
        rsq = T2[:, 0:512].rearrange("p (h n) -> p h n", h=4)
        on = T3[:, 0:512].rearrange("p (h n) -> p h n", h=4)
        dqh, dql, dkh, dkl = (over(nm, [P, S], F32R, w0 + 4 * K1 * i) for i, nm in enumerate(("dqh", "dql", "dkh", "dkl")))
        dvh, dvl = (over(nm, [P, TT, P], F32R, w0 + 4 * K1 * (4 + i)) for i, nm in enumerate(("dvh", "dvl")))
        pth, ptl = (over(nm, [P, 2, TT, P], F32R, a_r1 + 8 * K1 * i) for i, nm in enumerate(("pth", "ptl")))
        e = ((T1, T2), (acc[:], rstd[:]))
        memh, meml, kxh, kxl = (over(nm, [P, KT, M], F32R, a_r0 + 8 * K1 * i) for i, nm in enumerate(("memh", "meml", "kxh", "kxl")))
        vxh, vxl = (over(nm, [P, MT, D], F32R, w0 + 8 * K1 * i) for i, nm in enumerate(("vxh", "vxl")))
        vf = over("vf", [P, KT, M], F32, a_acc + 8 * K1)
        memr = over("memr", [P, MT, D], F32, a_acc + 8 * K1)
        qsh, qsl = (over(nm, [P, 2, KT, P], F32R, w0 + 16 * K1 + 8 * K1 * i) for i, nm in enumerate(("qsh", "qsl")))
        pxh, pxl = (over(nm, [P, 2, KT, P], F32R, a_r0 + 8 * K1 * i) for i, nm in enumerate(("pxh", "pxl")))
        ex = (T1, T2)
        outrow = (T1, T2)
        fgain, frow = acc, acc2

        ps = ctx.enter_context(nc.psum_tensor("ps", [P, 4, S], F32))
        bank = lambda b: ps[:, b // 2, (b % 2) * 512:(b % 2) * 512 + 512]

        s_cst, s_vec, s_lrow, s_x, s_rot, s_mem, s_frow = map(sem, ("s_cst", "s_vec", "s_lrow", "s_x", "s_rot", "s_mem", "s_frow"))
        s_raw = [sem("s_raw0"), sem("s_raw1")]
        s_whi, s_wlo = sem("s_whi"), sem("s_wlo")
        s_mm, s_evac = sem("s_mm"), sem("s_evac")
        s_setup_act, s_setup_dve, s_lam = sem("s_setup_act"), sem("s_setup_dve"), sem("s_lam")
        s_sqrt, s_rstd, s_sq2, s_acc2 = map(sem, ("s_sqrt", "s_rstd", "s_sq2", "s_acc2"))
        s_ahi, s_alo, s_sq, s_acc = sem("s_ahi"), sem("s_alo"), sem("s_sq"), sem("s_acc")
        s_silu, s_h, s_hhi, s_hlo = sem("s_silu"), sem("s_h"), sem("s_hhi"), sem("s_hlo")
        s_spill, s_reload = sem("s_spill"), sem("s_reload")
        s_dve, s_pool = sem("s_dve"), sem("s_pool")
        s_out = [sem("s_out0"), sem("s_out1")]

        (s_sg, s_rotd, s_qkh, s_qkl, s_vtr, s_ktr, s_vh, s_vl, s_kz, s_kzh, s_kzl, s_inner, s_inf, s_inh,
         s_inl, s_kv, s_r, s_rh, s_rl, s_o, s_rsq, s_rms, s_rroot, s_on, s_ytr, s_y) = map(sem, (
             "s_sg", "s_rotd", "s_qkh", "s_qkl", "s_vtr", "s_ktr", "s_vh", "s_vl", "s_kz", "s_kzh", "s_kzl",
             "s_inner", "s_inf", "s_inh", "s_inl", "s_kv", "s_r", "s_rh", "s_rl", "s_o", "s_rsq", "s_rms",
             "s_rroot", "s_on", "s_ytr", "s_y"))
        (s_dqh, s_dql, s_vt, s_dvtr, s_dvh, s_dvl, s_s, s_nm, s_exp, s_a, s_t, s_pth, s_ptl, s_pv, s_dsq,
         s_dms, s_droot, s_don, s_dytr, s_dy) = map(sem, (
             "s_dqh", "s_dql", "s_vt", "s_dvtr", "s_dvh", "s_dvl", "s_s", "s_nm", "s_exp", "s_a", "s_t",
             "s_pth", "s_ptl", "s_pv", "s_dsq", "s_dms", "s_droot", "s_don", "s_dytr", "s_dy"))
        s_rtile, s_itile, s_ms2, s_ra, s_mx, s_da, s_dn, s_xa = map(sem, ("s_rtile", "s_itile", "s_ms2", "s_ra", "s_mx", "s_da", "s_dn", "s_xa"))
        s_yhi, s_ylo = sem("s_yhi"), sem("s_ylo")
        (s_msq, s_mms, s_mroot, s_mn, s_mhi, s_mlo, s_khi, s_klo, s_vf, s_vxh, s_vxl, s_qh, s_ql, s_xs, s_xnm,
         s_xe, s_xn, s_xt, s_xph, s_xpl, s_xpv, s_xy, s_xyl, s_qc) = map(sem, (
             "s_msq", "s_mms", "s_mroot", "s_mn", "s_mhi", "s_mlo", "s_khi", "s_klo", "s_vf", "s_vxh", "s_vxl",
             "s_qh", "s_ql", "s_xs", "s_xnm", "s_xe", "s_xn", "s_xt", "s_xph", "s_xpl", "s_xpv", "s_xy", "s_xyl", "s_qc"))
        s_pd, s_phi, s_plo, s_psilu, s_pq, s_yy, s_fsq, s_fms, s_froot, s_fo = map(sem, (
            "s_pd", "s_phi", "s_plo", "s_psilu", "s_pq", "s_yy", "s_fsq", "s_fms", "s_froot", "s_fo"))

        def weights(name):
            return a[name].rearrange("l (k p) n -> p (l k) n", p=P)

        def landed(u):
            rotary = max(0, min(2, (u - U["win"]) // 2 + 1))
            return 16 * (u // 2 + 1 + (H - 1) * rotary)

        block = ctx.enter_context(nc.Block())

        @block.sync
        def _(sp):
            sp.dma_start(cst[:], consts).then_inc(s_cst, 16)
            xv = a["x"].rearrange("b (t p) d -> p (b t) d", p=P)
            for t in range(0, TT, 2):
                sp.dma_start(xin[:, t:t + 2], xv[:, t:t + 2]).then_inc(s_x, 16)
            vectors = (("ffn1_norm", G_FFN1), ("mix_norm", G_MIX), ("xattn_norm", G_X), ("mem_norm", G_MEM),
                       ("ffn2_norm", G_FFN2), ("norm_w_2", G_NORM2), ("pool_scale_2", G_PS))
            for name, row in vectors:
                sp.dma_start(grow[row:row + KT, :], a[name].rearrange("l (k p) -> (l k) p", p=P)).then_inc(s_vec, 16)
            sp.dma_start(grow[G_FIN:G_FIN + KT, :], a["final_norm"].rearrange("(k p) -> k p", p=P)).then_inc(s_vec, 16)
            sp.dma_start(grow[G_PB:G_PB + KT, :], a["pool_group_b_2"].rearrange("l g (k p) -> (l g k) p", p=P)).then_inc(s_vec, 16)
            sp.dma_start(grow[G_RET:G_RET + H, :], a["ret_out_norm"].rearrange("l h p -> (l h) p")).then_inc(s_vec, 16)
            sp.dma_start(grow[G_DIFF:G_DIFF + H, :], a["diff_out_norm"].rearrange("l h p -> (l h) p")).then_inc(s_vec, 16)
            for i, name in enumerate(("diff_lq1", "diff_lk1", "diff_lq2", "diff_lk2")):
                sp.dma_start(lrow[0:1, i, :], a[name]).then_inc(s_lrow, 16)

            def load(u, j, src, kn=KT, first=False):
                if not first:
                    sp.wait_ge(s_wlo, u - 1)
                sp.dma_start(raw[:, j, 0:kn], src).then_inc(s_raw[j], 16)

            def ffn(f, first):
                wg, wu = weights(f + "_w_gate"), weights(f + "_w_up")
                wd = weights(f + "_w_down")
                for c, (t0, k) in enumerate(CHUNKS):
                    u = U[f"{f}_up{c}"]
                    peel = 1 if first and c == 0 else 0
                    for j in range(4 * peel):
                        w = (wg, wu)[j % 2]
                        load(u + j, j % 2, w[:, :, (j // 2) * P:(j // 2 + 1) * P], first=(j < 2))
                    with sp.Fori(peel, k // 2) as i:
                        for j in range(4):
                            w = (wg, wu)[j % 2]
                            load(u + 4 * i + j, j % 2, w[:, :, bass.ds(i * (2 * P) + (t0 + j // 2) * P, P)])
                    u = U[f"{f}_down{c}"]
                    with sp.Fori(0, 2) as i:
                        for j in range(4):
                            load(u + 4 * i + j, j % 2, wd[:, t0:t0 + k, bass.ds(i * (4 * P) + j * P, P)], k)

            def project(u, w, count, col0=0):
                with sp.Fori(0, count // 4) as i:
                    for j in range(4):
                        load(u + 4 * i + j, j % 2, w[:, :, bass.ds(i * (4 * P) + (col0 + j * P), P)])

            ffn("ffn1", True)
            win = weights("w_in")
            for j in range(4):
                sp.wait_ge(s_wlo, U["win"] + j - 1)
                for h in range(H):
                    col = (j // 2) * 256 + 64 * h + 32 * (j % 2)
                    sp.dma_start(raw[:, j % 2, :, 32 * h:32 * h + 32], win[:, :, col:col + 32]).then_inc(s_raw[j % 2], 16)
            sp.wait_ge(s_acc, R_FFN1 + KT)
            sp.dma_start(spill, xt[:]).then_inc(s_spill, 16)
            project(U["win"] + 4, win, 20, 4 * P)

            def project_units(name, w, js):
                for j in js:
                    load(U[name] + j, j % 2, w[:, :, j * P:(j + 1) * P])

            project_units("wout", weights("w_out"), (0, 1))
            sp.wait_ge(s_evac, N["win"] + 24)
            sp.dma_start(rott[:], rot).then_inc(s_rot, 16)
            sp.wait_ge(s_dy, H)
            sp.dma_start(xt[:], spill).then_inc(s_reload, 16)
            sp.dma_start(memr[:], a["mem"].rearrange("b (t p) d -> p (b t) d", p=P)).then_inc(s_mem, 16)
            project_units("wout", weights("w_out"), range(2, KT))
            project(U["wq"], weights("xattn_wq"), KT)
            project(U["wkv"], weights("xattn_wkv"), 2 * KT)
            project(U["wo"], weights("xattn_wo"), KT)
            ffn("ffn2", False)
            win2 = weights("pool_in_w_2")
            project(U["pool_u"], win2, KT)
            wg2 = a["pool_group_w_2"].rearrange("l g (k p) n -> p (l g) k n", p=P)
            for g in range(4):
                u = U["pool_g"] + 4 * g
                for j in range(2):
                    load(u + j, j, win2[:, :, (KT + 2 * g + j) * P:(KT + 2 * g + j + 1) * P])
                for j in range(2):
                    load(u + 2 + j, j, wg2[:, g, :, j * P:(j + 1) * P], 2)
                if g == 0:
                    sp.wait_ge(s_mm, N["pool_stat"] + 2)
                    sp.dma_start(frow[0:1, :], a["final_norm_w_2"].rearrange("(o d) -> o d", o=1)).then_inc(s_frow, 16)
            project(U["pool_out"], weights("pool_out_w_2"), KT)
            for t in range(TT):
                sp.wait_ge(s_evac, N["final"] + t + 1)
                sp.dma_start(out[0, t * P:(t + 1) * P, :], outrow[t % 2]).then_inc(s_out[t % 2], 16)
            for j in range(2):
                sp.wait_ge(s_out[j], 16 * TT // 2)

        @block.tensor
        def _(pe):
            def slot_free(n):
                if isinstance(n, int) and n < 4:
                    return
                pe.wait_ge(s_evac, n - 3)

            def product(out_ap, pairs, first=True, last=True):
                for i, (lhs, rhs) in enumerate(pairs):
                    mm = pe.matmul(out_ap, lhs, rhs, start=first and i == 0, stop=last and i == len(pairs) - 1,
                                   skip_group_check=True)
                return mm

            def unit(n, u, j, slot, rh, rl, kts=range(KT), cols=S, ready=None):
                slot_free(n)
                pe.wait_ge(s_wlo, u + 1)
                for i, k in enumerate(kts):
                    if ready:
                        pe.wait_ge(ready[0], ready[1] + i + 1)
                    for p, (w, x) in enumerate(((w_hi, rh), (w_hi, rl), (w_lo, rh))):
                        for c0, c1 in HALVES:
                            if c0 >= cols:
                                continue
                            c1 = min(c1, cols)
                            mm = pe.matmul(ps[:, slot, c0:c1], w[:, j, i, :], x[:, k, c0:c1],
                                           start=(i == 0 and p == 0), stop=(i == len(kts) - 1 and p == 2))
                mm.then_inc(s_mm, 1)

            def units(stage, count, rh, rl, kts=range(KT), cols=S, ready=None):
                n0, u0 = N[stage], U[stage]
                with pe.Fori(0, count // 4) as i:
                    for j in range(4):
                        unit(n0 + j + 4 * i, u0 + j + 4 * i, j % 2, (n0 + j) % 4, rh, rl, kts, cols,
                             ready if j == 0 else None)

            def stat(stage, tiles):
                for i, (src, s_done, count) in enumerate(tiles):
                    n = N[stage] + i
                    slot_free(n)
                    pe.wait_ge(s_done, count)
                    for c0, c1 in HALVES:
                        mm = pe.matmul(ps[:, n % 4, c0:c1], ones, src[:, c0:c1], start=True, stop=True)
                    mm.then_inc(s_mm, 1)

            def ffn(f, rh, rl, hh, hl, r, pairs0):
                stat(f + "_stat", [(acc, s_acc, r + KT)])
                pairs = pairs0
                for c, (t0, k) in enumerate(CHUNKS):
                    units(f"{f}_up{c}", 2 * k, rh, rl, ready=(s_alo, r) if c == 0 else None)
                    units(f"{f}_down{c}", KT, hh, hl, kts=range(k), ready=(s_hlo, pairs))
                    pairs += k

            pe.wait_ge(s_cst, 16)
            pe.wait_ge(s_vec, 11 * 16)
            pe.transpose(ps[:, 0, 0:G_ROWS], grow[0:G_ROWS, :], cst[0:G_ROWS, C_ID:C_ID + G_ROWS])
            pe.wait_ge(s_lam, 1)
            pe.matmul(ps[:, 0, 512:514], cst[0:1, C_ONES:C_ONES + P], small[0:1, 4:6], start=True, stop=True).then_inc(s_mm, 1)
            for m in range(KT):
                n = N["xt"] + m
                slot_free(n)
                for t in range(TT):
                    if m == 0 and t == 0:
                        pe.wait_ge(s_x, 16 * TT // 2)
                    mm = pe.transpose(ps[:, n % 4, t * P:(t + 1) * P], xin[:, t, m * P:(m + 1) * P], ident)
                mm.then_inc(s_mm, 1)
            ffn("ffn1", r0h, r0l, r1h, r1l, R_XT, 0)
            stat("win_stat", [(acc, s_acc, R_FFN1 + KT)])
            units("win", 24, r0h, r0l, ready=(s_alo, R_FFN1))

            pe.wait_ge(s_evac, N["win"] + 24)

            def retention_scores(i, first):
                pe.wait_ge(s_rotd, i + 1)
                if not first:
                    pe.wait_ge(s_vl, i)
                for h in range(H):
                    mm = pe.transpose(bank(4)[:, h * P:(h + 1) * P], vc[:, h], ident)
                mm.then_inc(s_vtr, 1)
                for c in range(2):
                    mm = pe.transpose(bank(5)[:, c * P:(c + 1) * P], qk[:, 2 + c], ident)
                mm.then_inc(s_ktr, 1)
                pe.wait_ge(s_qkl, i + 1)
                if not first:
                    pe.wait_ge(s_inf, i)
                for h in range(H):
                    rows = slice(32 * h, 32 * h + 32)
                    if h >= 2:
                        pe.wait_ge(s_itile, 2 * i + h - 1)
                    pairs = [(kk[rows, 2 + c], qq[rows, c]) for c in range(2) for kk, qq in ((qkh, qkh), (qkh, qkl), (qkl, qkh))]
                    mm = product(bank(h % 2)[:, h // 2 * P:(h // 2 + 1) * P], pairs)
                    if h < 2:
                        mm.then_inc(s_itile, 1)
                mm.then_inc(s_inner, 1)

            def retention_output(i, first):
                pe.wait_ge(s_kzl, i + 1)
                pe.wait_ge(s_vl, i + 1)
                if not first:
                    pe.wait_ge(s_r, i)
                vh, vl = rvh[:].rearrange("p h n -> p (h n)"), rvl[:].rearrange("p h n -> p (h n)")
                for c in range(2):
                    mm = product(bank(2 + c), [(kzh[:, c], vh), (kzh[:, c], vl), (kzl[:, c], vh)])
                mm.then_inc(s_kv, 1)
                pe.wait_ge(s_inl, i + 1)
                if not first:
                    pe.wait_ge(s_rl, i)
                    pe.wait_ge(s_on, i)
                for h in range(H):
                    rows = slice(32 * h, 32 * h + 32)
                    o = bank(6)[:, h * P:(h + 1) * P]
                    mm = product(o, [(inh[:, h], rvh[:, h]), (inh[:, h], rvl[:, h]), (inl[:, h], rvh[:, h])], last=first)
                    if not first:
                        if h > 0:
                            pe.wait_ge(s_rtile, 3 * (i - 1) + h)
                        mm = product(o, [(qq[rows, c], rr[rows, c]) for c in range(2)
                                         for qq, rr in ((qkh, rsh), (qkh, rsl), (qkl, rsh))], first=False)
                        if h < H - 1:
                            mm.then_inc(s_rtile, 1)
                mm.then_inc(s_o, 1)

            def retention_turn(i, first):
                pe.wait_ge(s_on, i + 1)
                if not first:
                    pe.wait_ge(s_y, i)
                for h in range(H):
                    mm = pe.transpose(bank(7)[:, h * P:(h + 1) * P], on[:, h], ident)
                mm.then_inc(s_ytr, 1)

            retention_scores(0, True)
            retention_output(0, True)
            retention_scores(1, False)
            retention_turn(0, True)
            with pe.Fori(1, TT - 1) as i:
                retention_output(i, False)
                retention_scores(i + 1, False)
                retention_turn(i, False)
            retention_output(TT - 1, False)
            retention_turn(TT - 1, False)

            pe.wait_ge(s_y, TT)
            pe.sem_inc(s_t, 2)

            def scores(i, t):
                g = 8 * i + t
                w = (t + 1) * P
                if t == 0:
                    pe.wait_ge(s_dql, i + 1)
                for c in range(2):
                    rows = slice(64 * c, 64 * c + 64)
                    pe.wait_ge(s_exp, 2 * g + c + 1)
                    for c0 in range(0, w, 512):
                        c1 = min(c0 + 512, w)
                        product(ps[:, c, c0:c1], [(qq[rows, t * P:w], kk[rows, c0:c1])
                                                  for qq, kk in ((dqh, dkh), (dqh, dkl), (dql, dkh))], last=False)
                    mm = pe.matmul(ps[:, c, t * P:w], ident_r[:], mask_r[:], start=False, stop=True, skip_group_check=True)
                    mm.then_inc(s_s, 1)

            def turn_output(i):
                pe.wait_ge(s_don, i + 1)
                for t in range(TT):
                    mm = pe.transpose(ps[:, 3, t * P:(t + 1) * P], rfin[:, t * P:(t + 1) * P], ident)
                mm.then_inc(s_dytr, 1)

            def weighted_values(g, t):
                pe.wait_ge(s_ptl, g + 1)
                for b in range(t + 1):
                    mm = product(ps[:, 3, t * P:(t + 1) * P], [(pp[:, t % 2, b], vv[:, b]) for pp, vv in (
                        (pth, dvh), (pth, dvl), (ptl, dvh))], first=(b == 0), last=(b == t))
                mm.then_inc(s_pv, 1)

            def head(i, first):
                scores(i, 0)
                pe.wait_ge(s_vt, i + 1)
                if not first:
                    pe.wait_ge(s_ptl, 8 * i)
                for t in range(TT):
                    mm = pe.transpose(ps[:, 2, t * P:(t + 1) * P], T3[:, t * P:(t + 1) * P], ident)
                mm.then_inc(s_dvtr, 1)
                for t in range(TT):
                    g = 8 * i + t
                    if t + 1 < TT:
                        scores(i, t + 1)
                    pe.wait_ge(s_a, g + 1)
                    if t == 0:
                        pe.wait_ge(s_dvl, i + 1)
                    else:
                        pe.wait_ge(s_ptl, g)
                    for b in range(t + 1):
                        mm = pe.transpose(ps[:, 2, b * P:(b + 1) * P], e[t % 2][1][:, b * P:(b + 1) * P], ident)
                    mm.then_inc(s_t, 1)
                    if t == 0 and not first:
                        turn_output(i - 1)
                    if t == 1 and not first:
                        pe.wait_ge(s_dy, i)
                    if t >= 1:
                        weighted_values(g - 1, t - 1)
                weighted_values(8 * i + TT - 1, TT - 1)

            head(0, True)
            with pe.Fori(1, H) as i:
                head(i, False)
            turn_output(H - 1)

            pe.wait_ge(s_dy, H)
            units("wout", KT, r1h, r1l, ready=(s_ylo, 0))
            stat("wq_stat", [(acc, s_acc, R_WOUT + KT)])
            units("wq", KT, r0h, r0l, ready=(s_alo, R_WOUT))

            pe.wait_ge(s_mn, 1)
            for q in range(2):
                n = N["memt"] + q
                slot_free(n)
                for k in range(4):
                    for t in range(MT):
                        c = k * M + t * P
                        mm = pe.transpose(ps[:, n % 4, c:c + P], memr[:, t, (4 * q + k) * P:(4 * q + k + 1) * P], ident)
                mm.then_inc(s_mm, 1)
            pe.wait_ge(s_evac, N["memt"] + 2)
            units("wkv", 2 * KT, memh, meml, cols=M)
            for t in range(MT):
                n = N["vt"] + t
                slot_free(n)
                pe.wait_ge(s_evac, N["wkv"] + 2 * KT)
                for k in range(KT):
                    mm = pe.transpose(ps[:, n % 4, k * P:(k + 1) * P], vf[:, k, t * P:(t + 1) * P], ident)
                mm.then_inc(s_mm, 1)

            def xscores(i, par, first):
                pe.wait_ge(s_qc, i + 1)
                if not first:
                    pe.wait_ge(s_xe, i - 1)
                for h in range(H):
                    mm = product(ps[:, 3 * par, h * M:(h + 1) * M], [(qq[:, par, 2 * h + c], kk[:, 2 * h + c]) for c in range(2)
                                                                     for qq, kk in ((qsh, kxh), (qsh, kxl), (qsl, kxh))])
                mm.then_inc(s_xs, 1)

            def xturn(i, par, first):
                pe.wait_ge(s_xn, i + 1)
                if not first:
                    pe.wait_ge(s_xpl, i)
                for b in range(KT):
                    mm = pe.transpose(ps[:, 1, b * P:(b + 1) * P], ex[par][:, b * P:(b + 1) * P], ident)
                mm.then_inc(s_xt, 1)

            def xvalues(i, par, first):
                pe.wait_ge(s_xpl, i + 1)
                if not first:
                    pe.wait_ge(s_xyl, i)
                for f in range(KT):
                    h = f // 2
                    mm = product(ps[:, 2, f * P:(f + 1) * P], [(vv[:, t, f * P:(f + 1) * P], pp[:, par, h * MT + t])
                                                               for t in range(MT) for vv, pp in ((vxh, pxh), (vxl, pxh), (vxh, pxl))])
                mm.then_inc(s_xpv, 1)

            pe.wait_ge(s_evac, N["vt"] + MT)
            xscores(0, 0, True)
            xscores(1, 1, True)
            xturn(0, 0, True)
            xscores(2, 0, False)
            xturn(1, 1, False)
            xvalues(0, 0, True)
            xscores(3, 1, False)
            with pe.Fori(1, TT // 2 - 1) as i:
                for par in range(2):
                    xturn(2 * i + par, par, False)
                    xvalues(2 * i + (par - 1), 1 - par, False)
                    xscores(2 * i + (par + 2), par, False)
            for i in (TT - 2, TT - 1):
                xturn(i, i % 2, False)
                xvalues(i - 1, (i - 1) % 2, False)
            xvalues(TT - 1, 1, False)

            pe.wait_ge(s_xyl, TT)
            units("wo", KT, r1h, r1l)
            ffn("ffn2", r0h, r0l, r1h, r1l, R_WO, FT)
            stat("pool_stat", [(acc, s_acc, R_FFN2 + KT), (acc2, s_acc2, KT)])
            units("pool_u", KT, r0h, r0l, ready=(s_alo, R_FFN2))
            for g in range(4):
                n, u = N["pool_g"] + 4 * g, U["pool_g"] + 4 * g
                for j in range(2):
                    unit(n + j, u + j, j, (n + j) % 4, r0h, r0l)
                for j in range(2, 4):
                    unit(n + j, u + j, j % 2, (n + j) % 4, r1h, r1l, kts=range(2 * g, 2 * g + 2), ready=(s_plo, 2 * g))
            n = N["fgain"]
            slot_free(n)
            pe.wait_ge(s_frow, 16)
            for c0, c1 in HALVES:
                mm = pe.matmul(ps[:, n % 4, c0:c1], cst[0:1, C_ONES:C_ONES + P], frow[0:1, c0:c1], start=True, stop=True)
            mm.then_inc(s_mm, 1)
            units("pool_out", KT, r1h, r1l, ready=(s_plo, KT))
            for t in range(TT):
                n = N["final"] + t
                slot_free(n)
                for m in range(KT):
                    pe.wait_ge(s_evac, N["pool_out"] + m + 1)
                    mm = pe.transpose(ps[:, n % 4, m * P:(m + 1) * P], xt[:, m, t * P:(t + 1) * P], ident)
                mm.then_inc(s_mm, 1)

        @block.scalar
        def _(act):
            def step(n, u, j):
                act.wait_ge(s_mm, n + 1)
                if u + 2 < UNITS:
                    act.wait_ge(s_raw[j], landed(u + 2))
                    act.activation(w_hi[:, j], raw[:, j], ACT.Copy).then_inc(s_whi, 1)

            def loop_step(n0, u0, i, j):
                act.wait_ge(s_mm, 4 * i + (n0 + j + 1))
                act.wait_ge(s_raw[j % 2], 32 * i + landed(u0 + j + 2))
                act.activation(w_hi[:, j % 2], raw[:, j % 2], ACT.Copy).then_inc(s_whi, 1)

            def split_residual(n, r, m, xh, g, g_sq2=None):
                act.wait_ge(s_evac, n + 1)
                act.activation(xh[:, m], xt[:, m], ACT.Copy, scale=g[:, m:m + 1]).then_inc(s_ahi, 1)
                if r + m > 0:
                    act.wait_ge(s_acc, r + m)
                act.activation(T2, xt[:, m], ACT.Square).then_inc(s_sq, 1)
                if g_sq2 is not None:
                    if m > 0:
                        act.wait_ge(s_acc2, m)
                    act.activation(T3, xt[:, m], ACT.Square, scale=g_sq2[:, m:m + 1]).then_inc(s_sq2, 1)

            roots = [0]

            def root(n):
                act.wait_ge(s_evac, n + 1)
                act.activation(T2, T1, ACT.Sqrt).then_inc(s_sqrt, 1)
                roots[0] += 1

            def ffn(f, hh, pairs0, residual):
                pairs = pairs0
                hh_f = hh[:].rearrange("p t n -> p (t n)")
                root(N[f + "_stat"])
                for c, (t0, k) in enumerate(CHUNKS):
                    n0, u0 = N[f"{f}_up{c}"], U[f"{f}_up{c}"]
                    with act.Fori(0, k // 2) as i:
                        for q in range(2):
                            loop_step(n0, u0, i, 2 * q)
                            act.wait_ge(s_evac, 4 * i + (n0 + 2 * q + 1))
                            act.activation(T2, T1, ACT.Silu).then_inc(s_silu, 1)
                            loop_step(n0, u0, i, 2 * q + 1)
                            act.wait_ge(s_h, 2 * i + (pairs + q + 1))
                            act.wait_ge(s_rstd, 1)
                            act.activation(hh_f[:, bass.ds(i * (2 * S) + q * S, S)], T1, ACT.Copy).then_inc(s_hhi, 1)
                    pairs += k
                    n0, u0 = N[f"{f}_down{c}"], U[f"{f}_down{c}"]
                    if c < len(CHUNKS) - 1:
                        with act.Fori(0, 2) as i:
                            for j in range(4):
                                loop_step(n0, u0, i, j)
                    else:
                        for m in range(KT):
                            step(n0 + m, u0 + m, m % 2)
                            residual(n0 + m, m)

            act.wait_ge(s_cst, 16)
            act.activation(ident_r[:], ident, ACT.Copy)
            act.activation(mask_r[:], cst[:, C_MASK:C_MASK + P], ACT.Copy).then_inc(s_setup_act, 1)
            act.wait_ge(s_dve, 2)
            act.activation(small[0:1, 2:4], small[0:1, 0:2], ACT.Exp).then_inc(s_setup_act, 1)
            for m in range(KT):
                split_residual(N["xt"] + m, R_XT, m, r0h, gain[:, G_FFN1:G_FFN1 + KT])
            for u in range(2):
                act.wait_ge(s_raw[u], 16)
                act.activation(w_hi[:, u], raw[:, u], ACT.Copy).then_inc(s_whi, 1)
            ffn("ffn1", r1h, 0, lambda n, m: split_residual(n, R_FFN1, m, r0h, gain[:, G_MIX:G_MIX + KT]))
            root(N["win_stat"])
            for j in range(4):
                step(N["win"] + j, U["win"] + j, j % 2)
            with act.Fori(0, 5) as i:
                for j in range(4):
                    loop_step(N["win"] + 4, U["win"] + 4, i, j)

            act.wait_ge(s_evac, N["win"] + 24)
            act.activation(pa[:, 8:12], pa[:, 8:12], ACT.Silu).then_inc(s_sg, 1)

            def retention_split(i, first):
                act.wait_ge(s_rotd, i + 1)
                if not first:
                    act.wait_ge(s_o, i)
                act.activation(qkh[:], qk[:], ACT.Copy).then_inc(s_qkh, 1)
                act.wait_ge(s_vtr, i + 1)
                act.activation(rvh[:], bank(4).rearrange("p (h n) -> p h n", h=4), ACT.Copy).then_inc(s_vh, 1)
                act.wait_ge(s_kz, i + 1)
                act.activation(kzh[:], kz[:], ACT.Copy).then_inc(s_kzh, 1)

            def retention_scores(i):
                act.wait_ge(s_inf, i + 1)
                act.activation(inh[:], inf, ACT.Copy).then_inc(s_inh, 1)

            def retention_norm(i):
                act.wait_ge(s_o, i + 1)
                act.activation(rsq, bank(6).rearrange("p (h n) -> p h n", h=4), ACT.Square).then_inc(s_rsq, 1)

            def retention_root(i):
                act.wait_ge(s_rms, i + 1)
                act.activation(small[:, 8:12], small[:, 4:8], ACT.Sqrt).then_inc(s_rroot, 1)

            def retention_state(i):
                act.wait_ge(s_r, i + 1)
                act.activation(rsh[:], rs[:], ACT.Copy).then_inc(s_rh, 1)

            def retention_step(i):
                retention_norm(i)
                retention_state(i)
                retention_split(i + 1, False)
                retention_root(i)
                retention_scores(i + 1)

            retention_split(0, True)
            retention_scores(0)
            retention_step(0)
            with act.Fori(1, TT - 1) as i:
                retention_step(i)
            retention_norm(TT - 1)
            retention_root(TT - 1)

            act.wait_ge(s_y, TT)
            act.sem_inc(s_exp, 2)

            def exps(i, t):
                w = (t + 1) * P
                for c in range(2):
                    act.wait_ge(s_nm, 2 * (8 * i + t) + c + 1)
                    act.wait_ge(s_t, 8 * i + t + 1)
                    col = 2 * (t % 2) + c
                    act.activation(e[t % 2][c][:, 0:w], ps[:, c, 0:w], ACT.Exp, bias=small[:, 16 + col:17 + col],
                                   scale=DIFF_SCALE, accum_out=small[:, 20 + col:21 + col]).then_inc(s_exp, 1)

            def square_output(i):
                act.wait_ge(s_pv, 8 * i + TT)
                act.activation(acc2[:], ps[:, 3], ACT.Square).then_inc(s_dsq, 1)

            def root_output(i):
                act.wait_ge(s_dms, i + 1)
                act.activation(small[:, 32:40], small[:, 24:32], ACT.Sqrt).then_inc(s_droot, 1)

            def head(i, first):
                if first:
                    q, k = pa_f[:, 12 * S:13 * S], pb_f[:, 0:S]
                else:
                    q, k = pa_f[:, bass.ds(i * S + 12 * S, S)], pb_f[:, bass.ds(i * S, S)]
                    act.wait_ge(s_s, 16 * i)
                    act.wait_ge(s_y, TT)
                act.activation(dqh[:], q, ACT.Copy).then_inc(s_dqh, 1)
                act.activation(dkh[:], k, ACT.Copy).then_inc(s_dqh, 1)
                exps(i, 0)
                if not first:
                    square_output(i - 1)
                act.wait_ge(s_dvtr, i + 1)
                act.activation(dvh[:].rearrange("p t n -> p (t n)"), ps[:, 2], ACT.Copy).then_inc(s_dvh, 1)
                if not first:
                    root_output(i - 1)
                for t in range(TT):
                    g = 8 * i + t
                    w = (t + 1) * P
                    if t + 1 < TT:
                        exps(i, t + 1)
                    act.wait_ge(s_t, g + 3)
                    act.activation(pth[:, t % 2, 0:t + 1].rearrange("p t n -> p (t n)"), ps[:, 2, 0:w], ACT.Copy).then_inc(s_pth, 1)

            head(0, True)
            with act.Fori(1, H) as i:
                head(i, False)
            square_output(H - 1)
            root_output(H - 1)

            def split_output(count, src, xh, g=None):
                for k in range(KT):
                    scale = g[:, k:k + 1] if g is not None else 1.0
                    act.activation(xh[:, k], src[:, k], ACT.Copy, scale=scale).then_inc(s_yhi, 1)

            act.wait_ge(s_dy, H)
            split_output(0, y, r1h, ygain)
            act.wait_ge(s_mem, 16)
            for t in range(MT):
                act.activation((T3, T2)[t], memr[:, t], ACT.Square, accum_out=small[:, t:t + 1]).then_inc(s_msq, 1)
            act.wait_ge(s_mms, 1)
            act.activation(small[:, 4:6], small[:, 2:4], ACT.Sqrt).then_inc(s_mroot, 1)
            for m in range(KT):
                step(N["wout"] + m, U["wout"] + m, m % 2)
                split_residual(N["wout"] + m, R_WOUT, m, r0h, gain[:, G_X:G_X + KT])
            root(N["wq_stat"])
            r1h_f = r1h[:].rearrange("p t n -> p (t n)")
            with act.Fori(0, 2) as i:
                for j in range(4):
                    loop_step(N["wq"], U["wq"], i, j)
                    act.wait_ge(s_evac, 4 * i + (N["wq"] + j + 1))
                    act.wait_ge(s_mroot, 1)
                    act.activation(r1h_f[:, bass.ds(i * (4 * S) + j * S, S)], T1, ACT.Copy).then_inc(s_qh, 1)

            for q in range(2):
                n = N["memt"] + q
                act.wait_ge(s_mm, n + 1)
                for k in range(4):
                    act.activation(memh[:, 4 * q + k], ps[:, n % 4, k * M:(k + 1) * M], ACT.Copy,
                                   scale=gain[:, G_MEM + 4 * q + k:G_MEM + 4 * q + k + 1]).then_inc(s_mhi, 1)
            for m in range(2 * KT):
                n = N["wkv"] + m
                step(n, U["wkv"] + m, m % 2)
                if m < KT:
                    act.activation(kxh[:, m], ps[:, n % 4, 0:M], ACT.Copy).then_inc(s_khi, 1)
            for t in range(MT):
                n = N["vt"] + t
                act.wait_ge(s_mm, n + 1)
                act.activation(vxh[:, t], ps[:, n % 4], ACT.Copy).then_inc(s_vxh, 1)

            def xexp(i, par, first):
                act.wait_ge(s_xnm, i + 1)
                if not first:
                    act.wait_ge(s_xt, i - 1)
                for h in range(H):
                    ins = act.activation(ex[par][:, h * M:(h + 1) * M], ps[:, 3 * par, h * M:(h + 1) * M], ACT.Exp, scale=XATTN_SCALE,
                                         bias=small[:, 16 + h:17 + h], accum_out=small[:, 20 + h:21 + h])
                ins.then_inc(s_xe, 1)

            def xweights(i, par, first):
                act.wait_ge(s_xt, i + 1)
                if not first:
                    act.wait_ge(s_xpv, i - 1)
                act.activation(pxh[:, par].rearrange("p k n -> p (k n)"), ps[:, 1], ACT.Copy).then_inc(s_xph, 1)

            def xout(i, at):
                act.wait_ge(s_xpv, i + 1)
                act.activation(r1h[:, :, at], ps[:, 2].rearrange("p (k n) -> p k n", k=KT), ACT.Copy).then_inc(s_xy, 1)

            act.wait_ge(s_evac, N["vt"] + MT)
            xexp(0, 0, True)
            xweights(0, 0, True)
            xexp(1, 1, True)
            xweights(1, 1, True)
            xexp(2, 0, False)
            xout(0, slice(0, P))
            with act.Fori(1, TT // 2 - 1) as i:
                for par in range(2):
                    xweights(2 * i + par, par, False)
                    xexp(2 * i + (par + 1), 1 - par, False)
                    xout(2 * i + (par - 1), bass.ds(i * (2 * P) + (par - 1) * P, P))
            xweights(TT - 2, 0, False)
            xexp(TT - 1, 1, False)
            xout(TT - 3, slice((TT - 3) * P, (TT - 2) * P))
            xweights(TT - 1, 1, False)
            xout(TT - 2, slice((TT - 2) * P, (TT - 1) * P))
            xout(TT - 1, slice((TT - 1) * P, TT * P))
            for m in range(KT):
                step(N["wo"] + m, U["wo"] + m, m % 2)
                split_residual(N["wo"] + m, R_WO, m, r0h, gain[:, G_FFN2:G_FFN2 + KT])
            ffn("ffn2", r1h, FT, lambda n, m: split_residual(n, R_FFN2, m, r0h, gain2, gain[:, G_FIN:G_FIN + KT]))

            root(N["pool_stat"])
            act.wait_ge(s_ms2, 1)
            act.activation(T2, T1, ACT.Sqrt).then_inc(s_sqrt, 1)
            for t in range(KT):
                step(N["pool_u"] + t, U["pool_u"] + t, t % 2)
                act.wait_ge(s_pd, t + 1)
                act.activation(r1h[:, t], (T3, T2)[t // 2 % 2], ACT.Copy).then_inc(s_phi, 1)
            for g in range(4):
                n, u = N["pool_g"] + 4 * g, U["pool_g"] + 4 * g
                for j in range(2):
                    step(n + j, u + j, j)
                    act.wait_ge(s_evac, n + j + 1)
                    act.activation((T1, T2)[j], (T1, T2)[j], ACT.Silu).then_inc(s_psilu, 1)
                for j in range(2):
                    step(n + 2 + j, u + 2 + j, j)
                    act.wait_ge(s_yy, 2 * g + j + 1)
                    act.wait_ge(s_mm, n + 4)
                    act.activation(r1h[:, 2 * g + j], T3, ACT.Copy).then_inc(s_phi, 1)
            for m in range(KT):
                step(N["pool_out"] + m, U["pool_out"] + m, m % 2)
            for t in range(TT):
                n = N["final"] + t
                act.wait_ge(s_mm, n + 1)
                act.activation(T3, ps[:, n % 4], ACT.Square, accum_out=small[:, t:t + 1]).then_inc(s_fsq, 1)
                act.wait_ge(s_fms, t + 1)
                act.activation(small[:, 16 + t:17 + t], small[:, 8 + t:9 + t], ACT.Sqrt).then_inc(s_froot, 1)

        @block.vector
        def _(dve):
            chain = [0]

            def link(ins):
                chain[0] += 1
                ins.then_inc(s_dve, 1)
                dve.wait_ge(s_dve, chain[0])

            def step(n, u, j):
                if u + 2 < UNITS:
                    dve.wait_ge(s_whi, u + 3)
                    dve.tensor_tensor(w_lo[:, j], raw[:, j], w_hi[:, j].bitcast(F32), ALU.subtract).then_inc(s_wlo, 1)
                    dve.wait_ge(s_wlo, u + 3)
                dve.wait_ge(s_mm, n + 1)

            def loop_step(n0, u0, i, j):
                dve.wait_ge(s_whi, 4 * i + (u0 + j + 3))
                dve.tensor_tensor(w_lo[:, j % 2], raw[:, j % 2], w_hi[:, j % 2].bitcast(F32), ALU.subtract).then_inc(s_wlo, 1)
                dve.wait_ge(s_wlo, 4 * i + (u0 + j + 3))
                dve.wait_ge(s_mm, 4 * i + (n0 + j + 1))

            def split_residual(r, m, xh, xl, g, two=False):
                dve.wait_ge(s_ahi, r + m + 1)
                dve.scalar_tensor_tensor(out=xl[:, m], in0=xt[:, m], scalar=g[:, m:m + 1], in1=xh[:, m].bitcast(F32),
                                         op0=ALU.mult, op1=ALU.subtract).then_inc(s_alo, 1)
                for total, part, done, own, r0 in ((acc, T2, s_sq, s_acc, r),) + (((acc2, T3, s_sq2, s_acc2, 0),) if two else ()):
                    dve.wait_ge(done, r0 + m + 1)
                    if m == 0:
                        dve.tensor_copy(total[:], part).then_inc(own, 1)
                    else:
                        dve.wait_ge(own, r0 + m)
                        dve.tensor_tensor(total[:], total[:], part, ALU.add).then_inc(own, 1)

            roots = [0]

            def factors(n, dst):
                dve.wait_ge(s_mm, n + 1)
                dve.tensor_scalar(T1, ps[:, n % 4], 1.0 / D, EPS, ALU.mult, ALU.add).then_inc(s_evac, 1)
                inverse(dst)

            def inverse(dst):
                roots[0] += 1
                dve.wait_ge(s_sqrt, roots[0])
                dve.reciprocal(dst[:], T2).then_inc(s_rstd, 1)
                dve.wait_ge(s_rstd, roots[0])

            def residual_add(n, m, scale):
                dve.wait_ge(s_evac, n)
                dve.scalar_tensor_tensor(out=xt[:, m], in0=ps[:, n % 4], scalar=scale, in1=xt[:, m],
                                         op0=ALU.mult, op1=ALU.add).then_inc(s_evac, 1)

            def ffn(f, hh, hl, pairs0, split):
                pairs = pairs0
                hh_f, hl_f = (t[:].rearrange("p t n -> p (t n)") for t in (hh, hl))
                xt_f = xt[:].rearrange("p t n -> p (t n)")
                factors(N[f + "_stat"], rstd)
                for c, (t0, k) in enumerate(CHUNKS):
                    n0, u0 = N[f"{f}_up{c}"], U[f"{f}_up{c}"]
                    with dve.Fori(0, k // 2) as i:
                        for q in range(2):
                            loop_step(n0, u0, i, 2 * q)
                            dve.tensor_tensor(T1, ps[:, (n0 + 2 * q) % 4], rstd[:], ALU.mult).then_inc(s_evac, 1)
                            loop_step(n0, u0, i, 2 * q + 1)
                            dve.tensor_tensor(T3, ps[:, (n0 + 2 * q + 1) % 4], rstd[:], ALU.mult).then_inc(s_evac, 1)
                            dve.wait_ge(s_silu, 2 * i + (pairs + q + 1))
                            dve.wait_ge(s_evac, 4 * i + (n0 + 2 * q + 2))
                            dve.tensor_tensor(T1, T2, T3, ALU.mult).then_inc(s_h, 1)
                            dve.wait_ge(s_hhi, 2 * i + (pairs + q + 1))
                            at_t = bass.ds(i * (2 * S) + q * S, S)
                            dve.tensor_tensor(hl_f[:, at_t], T1, hh_f[:, at_t].bitcast(F32), ALU.subtract).then_inc(s_hlo, 1)
                    pairs += k
                    n0, u0 = N[f"{f}_down{c}"], U[f"{f}_down{c}"]
                    if c < len(CHUNKS) - 1:
                        with dve.Fori(0, 2) as i:
                            for j in range(4):
                                loop_step(n0, u0, i, j)
                                at_m = bass.ds(i * (4 * S) + j * S, S)
                                dve.wait_ge(s_evac, 4 * i + (n0 + j))
                                dve.scalar_tensor_tensor(out=xt_f[:, at_m], in0=ps[:, (n0 + j) % 4], scalar=0.5, in1=xt_f[:, at_m],
                                                         op0=ALU.mult, op1=ALU.add).then_inc(s_evac, 1)
                    else:
                        for m in range(KT):
                            step(n0 + m, u0 + m, m % 2)
                            residual_add(n0 + m, m, 0.5)
                            split(m)

            for t in (t1, t2, t3):
                dve.memset(t[:, 0:PAD], 0.0)
            dve.memset(lamv[:, 0:1], 1.0)
            dve.wait_ge(s_lrow, 64)
            prod = T3[0:1, 0:128].rearrange("p (a n) -> p a n", a=2)
            link(dve.tensor_tensor(prod, lrow[0:1, 0::2, :], lrow[0:1, 1::2, :], ALU.mult))
            link(dve.tensor_reduce(small[0:1, 0:2], prod, AX.X, ALU.add))
            dve.wait_ge(s_setup_act, 2)
            link(dve.tensor_tensor(small[0:1, 6:7], small[0:1, 3:4], small[0:1, 2:3], ALU.subtract))
            for c in (4, 5):
                ins = dve.tensor_scalar(small[0:1, c:c + 1], small[0:1, 6:7], -LAMBDA_INIT, None, ALU.add)
                if c == 4:
                    link(ins)
            ins.then_inc(s_lam, 1)
            dve.wait_ge(s_mm, 1)
            link(dve.tensor_copy(gain[:], ps[:, 0, 0:G_ROWS]))
            link(dve.tensor_tensor(gain2[:], gain[:, G_FIN:G_FIN + KT], gain[:, G_NORM2:G_NORM2 + KT], ALU.mult))
            dve.tensor_copy(ygain[:, 0:4], gain[:, G_RET:G_RET + 4])
            dve.tensor_scalar(ygain[:, 4:8], gain[:, G_DIFF:G_DIFF + 4], 1.0 - LAMBDA_INIT, None, ALU.mult)
            dve.tensor_copy(lamv[:, 1:2], ps[:, 0, 512:513]).then_inc(s_evac, 1)
            for m in range(KT):
                n = N["xt"] + m
                dve.wait_ge(s_mm, n + 1)
                dve.tensor_copy(xt[:, m], ps[:, n % 4]).then_inc(s_evac, 1)
                split_residual(R_XT, m, r0h, r0l, gain[:, G_FFN1:G_FFN1 + KT])
            for u in range(2):
                dve.wait_ge(s_whi, u + 1)
                dve.tensor_tensor(w_lo[:, u], raw[:, u], w_hi[:, u].bitcast(F32), ALU.subtract).then_inc(s_wlo, 1)
            ffn("ffn1", r1h, r1l, 0, lambda m: split_residual(R_FFN1, m, r0h, r0l, gain[:, G_MIX:G_MIX + KT]))

            factors(N["win_stat"], rstd)
            for dst, count, first in ((pa_f, 16, 0), (pb_f, 8, 16)):
                if first == 16:
                    dve.wait_ge(s_spill, 16)
                with dve.Fori(0, count // 4) as i:
                    for j in range(4):
                        loop_step(N["win"] + first, U["win"] + first, i, j)
                        dve.tensor_tensor(dst[:, bass.ds(i * (4 * S) + j * S, S)], ps[:, (N["win"] + first + j) % 4], rstd[:],
                                          ALU.mult).then_inc(s_evac, 1)

            zeta = cst[:, C_ZETA:C_ZETA + P].unsqueeze(1).to_broadcast([P, 2, P])
            decay = cst[:, C_DECAY:C_DECAY + 4 * P].rearrange("p (h n) -> p h n", h=4)

            def retention_split(i):
                dve.wait_ge(s_qkh, i + 1)
                dve.tensor_tensor(qkl[:], qk[:], qkh[:].bitcast(F32), ALU.subtract).then_inc(s_qkl, 1)
                dve.wait_ge(s_ktr, i + 1)
                dve.tensor_tensor(kz[:], bank(5)[:, 0:2 * P].rearrange("p (c n) -> p c n", c=2), zeta, ALU.mult).then_inc(s_kz, 1)
                dve.wait_ge(s_vh, i + 1)
                dve.tensor_tensor(rvl[:], bank(4).rearrange("p (h n) -> p h n", h=4), rvh[:].bitcast(F32), ALU.subtract).then_inc(s_vl, 1)
                dve.wait_ge(s_kzh, i + 1)
                dve.tensor_tensor(kzl[:], kz[:], kzh[:].bitcast(F32), ALU.subtract).then_inc(s_kzl, 1)

            def retention_scores(i):
                dve.wait_ge(s_inner, i + 1)
                scores = ps[:, 0].rearrange("p (b h n) -> p h b n", b=2, h=4)[:, 0:2]
                dve.tensor_tensor(inf.rearrange("p (h b) n -> p h b n", b=2), scores, decay.rearrange("p (h b) n -> p h b n", b=2),
                                  ALU.mult).then_inc(s_inf, 1)
                dve.wait_ge(s_inh, i + 1)
                dve.tensor_tensor(inl[:], inf, inh[:].bitcast(F32), ALU.subtract).then_inc(s_inl, 1)

            def retention_state(i, first):
                dve.wait_ge(s_kv, i + 1)
                for c in range(2):
                    for h in range(H):
                        rows, kv = slice(32 * h, 32 * h + 32), bank(2 + c)[32 * h:32 * h + 32, h * P:(h + 1) * P]
                        if first:
                            ins = dve.tensor_copy(rs[rows, c], kv)
                        else:
                            ins = dve.scalar_tensor_tensor(out=rs[rows, c], in0=rs[rows, c], scalar=cst[rows, C_GCH:C_GCH + 1],
                                                           in1=kv, op0=ALU.mult, op1=ALU.add)
                ins.then_inc(s_r, 1)

            def split_state(i):
                dve.wait_ge(s_rh, i + 1)
                dve.tensor_tensor(rsl[:], rs[:], rsh[:].bitcast(F32), ALU.subtract).then_inc(s_rl, 1)

            def mean_squares(i):
                dve.wait_ge(s_rsq, i + 1)
                dve.tensor_reduce(small[:, 12:16], rsq, AX.X, ALU.add).then_inc(s_ra, 1)
                dve.wait_ge(s_ra, 4 * i + 1)
                dve.tensor_tensor(small[:, 56:60], small[:, 12:16], cst[:, C_XI2:C_XI2 + 4], ALU.mult).then_inc(s_ra, 1)
                dve.wait_ge(s_ra, 4 * i + 2)
                dve.tensor_scalar(small[:, 4:8], small[:, 56:60], EPS, None, ALU.add).then_inc(s_rms, 1)

            def normalize(i):
                dve.wait_ge(s_rroot, i + 1)
                dve.reciprocal(small[:, 12:16], small[:, 8:12]).then_inc(s_ra, 1)
                dve.wait_ge(s_ra, 4 * i + 3)
                dve.tensor_tensor(small[:, 60:64], small[:, 12:16], cst[:, C_XI:C_XI + 4], ALU.mult).then_inc(s_ra, 1)
                dve.wait_ge(s_ra, 4 * i + 4)
                dve.tensor_tensor(on, bank(6).rearrange("p (h n) -> p h n", h=4),
                                  small[:, 60:64].unsqueeze(2).to_broadcast([P, 4, P]), ALU.mult).then_inc(s_on, 1)

            def retention_gate(i, at):
                dve.wait_ge(s_ytr, i + 1)
                dve.tensor_tensor(y[:, 0:4, at], bank(7).rearrange("p (h n) -> p h n", h=4), pa[:, 8:12, at], ALU.mult).then_inc(s_y, 1)

            def retention_step(i, at, first):
                retention_state(i, first)
                split_state(i)
                mean_squares(i)
                retention_split(i + 1)
                normalize(i)
                retention_scores(i + 1)
                retention_gate(i, at)

            dve.wait_ge(s_sg, 1)
            retention_split(0)
            retention_scores(0)
            retention_step(0, slice(0, P), True)
            with dve.Fori(1, TT - 1) as i:
                retention_step(i, bass.ds(i * P, P), False)
            mean_squares(TT - 1)
            normalize(TT - 1)
            retention_gate(TT - 1, slice((TT - 1) * P, TT * P))

            def maxima(i, t):
                for c in range(2):
                    k = 2 * (8 * i + t) + c
                    col = 2 * (t % 2) + c
                    dve.wait_ge(s_s, k + 1)
                    dve.tensor_reduce(small[:, 52 + c:53 + c], ps[:, c, 0:(t + 1) * P], AX.X, ALU.max).then_inc(s_mx, 1)
                    dve.wait_ge(s_mx, k + 1)
                    dve.tensor_scalar(small[:, 16 + col:17 + col], small[:, 52 + c:53 + c], -DIFF_SCALE, None, ALU.mult).then_inc(s_nm, 1)

            def combine(i, t):
                g = 8 * i + t
                e0, e1 = (x[:, 0:(t + 1) * P] for x in e[t % 2])
                dve.wait_ge(s_exp, 2 * g + 4)
                dve.reciprocal(small[:, 48:50], small[:, 20 + 2 * (t % 2):22 + 2 * (t % 2)]).then_inc(s_da, 1)
                dve.wait_ge(s_da, 3 * g + 1)
                dve.tensor_tensor(small[:, 50:52], small[:, 48:50], lamv[:], ALU.mult).then_inc(s_da, 1)
                dve.wait_ge(s_da, 3 * g + 2)
                dve.tensor_scalar(e0, e0, small[:, 50:51], None, ALU.mult).then_inc(s_da, 1)
                dve.wait_ge(s_da, 3 * g + 3)
                dve.scalar_tensor_tensor(out=e1, in0=e1, scalar=small[:, 51:52], in1=e0, op0=ALU.mult, op1=ALU.add).then_inc(s_a, 1)

            def split_weights(i, t):
                dve.wait_ge(s_pth, 8 * i + t + 1)
                dve.tensor_tensor(ptl[:, t % 2, 0:t + 1].rearrange("p t n -> p (t n)"), ps[:, 2, 0:(t + 1) * P],
                                  pth[:, t % 2, 0:t + 1].rearrange("p t n -> p (t n)").bitcast(F32), ALU.subtract).then_inc(s_ptl, 1)

            def mean_square(i):
                dve.wait_ge(s_dsq, i + 1)
                dve.tensor_reduce(small[:, 40:48], acc2[:].rearrange("p (t n) -> p t n", t=TT), AX.X, ALU.add).then_inc(s_dn, 1)
                dve.wait_ge(s_dn, 2 * i + 1)
                dve.tensor_scalar(small[:, 24:32], small[:, 40:48], 1.0 / P, EPS, ALU.mult, ALU.add).then_inc(s_dms, 1)

            def normalize_output(i):
                dve.wait_ge(s_droot, i + 1)
                dve.reciprocal(small[:, 40:48], small[:, 32:40]).then_inc(s_dn, 1)
                dve.wait_ge(s_dn, 2 * i + 2)
                dve.tensor_tensor(rfin[:].rearrange("p (t n) -> p t n", t=TT), ps[:, 3].rearrange("p (t n) -> p t n", t=TT),
                                  small[:, 40:48].unsqueeze(2).to_broadcast([P, TT, P]), ALU.mult).then_inc(s_don, 1)

            def keep_output(i, at):
                dve.wait_ge(s_dytr, i + 1)
                dve.tensor_copy(y_f[:, at], ps[:, 3]).then_inc(s_dy, 1)

            def head(i, first):
                q, k, v = (bass.ds(i * S + c * S, S) if not first else slice(c * S, (c + 1) * S) for c in (12, 0, 4))
                dve.tensor_copy(T3, pb_f[:, v]).then_inc(s_vt, 1)
                dve.wait_ge(s_dqh, 2 * i + 1)
                dve.tensor_tensor(dql[:], pa_f[:, q], dqh[:].bitcast(F32), ALU.subtract)
                dve.wait_ge(s_dqh, 2 * i + 2)
                dve.tensor_tensor(dkl[:], pb_f[:, k], dkh[:].bitcast(F32), ALU.subtract).then_inc(s_dql, 1)
                maxima(i, 0)
                if not first:
                    mean_square(i - 1)
                dve.wait_ge(s_dvh, i + 1)
                dve.tensor_tensor(dvl[:].rearrange("p t n -> p (t n)"), ps[:, 2], dvh[:].rearrange("p t n -> p (t n)").bitcast(F32),
                                  ALU.subtract).then_inc(s_dvl, 1)
                for t in range(TT):
                    if t >= 1:
                        split_weights(i, t - 1)
                    combine(i, t)
                    if t + 1 < TT:
                        maxima(i, t + 1)
                    if t == 0 and not first:
                        normalize_output(i - 1)
                    if t == 1 and not first:
                        keep_output(i - 1, bass.ds(i * S + 3 * S, S))
                split_weights(i, TT - 1)

            head(0, True)
            with dve.Fori(1, H) as i:
                head(i, False)
            mean_square(H - 1)
            normalize_output(H - 1)
            keep_output(H - 1, slice(7 * S, 8 * S))

            def split_output(count, src, xh, xl, g=None):
                for k in range(KT):
                    dve.wait_ge(s_yhi, count + k + 1)
                    dve.scalar_tensor_tensor(out=xl[:, k], in0=src[:, k], scalar=1.0 if g is None else g[:, k:k + 1],
                                             in1=xh[:, k].bitcast(F32), op0=ALU.mult, op1=ALU.subtract).then_inc(s_ylo, 1)

            split_output(0, y, r1h, r1l, ygain)
            dve.wait_ge(s_msq, MT)
            dve.tensor_scalar(small[:, 2:4], small[:, 0:2], 1.0 / D, EPS, ALU.mult, ALU.add).then_inc(s_mms, 1)
            dve.wait_ge(s_mroot, 1)
            link(dve.reciprocal(small[:, 6:8], small[:, 4:6]))
            for t in range(MT):
                ins = dve.tensor_scalar(memr[:, t], memr[:, t], small[:, 6 + t:7 + t], None, ALU.mult)
            ins.then_inc(s_mn, 1)
            dve.wait_ge(s_reload, 16)
            for m in range(KT):
                step(N["wout"] + m, U["wout"] + m, m % 2)
                residual_add(N["wout"] + m, m, 1.0)
                split_residual(R_WOUT, m, r0h, r0l, gain[:, G_X:G_X + KT])
            factors(N["wq_stat"], rstd)
            r1h_f, r1l_f = (t[:].rearrange("p t n -> p (t n)") for t in (r1h, r1l))
            with dve.Fori(0, 2) as i:
                for j in range(4):
                    loop_step(N["wq"], U["wq"], i, j)
                    dve.tensor_tensor(T1, ps[:, (N["wq"] + j) % 4], rstd[:], ALU.mult).then_inc(s_evac, 1)
                    dve.wait_ge(s_qh, 4 * i + (j + 1))
                    at_q = bass.ds(i * (4 * S) + j * S, S)
                    dve.tensor_tensor(r1l_f[:, at_q], T1, r1h_f[:, at_q].bitcast(F32), ALU.subtract).then_inc(s_ql, 1)
                    dve.wait_ge(s_ql, 4 * i + (j + 1))

            for q in range(2):
                n = N["memt"] + q
                for k in range(4):
                    f = 4 * q + k
                    dve.wait_ge(s_mhi, 4 * q + 4)
                    ins = dve.scalar_tensor_tensor(out=meml[:, f], in0=ps[:, n % 4, k * M:(k + 1) * M], scalar=gain[:, G_MEM + f:G_MEM + f + 1],
                                                   in1=memh[:, f].bitcast(F32), op0=ALU.mult, op1=ALU.subtract)
                ins.then_inc(s_evac, 1)
            for m in range(2 * KT):
                n = N["wkv"] + m
                step(n, U["wkv"] + m, m % 2)
                if m < KT:
                    dve.wait_ge(s_khi, m + 1)
                    dve.tensor_tensor(kxl[:, m], ps[:, n % 4, 0:M], kxh[:, m].bitcast(F32), ALU.subtract).then_inc(s_evac, 1)
                else:
                    dve.tensor_copy(vf[:, m - KT], ps[:, n % 4, 0:M]).then_inc(s_evac, 1)
            for t in range(MT):
                dve.wait_ge(s_vxh, t + 1)
                dve.tensor_tensor(vxl[:, t], ps[:, (N["vt"] + t) % 4], vxh[:, t].bitcast(F32), ALU.subtract).then_inc(s_evac, 1)

            def xmax(i, par):
                dve.wait_ge(s_xs, i + 1)
                dve.tensor_reduce(small[:, 52:56], ps[:, 3 * par].rearrange("p (h n) -> p h n", h=H), AX.X, ALU.max).then_inc(s_xa, 1)
                dve.wait_ge(s_xa, 2 * i + 1)
                dve.tensor_scalar(small[:, 16:20], small[:, 52:56], -XATTN_SCALE, None, ALU.mult).then_inc(s_xnm, 1)

            def xnorm(i, par):
                dve.wait_ge(s_xe, i + 1)
                dve.reciprocal(small[:, 48:52], small[:, 20:24]).then_inc(s_xa, 1)
                dve.wait_ge(s_xa, 2 * i + 2)
                v = ex[par].rearrange("p (h n) -> p h n", h=H)
                dve.tensor_tensor(v, v, small[:, 48:52].unsqueeze(2).to_broadcast([P, H, M]), ALU.mult).then_inc(s_xn, 1)

            def xweights(i, par):
                dve.wait_ge(s_xph, i + 1)
                dve.tensor_tensor(pxl[:, par].rearrange("p k n -> p (k n)"), ps[:, 1],
                                  pxh[:, par].rearrange("p k n -> p (k n)").bitcast(F32), ALU.subtract).then_inc(s_xpl, 1)

            def xout(i, at):
                dve.wait_ge(s_xy, i + 1)
                dve.tensor_tensor(r1l[:, :, at], ps[:, 2].rearrange("p (k n) -> p k n", k=KT), r1h[:, :, at].bitcast(F32),
                                  ALU.subtract).then_inc(s_xyl, 1)

            xmax(0, 0)
            xnorm(0, 0)
            xmax(1, 1)
            xweights(0, 0)
            xnorm(1, 1)
            xmax(2, 0)
            xweights(1, 1)
            xnorm(2, 0)
            xout(0, slice(0, P))
            with dve.Fori(1, TT // 2 - 1) as i:
                for par in range(2):
                    xmax(2 * i + (par + 1), 1 - par)
                    xweights(2 * i + par, par)
                    xnorm(2 * i + (par + 1), 1 - par)
                    xout(2 * i + (par - 1), bass.ds(i * (2 * P) + (par - 1) * P, P))
            xmax(TT - 1, 1)
            xweights(TT - 2, 0)
            xnorm(TT - 1, 1)
            xout(TT - 3, slice((TT - 3) * P, (TT - 2) * P))
            xweights(TT - 1, 1)
            xout(TT - 2, slice((TT - 2) * P, (TT - 1) * P))
            xout(TT - 1, slice((TT - 1) * P, TT * P))
            for m in range(KT):
                step(N["wo"] + m, U["wo"] + m, m % 2)
                residual_add(N["wo"] + m, m, 1.0)
                split_residual(R_WO, m, r0h, r0l, gain[:, G_FFN2:G_FFN2 + KT])
            ffn("ffn2", r1h, r1l, FT, lambda m: split_residual(R_FFN2, m, r0h, r0l, gain2, True))

            factors(N["pool_stat"], rfin)
            n = N["pool_stat"] + 1
            dve.wait_ge(s_mm, n + 1)
            dve.tensor_tensor(T1, ps[:, n % 4], rfin[:], ALU.mult).then_inc(s_evac, 1)
            dve.wait_ge(s_evac, n + 1)
            link(dve.tensor_tensor(T3, T1, rfin[:], ALU.mult))
            dve.tensor_scalar(T1, T3, 1.0 / D, EPS, ALU.mult, ALU.add).then_inc(s_ms2, 1)
            inverse(rstd)
            link(dve.tensor_tensor(rstd[:], rstd[:], rfin[:], ALU.mult))
            for t in range(KT):
                n = N["pool_u"] + t
                g = t // 2
                window = 2 << g
                step(n, U["pool_u"] + t, t % 2)
                dve.tensor_tensor(T1, ps[:, n % 4], rstd[:], ALU.mult).then_inc(s_evac, 1)
                dve.wait_ge(s_evac, n + 1)
                src, dst, other = t1, t2, t3
                for k in range(g + 1):
                    sh = 1 << k
                    link(dve.tensor_tensor(dst[:, PAD:], src[:, PAD:], src[:, PAD - sh:PAD - sh + S], ALU.add))
                    src, dst, other = dst, (t3 if dst is t2 else t2), None
                head = slice(PAD, 2 * PAD)
                rest = slice(2 * PAD, PAD + S)
                dve.scalar_tensor_tensor(out=dst[:, rest], in0=src[:, rest], scalar=1.0 / window, in1=t1[:, rest],
                                         op0=ALU.mult, op1=ALU.subtract)
                link(dve.tensor_tensor(small[:, 0:PAD], src[:, head], cst[:, C_INV + 16 * g:C_INV + 16 * (g + 1)], ALU.mult))
                dve.tensor_tensor(dst[:, head], small[:, 0:PAD], t1[:, head], ALU.subtract).then_inc(s_pd, 1)
                dve.wait_ge(s_phi, t + 1)
                dve.tensor_tensor(r1l[:, t], dst[:, PAD:], r1h[:, t].bitcast(F32), ALU.subtract).then_inc(s_plo, 1)
            for g in range(4):
                n, u = N["pool_g"] + 4 * g, U["pool_g"] + 4 * g
                for j in range(2):
                    step(n + j, u + j, j)
                    dve.tensor_tensor((T1, T2)[j], ps[:, (n + j) % 4], rstd[:], ALU.mult).then_inc(s_evac, 1)
                for j in range(2):
                    f = 2 * g + j
                    step(n + 2 + j, u + 2 + j, j)
                    dve.tensor_scalar(T3, ps[:, (n + 2 + j) % 4], gain[:, G_PB + f:G_PB + f + 1], gain[:, G_PS + f:G_PS + f + 1],
                                      ALU.add, ALU.mult).then_inc(s_evac, 1)
                    dve.wait_ge(s_evac, n + 3 + j)
                    dve.wait_ge(s_psilu, f + 1)
                    dve.tensor_tensor(T3, T3, (T1, T2)[j], ALU.mult).then_inc(s_yy, 1)
                    dve.wait_ge(s_phi, KT + f + 1)
                    dve.tensor_tensor(r1l[:, f], T3, r1h[:, f].bitcast(F32), ALU.subtract).then_inc(s_plo, 1)
            n = N["fgain"]
            dve.wait_ge(s_mm, n + 1)
            dve.tensor_copy(fgain[:], ps[:, n % 4]).then_inc(s_evac, 1)
            for m in range(KT):
                n = N["pool_out"] + m
                x1 = (T1, T3)[m % 2]
                link(dve.scalar_tensor_tensor(out=x1, in0=xt[:, m], scalar=gain[:, G_FIN + m:G_FIN + m + 1], in1=rfin[:],
                                              op0=ALU.mult, op1=ALU.mult))
                step(n, U["pool_out"] + m, m % 2)
                dve.tensor_tensor(xt[:, m], x1, ps[:, n % 4], ALU.add).then_inc(s_evac, 1)
            for t in range(TT):
                n = N["final"] + t
                dve.wait_ge(s_fsq, t + 1)
                dve.tensor_scalar(small[:, 8 + t:9 + t], small[:, t:t + 1], 1.0 / D, EPS, ALU.mult, ALU.add).then_inc(s_fms, 1)
                dve.wait_ge(s_froot, t + 1)
                link(dve.reciprocal(small[:, 24 + t:25 + t], small[:, 16 + t:17 + t]))
                if t >= 2:
                    dve.wait_ge(s_out[t % 2], 16 * (t // 2))
                dve.scalar_tensor_tensor(out=outrow[t % 2], in0=ps[:, n % 4], scalar=small[:, 24 + t:25 + t], in1=fgain[:],
                                         op0=ALU.mult, op1=ALU.mult).then_inc(s_evac, 1)

        @block.gpsimd
        def _(pool):
            cos, sin = (lambda i, k=k: rott[:, k:k + 1, bass.ds(i * P, P)].to_broadcast([P, 2, P]) for k in range(2))

            def retention_chunk(i, first):
                at_i = bass.ds(i * P, P)
                left, right = pa[:, 0:4:2, at_i], pa[:, 1:4:2, at_i]
                if not first:
                    pool.wait_ge(s_qkl, i)
                    pool.wait_ge(s_ktr, i)
                for k, (half, table) in enumerate(((left, cos), (right, sin), (left, sin), (right, cos))):
                    pool.tensor_tensor(rtmp[k], half, table(i), ALU.mult).then_inc(s_pool, 1)
                pool.wait_ge(s_pool, 4 * i + 4)
                pool.tensor_tensor(qk[:, 0:4:2], rtmp[0], rtmp[1], ALU.subtract)
                pool.tensor_tensor(qk[:, 1:4:2], rtmp[2], rtmp[3], ALU.add)
                pool.tensor_copy(vc[:], pa[:, 4:8, at_i]).then_inc(s_rotd, 1)

            pool.wait_ge(s_rot, 16)
            retention_chunk(0, True)
            with pool.Fori(1, TT) as i:
                retention_chunk(i, False)

            def query_tile(i, par, at, first):
                if not first:
                    pool.wait_ge(s_xs, i - 1)
                pool.tensor_copy(qsh[:, par], r1h[:, :, at])
                pool.tensor_copy(qsl[:, par], r1l[:, :, at]).then_inc(s_qc, 1)

            pool.wait_ge(s_ql, KT)
            pool.wait_ge(s_mm, N["wq"] + KT)
            query_tile(0, 0, slice(0, P), True)
            query_tile(1, 1, slice(P, 2 * P), True)
            with pool.Fori(1, TT // 2) as i:
                for par in range(2):
                    query_tile(2 * i + par, par, bass.ds(i * (2 * P) + par * P, P), False)


_INS = ["x", "mem", "ffn1_norm", "ffn1_w_gate", "ffn1_w_up", "ffn1_w_down", "mix_norm", "w_in", "ret_out_norm",
        "diff_lq1", "diff_lk1", "diff_lq2", "diff_lk2", "diff_out_norm", "w_out", "xattn_norm", "mem_norm",
        "xattn_wq", "xattn_wkv", "xattn_wo", "ffn2_norm", "ffn2_w_gate", "ffn2_w_up", "ffn2_w_down", "final_norm",
        "norm_w_2", "pool_in_w_2", "pool_group_w_2", "pool_group_b_2", "pool_scale_2", "pool_out_w_2", "final_norm_w_2"]


def kernel(**inputs):
    import concourse.bacc as bacc
    from concourse.bass_utils import run_bass_kernel_spmd

    nc = bacc.Bacc("TRN2", target_bir_lowering=False, num_devices=1, dynamic_dma_scratch_size=1024)
    arrays = {name: np.ascontiguousarray(inputs[name]) for name in _INS}
    arrays["constants"] = constants()
    arrays["rotary"] = rotary_tables()
    aps = {name: nc.dram_tensor("in_" + name, v.shape, mybir.dt.from_np(v.dtype), kind="ExternalInput").ap()
           for name, v in arrays.items()}
    spill = nc.dram_tensor("spill", (P, KT, S), F32, kind="Internal").ap()
    out = nc.dram_tensor("out_0", (1, S, D), F32, kind="ExternalOutput").ap()
    build(nc, aps, aps["constants"], aps["rotary"], spill, out)
    r = run_bass_kernel_spmd(nc, [{"in_" + k: v for k, v in arrays.items()}], core_ids=[0])
    return r.results[0]["out_0"]
```

```python
from contextlib import ExitStack

import numpy as np
import concourse.bass as bass
from concourse import mybir

ALU = mybir.AluOpType
ACT = mybir.ActivationFunctionType
AX = mybir.AxisListType
F32 = mybir.dt.float32
F32R = mybir.dt.float32r

P = 128
S = 1024
D = 1024
KT = D // P
TT = S // P
FF = 2816
FT = FF // P
CHUNKS = ((0, 8), (8, 8), (16, 6))
M = 256
MT = M // P
H = 4
EPS = 1e-6
LAMBDA_INIT = 0.2
DIFF_SCALE = 0.125
XATTN_SCALE = 0.0625
HALVES = ((0, 512), (512, 1024))

G_FFN1, G_MIX, G_X, G_MEM, G_FFN2, G_FIN, G_NORM2, G_PB, G_PS, G_RET, G_DIFF, G_ROWS = (
    0, 8, 16, 24, 32, 40, 48, 56, 64, 72, 76, 80)

C_ID, C_MASK, C_ONES, C_DECAY, C_ZETA, C_XI, C_XI2, C_GCH, C_INV, C_COLS = (
    0, 128, 256, 384, 896, 1024, 1028, 1032, 1033, 1033 + 64)


def constants():
    c = np.zeros((P, C_COLS), np.float32)
    n = np.arange(P)
    c[:, C_ID:C_ID + P] = np.eye(P)
    c[:, C_MASK:C_MASK + P] = np.where(n[None, :] <= n[:, None], 0.0, -2.0 ** 100)
    c[:, C_ONES:C_ONES + P] = 1.0
    log_g = np.log(1.0 - 2.0 ** (-5.0 - np.arange(H)))
    for h in range(H):
        c[:, C_DECAY + h * P:C_DECAY + (h + 1) * P] = np.where(
            n[:, None] <= n[None, :], np.exp(-(n[:, None] + 1.0) * log_g[h]), 0.0)
        c[:, C_ZETA + 32 * h:C_ZETA + 32 * (h + 1)] = np.exp((P - 1.0 - n) * log_g[h])[:, None]
        xi = np.exp((n + 1.0) * log_g[h]) / 8.0
        c[:, C_XI + h] = xi
        c[:, C_XI2 + h] = xi * xi / P
        c[32 * h:32 * h + 32, C_GCH] = np.exp(P * log_g[h])
    for g in range(4):
        c[:, C_INV + 16 * g:C_INV + 16 * (g + 1)] = 1.0 / np.minimum(np.arange(1, 17), 2 << g)
    return c


def rotary_tables():
    inv = (1.0 / (np.float32(10000.0) ** (np.arange(0, 64, 2, dtype=np.float32) / np.float32(64)))).astype(np.float32)
    ang = (np.arange(S, dtype=np.float32)[None, :] * inv[:, None]).astype(np.float32)
    t = np.stack([np.cos(ang), np.sin(ang)], 1).astype(np.float32)
    return np.ascontiguousarray(np.tile(t, (H, 1, 1)))


def plan():
    at, n, u = {}, 0, 0
    order = [("gains", 1, 0), ("xt", KT, 0)]
    for f in ("ffn1", "ffn2"):
        stages = []
        for c, (_, k) in enumerate(CHUNKS):
            stages += [(f"{f}_up{c}", 2 * k, 2 * k), (f"{f}_down{c}", KT, KT)]
        if f == "ffn1":
            order += stages
            order += [("win", 24, 24), ("wout", KT, KT), ("wq", KT, KT),
                      ("memt", 2, 0), ("wkv", 2 * KT, 2 * KT), ("vt", MT, 0), ("wo", KT, KT)]
        else:
            order += stages
    order += [("pool_u", KT, KT), ("pool_g", 2 * KT, 2 * KT), ("fgain", 1, 0), ("pool_out", KT, KT),
              ("final", TT, 0)]
    for name, dn, du in order:
        at[name] = (n, u)
        n += dn
        u += du
    at["end"] = (n, u)
    return at


def build(nc, a, consts, rot, spill, out):
    at = plan()
    N = {k: v[0] for k, v in at.items()}
    U = {k: v[1] for k, v in at.items()}
    UNITS = U["end"]
    R_XT, R_FFN1, R_WOUT, R_WO, R_FFN2 = 0, 8, 16, 24, 32

    with ExitStack() as ctx:
        sem = lambda name: ctx.enter_context(nc.semaphore(name))
        base = [(nc.sbuf_base + 63) // 64 * 64]

        def here(name, shape, dt=F32):
            t = nc.alloc_sbuf_tensor_at(name, shape, dt, offset=base[0])
            base[0] += (int(np.prod(shape[1:])) * 4 + 31) // 32 * 32
            return t

        def over(name, shape, dt, offset):
            return nc.alloc_sbuf_tensor_at(name, shape, dt, offset=offset)

        K1 = 1024
        a_xt = base[0]
        xt = here("xt", [P, KT, S])
        a_r0 = base[0]
        r0h, r0l = here("r0h", [P, KT, S], F32R), here("r0l", [P, KT, S], F32R)
        a_r1 = base[0]
        r1h, r1l = here("r1h", [P, KT, S], F32R), here("r1l", [P, KT, S], F32R)
        raw = here("raw", [P, 2, KT, P])
        w_hi, w_lo = here("w_hi", [P, 2, KT, P], F32R), here("w_lo", [P, 2, KT, P], F32R)
        PAD = 16
        t1, t2, t3 = (here(f"t{i}", [P, PAD + S]) for i in (1, 2, 3))
        T1, T2, T3 = (t[:, PAD:PAD + S] for t in (t1, t2, t3))
        a_acc = base[0]
        acc, rstd, acc2, rfin = here("acc", [P, S]), here("rstd", [P, S]), here("acc2", [P, S]), here("rfin", [P, S])
        cst = here("cst", [P, C_COLS])
        gain = here("gain", [P, G_ROWS])
        ygain, gain2 = here("ygain", [P, 8]), here("gain2", [P, KT])
        ident_r, mask_r = here("ident_r", [P, P], F32R), here("mask_r", [P, P], F32R)
        lamv = here("lamv", [P, 2])
        small = here("small", [P, 64])
        assert base[0] <= nc.sbuf_usable_end, (base[0], nc.sbuf_usable_end)
        ident, ones = cst[:, C_ID:C_ID + P], cst[:, C_ONES:C_ONES + P]

        xin = over("xin", [P, TT, D], F32, a_r1)
        grow = over("grow", [P, P], F32, a_r1 + 32 * K1)
        lrow = over("lrow", [P, 4, 64], F32, a_r1 + 33 * K1)
        pa = over("pa", [P, 16, S], F32, a_r1)
        pb = over("pb", [P, 8, S], F32, a_xt)
        pa_f, pb_f = pa[:].rearrange("p t n -> p (t n)"), pb[:].rearrange("p t n -> p (t n)")
        y = over("y", [P, 8, S], F32, a_r0)
        y_f = y[:].rearrange("p t n -> p (t n)")
        w0 = a_r0 + 32 * K1
        rcos, rsin = T2, T3
        rtmp = [T1[:, c:c + 2 * P].rearrange("p (c n) -> p c n", c=2) for c in (0, 2 * P, 4 * P, 6 * P)]
        inf, rsq, on = (t.rearrange("p (h n) -> p h n", h=4) for t in (acc[:, 0:512], acc[:, 512:1024], rstd[:, 0:512]))
        qk, vc = (acc2[:, c:c + 512].rearrange("p (c n) -> p c n", c=4) for c in (0, 512))
        w1 = a_r0 + 16 * K1
        qbh, qbl = over("qbh", [P, 2, 2, H, P], F32R, w1), over("qbl", [P, 2, 2, H, P], F32R, w1 + 8 * K1)
        rbh, rbl = over("rbh", [P, 2, H, P], F32R, w0), over("rbl", [P, 2, H, P], F32R, w0 + 4 * K1)
        qkh, qkl = over("qkh", [P, 2, 4, P], F32R, w0 + 8 * K1), over("qkl", [P, 2, 4, P], F32R, w0 + 12 * K1)
        rvh, rvl = over("rvh", [P, 2, 4, P], F32R, w0 + 16 * K1), over("rvl", [P, 2, 4, P], F32R, w0 + 20 * K1)
        kz = over("kz", [P, 2, P], F32, w0 + 24 * K1)
        kzh, kzl = over("kzh", [P, 2, P], F32R, w0 + 25 * K1), over("kzl", [P, 2, P], F32R, w0 + 26 * K1)
        inh, inl = over("inh", [P, 4, P], F32R, w0 + 27 * K1), over("inl", [P, 4, P], F32R, w0 + 29 * K1)
        rs = over("rs", [P, 2, P], F32, w0 + 31 * K1)
        dqh, dql, dkh, dkl = (over(nm, [P, S], F32R, w0 + 4 * K1 * i) for i, nm in enumerate(("dqh", "dql", "dkh", "dkl")))
        dv = over("dv", [P, TT, 2, P], F32R, w0 + 16 * K1)
        pth, ptl = (over(nm, [P, 4, TT, P], F32R, a_r1 + 16 * K1 * i) for i, nm in enumerate(("pth", "ptl")))
        turned, raw_out = acc2, rfin
        e = ((T1, T2), (acc[:], rstd[:]))
        memh, meml, kxh, kxl = (over(nm, [P, KT, M], F32R, a_r0 + 8 * K1 * i) for i, nm in enumerate(("memh", "meml", "kxh", "kxl")))
        vxh, vxl = (over(nm, [P, MT, D], F32R, w0 + 8 * K1 * i) for i, nm in enumerate(("vxh", "vxl")))
        vf = over("vf", [P, KT, M], F32, a_acc + 8 * K1)
        memr = over("memr", [P, MT, D], F32, a_acc + 8 * K1)
        qsh, qsl = (over(nm, [P, 2, KT, P], F32R, w0 + 16 * K1 + 8 * K1 * i) for i, nm in enumerate(("qsh", "qsl")))
        pxh, pxl = (over(nm, [P, 2, KT, P], F32R, a_r0 + 8 * K1 * i) for i, nm in enumerate(("pxh", "pxl")))
        ex = (T1, T2)
        outrow = (T1, T2, rstd[:], rfin[:])
        fgain, frow = acc, acc2

        ps = ctx.enter_context(nc.psum_tensor("ps", [P, 4, S], F32))
        bank = lambda b: ps[:, b // 2, (b % 2) * 512:(b % 2) * 512 + 512]

        s_cst, s_vec, s_lrow, s_x, s_rot, s_mem, s_frow = map(sem, ("s_cst", "s_vec", "s_lrow", "s_x", "s_rot", "s_mem", "s_frow"))
        s_raw = [sem("s_raw0"), sem("s_raw1")]
        s_whi, s_wlo = sem("s_whi"), sem("s_wlo")
        s_mm, s_evac = sem("s_mm"), sem("s_evac")
        s_stat, s_ms = sem("s_stat"), sem("s_ms")
        s_setup_act, s_lam = sem("s_setup_act"), sem("s_lam")
        s_sqrt, s_rstd, s_sq2, s_acc2 = map(sem, ("s_sqrt", "s_rstd", "s_sq2", "s_acc2"))
        s_ahi, s_alo, s_sq, s_acc = sem("s_ahi"), sem("s_alo"), sem("s_sq"), sem("s_acc")
        s_silu, s_h, s_hhi, s_hlo = sem("s_silu"), sem("s_h"), sem("s_hhi"), sem("s_hlo")
        s_spill, s_reload = sem("s_spill"), sem("s_reload")
        s_dve, s_pool = sem("s_dve"), sem("s_pool")
        s_out = [sem(f"s_out{i}") for i in range(4)]

        (s_sg, s_rotd, s_qkh, s_qkl, s_vtr, s_ktr, s_vh, s_vl, s_kz, s_kzh, s_kzl, s_inner, s_inf, s_inh,
         s_inl, s_kv, s_r, s_rh, s_rl, s_o, s_rsq, s_rms, s_rroot, s_on, s_ytr, s_y) = map(sem, (
             "s_sg", "s_rotd", "s_qkh", "s_qkl", "s_vtr", "s_ktr", "s_vh", "s_vl", "s_kz", "s_kzh", "s_kzl",
             "s_inner", "s_inf", "s_inh", "s_inl", "s_kv", "s_r", "s_rh", "s_rl", "s_o", "s_rsq", "s_rms",
             "s_rroot", "s_on", "s_ytr", "s_y"))
        (s_dqh, s_dql, s_vt, s_dvtr, s_dvh, s_dvl, s_s, s_nm, s_exp, s_a, s_t, s_pth, s_ptl, s_pv, s_dsq,
         s_dms, s_droot, s_don, s_dytr, s_dy) = map(sem, (
             "s_dqh", "s_dql", "s_vt", "s_dvtr", "s_dvh", "s_dvl", "s_s", "s_nm", "s_exp", "s_a", "s_t",
             "s_pth", "s_ptl", "s_pv", "s_dsq", "s_dms", "s_droot", "s_don", "s_dytr", "s_dy"))
        s_qb, s_zero, s_zero2 = sem("s_qb"), sem("s_zero"), sem("s_zero2")
        s_oc, s_oadd = sem("s_oc"), sem("s_oadd")
        s_ms2, s_ra, s_mx, s_da, s_dn, s_xa = map(sem, ("s_ms2", "s_ra", "s_mx", "s_da", "s_dn", "s_xa"))
        s_yhi, s_ylo = sem("s_yhi"), sem("s_ylo")
        (s_msq, s_mms, s_mroot, s_mn, s_mhi, s_khi, s_vxh, s_qh, s_ql, s_xs, s_xnm,
         s_xe, s_xn, s_xt, s_xph, s_xpl, s_xpv, s_xy, s_xyl, s_qc) = map(sem, (
             "s_msq", "s_mms", "s_mroot", "s_mn", "s_mhi", "s_khi", "s_vxh",
             "s_qh", "s_ql", "s_xs", "s_xnm", "s_xe", "s_xn", "s_xt", "s_xph", "s_xpl", "s_xpv", "s_xy", "s_xyl", "s_qc"))
        s_pd, s_phi, s_plo, s_psilu, s_yy, s_fsq, s_fms, s_froot = map(sem, (
            "s_pd", "s_phi", "s_plo", "s_psilu", "s_yy", "s_fsq", "s_fms", "s_froot"))

        def weights(name):
            return a[name].rearrange("l (k p) n -> p (l k) n", p=P)

        def landed(u):
            rotary = max(0, min(2, (u - U["win"]) // 2 + 1))
            return 16 * (u // 2 + 1 + (H - 1) * rotary)

        def span(start, size):
            return slice(start, start + size) if isinstance(start, int) else bass.ds(start, size)

        block = ctx.enter_context(nc.Block())

        @block.sync
        def _(sp):
            sp.dma_start(cst[:], consts).then_inc(s_cst, 16)
            xv = a["x"].rearrange("b (t p) d -> p (b t) d", p=P)
            for t in (0, 2):
                sp.dma_start(xin[:, t:t + 2], xv[:, t:t + 2]).then_inc(s_x, 16)
            vectors = (("ffn1_norm", G_FFN1), ("mix_norm", G_MIX), ("xattn_norm", G_X), ("mem_norm", G_MEM),
                       ("ffn2_norm", G_FFN2), ("norm_w_2", G_NORM2), ("pool_scale_2", G_PS))
            for name, row in vectors:
                sp.dma_start(grow[row:row + KT, :], a[name].rearrange("l (k p) -> (l k) p", p=P)).then_inc(s_vec, 16)
            sp.dma_start(grow[G_FIN:G_FIN + KT, :], a["final_norm"].rearrange("(k p) -> k p", p=P)).then_inc(s_vec, 16)
            sp.dma_start(grow[G_PB:G_PB + KT, :], a["pool_group_b_2"].rearrange("l g (k p) -> (l g k) p", p=P)).then_inc(s_vec, 16)
            sp.dma_start(grow[G_RET:G_RET + H, :], a["ret_out_norm"].rearrange("l h p -> (l h) p")).then_inc(s_vec, 16)
            sp.dma_start(grow[G_DIFF:G_DIFF + H, :], a["diff_out_norm"].rearrange("l h p -> (l h) p")).then_inc(s_vec, 16)
            for i, name in enumerate(("diff_lq1", "diff_lk1", "diff_lq2", "diff_lk2")):
                sp.dma_start(lrow[0:1, i, :], a[name]).then_inc(s_lrow, 16)
            for t in (4, 6):
                sp.dma_start(xin[:, t:t + 2], xv[:, t:t + 2]).then_inc(s_x, 16)
            def load(u, j, src, kn=KT, first=False):
                if not first:
                    sp.wait_ge(s_wlo, u - 1)
                sp.dma_start(raw[:, j, 0:kn], src).then_inc(s_raw[j], 16)

            def ffn(f, first):
                wg, wu = weights(f + "_w_gate"), weights(f + "_w_up")
                wd = weights(f + "_w_down")
                for c, (t0, k) in enumerate(CHUNKS):
                    u = U[f"{f}_up{c}"]
                    peel = 1 if first and c == 0 else 0
                    for j in range(4 * peel):
                        w = (wg, wu)[j % 2]
                        load(u + j, j % 2, w[:, :, (j // 2) * P:(j // 2 + 1) * P], first=(j < 2))
                    with sp.Fori(peel, k // 2) as i:
                        for j in range(4):
                            w = (wg, wu)[j % 2]
                            load(u + 4 * i + j, j % 2, w[:, :, bass.ds(i * (2 * P) + (t0 + j // 2) * P, P)])
                    u = U[f"{f}_down{c}"]
                    with sp.Fori(0, 2) as i:
                        for j in range(4):
                            load(u + 4 * i + j, j % 2, wd[:, t0:t0 + k, bass.ds(i * (4 * P) + j * P, P)], k)

            def project(u, w, count, col0=0):
                with sp.Fori(0, count // 4) as i:
                    for j in range(4):
                        load(u + 4 * i + j, j % 2, w[:, :, bass.ds(i * (4 * P) + (col0 + j * P), P)])

            ffn("ffn1", True)
            win = weights("w_in")
            for j in range(4):
                sp.wait_ge(s_wlo, U["win"] + j - 1)
                for h in range(H):
                    col = (j // 2) * 256 + 64 * h + 32 * (j % 2)
                    sp.dma_start(raw[:, j % 2, :, 32 * h:32 * h + 32], win[:, :, col:col + 32]).then_inc(s_raw[j % 2], 16)
            sp.wait_ge(s_acc, R_FFN1 + KT)
            sp.dma_start(spill, xt[:]).then_inc(s_spill, 16)
            sp.wait_ge(s_rstd, 2)
            sp.dma_start(rcos, rot[:, 0]).then_inc(s_rot, 16)
            sp.dma_start(rsin, rot[:, 1]).then_inc(s_rot, 16)
            project(U["win"] + 4, win, 20, 4 * P)

            def project_units(name, w, js):
                for j in js:
                    load(U[name] + j, j % 2, w[:, :, j * P:(j + 1) * P])

            project_units("wout", weights("w_out"), (0, 1))
            sp.wait_ge(s_dql, H)
            sp.wait_ge(s_vt, H)
            sp.dma_start(xt[:], spill).then_inc(s_reload, 16)
            sp.wait_ge(s_dy, 2 * H)
            sp.dma_start(memr[:], a["mem"].rearrange("b (t p) d -> p (b t) d", p=P)).then_inc(s_mem, 16)
            project_units("wout", weights("w_out"), range(2, KT))
            project(U["wq"], weights("xattn_wq"), KT)
            project(U["wkv"], weights("xattn_wkv"), 2 * KT)
            project(U["wo"], weights("xattn_wo"), KT)
            ffn("ffn2", False)
            win2 = weights("pool_in_w_2")
            project(U["pool_u"], win2, KT)
            wg2 = a["pool_group_w_2"].rearrange("l g (k p) n -> p (l g) k n", p=P)
            for g in range(4):
                u = U["pool_g"] + 4 * g
                for j in range(2):
                    load(u + j, j, win2[:, :, (KT + 2 * g + j) * P:(KT + 2 * g + j + 1) * P])
                for j in range(2):
                    load(u + 2 + j, j, wg2[:, g, :, j * P:(j + 1) * P], 2)
                if g == 0:
                    sp.wait_ge(s_stat, 6)
                    sp.dma_start(frow[0:1, :], a["final_norm_w_2"].rearrange("(o d) -> o d", o=1)).then_inc(s_frow, 16)
            project(U["pool_out"], weights("pool_out_w_2"), KT)
            for t in range(TT):
                sp.wait_ge(s_evac, N["final"] + t + 1)
                sp.dma_start(out[0, t * P:(t + 1) * P, :], outrow[t % 4]).then_inc(s_out[t % 4], 16)
            for j in range(4):
                sp.wait_ge(s_out[j], 16 * TT // 4)

        @block.tensor
        def _(pe):
            def slot_free(n):
                if isinstance(n, int) and n < 4:
                    return
                pe.wait_ge(s_evac, n - 3)

            def product(out_ap, pairs, first=True, last=True):
                for i, (lhs, rhs) in enumerate(pairs):
                    mm = pe.matmul(out_ap, lhs, rhs, start=first and i == 0, stop=last and i == len(pairs) - 1,
                                   skip_group_check=True)
                return mm

            def unit(n, u, j, slot, rh, rl, kts=range(KT), cols=S, ready=None, midway=None):
                slot_free(n)
                pe.wait_ge(s_wlo, u + 1)
                for i, k in enumerate(kts):
                    if midway and i == 3:
                        midway()
                    if ready:
                        pe.wait_ge(ready[0], ready[1] + i + 1)
                    for p, (w, x) in enumerate(((w_hi, rh), (w_hi, rl), (w_lo, rh))):
                        for c0, c1 in HALVES:
                            if c0 >= cols:
                                continue
                            c1 = min(c1, cols)
                            mm = pe.matmul(ps[:, slot, c0:c1], w[:, j, i, :], x[:, k, c0:c1],
                                           start=(i == 0 and p == 0), stop=(i == len(kts) - 1 and p == 2))
                mm.then_inc(s_mm, 1)

            def units(stage, count, rh, rl, kts=range(KT), cols=S, ready=None, begin=0):
                n0, u0 = N[stage], U[stage]
                with pe.Fori(begin, count // 4) as i:
                    for j in range(4):
                        unit(n0 + j + 4 * i, u0 + j + 4 * i, j % 2, (n0 + j) % 4, rh, rl, kts, cols,
                             ready if j == 0 else None)

            stats = [0]

            def unit_pair(n, u, rh, rl, ready):
                for j, k in [(0, k) for k in range(4)] + [(1, k) for k in range(4)] + [
                        (j, k) for k in (4, 5) for j in range(2)] + [(j, k) for j in range(2) for k in (6, 7)]:
                    if k == 0:
                        slot_free(n + j)
                        pe.wait_ge(s_wlo, u + j + 1)
                    pe.wait_ge(ready[0], ready[1] + k + 1)
                    for p, (w, x) in enumerate(((w_hi, rh), (w_hi, rl), (w_lo, rh))):
                        for c0, c1 in HALVES:
                            mm = pe.matmul(ps[:, (n + j) % 4, c0:c1], w[:, j, k, :], x[:, k, c0:c1],
                                           start=(k == 0 and p == 0), stop=(k == KT - 1 and p == 2))
                    if k == KT - 1:
                        mm.then_inc(s_mm, 1)

            def opening(stage, count, rh, rl, tiles, ready, pair=False):
                n0, u0 = N[stage], U[stage]
                if pair:
                    unit_pair(n0, u0, rh, rl, ready)
                else:
                    unit(n0, u0, 0, n0 % 4, rh, rl, ready=ready)
                read = {}
                for i, (src, s_done, total) in enumerate(tiles):
                    n = n0 + 3 - i
                    pe.wait_ge(s_evac, n - 3)
                    pe.wait_ge(s_done, total)
                    for c0, c1 in HALVES:
                        mm = pe.matmul(ps[:, n % 4, c0:c1], ones, src[:, c0:c1], start=True, stop=True)
                    mm.then_inc(s_stat, 1)
                    stats[0] += 1
                    read[n] = stats[0]
                for j in range(2 if pair else 1, 4):
                    if n0 + j in read:
                        pe.wait_ge(s_ms, read[n0 + j])
                    unit(n0 + j, u0 + j, j % 2, (n0 + j) % 4, rh, rl)
                units(stage, count, rh, rl, begin=1)

            def ffn(f, rh, rl, hh, hl, r, pairs0):
                pairs = pairs0
                for c, (t0, k) in enumerate(CHUNKS):
                    if c == 0:
                        opening(f"{f}_up{c}", 2 * k, rh, rl, [(acc, s_acc, r + KT)], (s_alo, r), pair=(f == "ffn1"))
                    else:
                        units(f"{f}_up{c}", 2 * k, rh, rl)
                    units(f"{f}_down{c}", KT, hh, hl, kts=range(k), ready=(s_hlo, pairs))
                    pairs += k

            pe.wait_ge(s_cst, 16)
            pe.wait_ge(s_vec, 11 * 16)
            pe.transpose(ps[:, 0, 0:G_ROWS], grow[0:G_ROWS, :], cst[0:G_ROWS, C_ID:C_ID + G_ROWS])
            pe.wait_ge(s_lam, 1)
            pe.matmul(ps[:, 0, 512:514], cst[0:1, C_ONES:C_ONES + P], small[0:1, 4:6], start=True, stop=True).then_inc(s_mm, 1)
            for m in range(KT):
                n = N["xt"] + m
                slot_free(n)
                for t in range(TT):
                    if m == 0 and t == 0:
                        pe.wait_ge(s_x, 16 * TT // 2)
                    mm = pe.transpose(ps[:, n % 4, t * P:(t + 1) * P], xin[:, t, m * P:(m + 1) * P], ident)
                mm.then_inc(s_mm, 1)
            ffn("ffn1", r0h, r0l, r1h, r1l, R_XT, 0)
            opening("win", 24, r0h, r0l, [(acc, s_acc, R_FFN1 + KT)], (s_alo, R_FFN1))

            pe.wait_ge(s_evac, N["win"] + 24)

            def retention_transposes(i, first):
                pe.wait_ge(s_rotd, i + 1)
                if not first:
                    pe.wait_ge(s_vl, i)
                for h in range(H):
                    mm = pe.transpose(bank(4)[:, h * P:(h + 1) * P], vc[:, h], ident)
                mm.then_inc(s_vtr, 1)
                for c in range(2):
                    mm = pe.transpose(bank(5)[:, c * P:(c + 1) * P], qk[:, 2 + c], ident)
                mm.then_inc(s_ktr, 1)

            def retention_scores(i, par, first):
                pe.wait_ge(s_qb, i + 1)
                if not first:
                    pe.wait_ge(s_inf, i)
                block_q = lambda t, c: t[:, par, c].rearrange("p h n -> p (h n)")
                mm = product(bank(0), [(kk[:, par, 2 + c], block_q(qq, c)) for c in range(2)
                                       for kk, qq in ((qkh, qbh), (qkh, qbl), (qkl, qbh))])
                mm.then_inc(s_inner, 1)

            def retention_share(i, par, first):
                pe.wait_ge(s_kzl, i + 1)
                if not first:
                    pe.wait_ge(s_r, i)
                vh, vl = (t[:, par].rearrange("p h n -> p (h n)") for t in (rvh, rvl))
                for c in range(2):
                    mm = product(bank(2 + c), [(kzh[:, c], vh), (kzh[:, c], vl), (kzl[:, c], vh)])
                mm.then_inc(s_kv, 1)

            def retention_output(i, par, first, second=False):
                pe.wait_ge(s_inl, i + 1)
                if not first:
                    pe.wait_ge(s_rl, i)
                    if not second:
                        pe.wait_ge(s_on, i - 1)
                out_bank = bank(1 if par else 6)
                if not first:
                    block_r = lambda t, c: t[:, c].rearrange("p h n -> p (h n)")
                    product(out_bank, [(qq[:, par, c], block_r(rr, c)) for c in range(2)
                                       for qq, rr in ((qkh, rbh), (qkh, rbl), (qkl, rbh))], last=False)
                for h in range(H):
                    mm = product(out_bank[:, h * P:(h + 1) * P], [(inh[:, h], rvh[:, par, h]), (inh[:, h], rvl[:, par, h]),
                                                                  (inl[:, h], rvh[:, par, h])], first=first)
                mm.then_inc(s_o, 1)

            def retention_turn(i, first):
                pe.wait_ge(s_on, i + 1)
                if not first:
                    pe.wait_ge(s_y, i)
                for h in range(H):
                    mm = pe.transpose(bank(7)[:, h * P:(h + 1) * P], on[:, h], ident)
                mm.then_inc(s_ytr, 1)

            def retention_step(i, par, second=False):
                retention_transposes(i + 1, False)
                retention_share(i, par, False)
                retention_output(i, par, False, second)
                retention_turn(i - 1, second)
                retention_scores(i + 1, 1 - par, False)

            retention_transposes(0, True)
            retention_scores(0, 0, True)
            retention_transposes(1, False)
            retention_share(0, 0, True)
            retention_output(0, 0, True)
            retention_scores(1, 1, False)
            retention_step(1, 1, True)
            retention_step(2, 0)
            with pe.Fori(1, 3) as i:
                retention_step(2 * i + 1, 1)
                retention_step(2 * i + 2, 0)
            retention_output(TT - 1, 1, False)
            retention_turn(TT - 2, False)

            pe.sem_inc(s_t, 2)

            def scores(i, t, c):
                g = 8 * i + t
                w = (t + 1) * P
                rows = slice(64 * c, 64 * c + 64)
                pe.wait_ge(s_exp, 2 * g + c + 1)
                for c0 in range(0, w, 512):
                    c1 = min(c0 + 512, w)
                    product(ps[:, c, c0:c1], [(qq[rows, t * P:w], kk[rows, c0:c1])
                                              for qq, kk in ((dqh, dkh), (dqh, dkl), (dql, dkh))], last=False)
                mm = pe.matmul(ps[:, c, t * P:w], ident_r[:], mask_r[:], start=False, stop=True, skip_group_check=True)
                mm.then_inc(s_s, 1)

            def weighted_values(g, t):
                pe.wait_ge(s_ptl, g + 1)
                pe.wait_ge(s_oadd, g + 1)
                o = bank(6 + t % 2)
                for b in range(t + 1):
                    pe.matmul(o[:, 0:256], pth[:, t % 4, b], dv[:, b].rearrange("p c n -> p (c n)"), start=(b == 0),
                              stop=False, skip_group_check=True)
                    mm = pe.matmul(o[:, 0:P], ptl[:, t % 4, b], dv[:, b, 0], start=False, stop=(b == t),
                                   skip_group_check=True)
                mm.then_inc(s_pv, 1)

            def turn_weights(i, t):
                g = 8 * i + t
                pe.wait_ge(s_a, g + 1)
                if t == 0:
                    pe.wait_ge(s_dvl, i + 1)
                else:
                    pe.wait_ge(s_ptl, g)
                for b in range(t + 1):
                    mm = pe.transpose(ps[:, 2, b * P:(b + 1) * P], e[t % 2][1][:, b * P:(b + 1) * P], ident)
                mm.then_inc(s_t, 1)

            def turn_output(i, half, last=False):
                if half == 0:
                    pe.wait_ge(s_don, i + 1)
                pe.wait_ge(s_oadd, 8 * i + (12 if not last else 10) + half * (not last))
                for t in range(4):
                    c = (4 * half + t) * P
                    mm = pe.transpose(bank(7 - half)[:, t * P:(t + 1) * P], turned[:, c:c + P], ident)
                mm.then_inc(s_dytr, 1)

            def head(i, first):
                if not first:
                    weighted_values(8 * i - 2, TT - 2)
                pe.wait_ge(s_dql, i + 1)
                scores(i, 0, 0)
                scores(i, 0, 1)
                scores(i, 1, 0)
                if first:
                    retention_turn(TT - 1, False)
                pe.wait_ge(s_vt, i + 1)
                if not first:
                    pe.wait_ge(s_ptl, 8 * i)
                for t in range(TT):
                    mm = pe.transpose(ps[:, 2, t * P:(t + 1) * P], T3[:, t * P:(t + 1) * P], ident)
                mm.then_inc(s_dvtr, 1)
                if not first:
                    weighted_values(8 * i - 1, TT - 1)
                scores(i, 1, 1)
                turn_weights(i, 0)
                for t in range(1, TT):
                    if t + 1 < TT:
                        scores(i, t + 1, 0)
                    if t in (5, 6) and not first:
                        pe.wait_ge(s_dy, 2 * i + (t - 6))
                    if t >= 2:
                        weighted_values(8 * i + t - 2, t - 2)
                    if t + 1 < TT:
                        scores(i, t + 1, 1)
                    if t in (4, 5) and not first:
                        turn_output(i - 1, t - 4)
                    turn_weights(i, t)

            head(0, True)
            with pe.Fori(1, H - 1) as i:
                head(i, False)
            head(H - 1, False)
            weighted_values(8 * H - 2, TT - 2)
            weighted_values(8 * H - 1, TT - 1)

            def turn_last_head():
                turn_output(H - 1, 0, True)
                turn_output(H - 1, 1, True)

            for j in range(4):
                if N["wout"] % 4 + j == 3:
                    pe.wait_ge(s_dy, 2 * H)
                unit(N["wout"] + j, U["wout"] + j, j % 2, (N["wout"] + j) % 4, r1h, r1l, ready=(s_ylo, 0) if j == 0 else None,
                     midway=turn_last_head if j == 0 else None)
            units("wout", KT, r1h, r1l, begin=1)
            opening("wq", KT, r0h, r0l, [(acc, s_acc, R_WOUT + KT)], (s_alo, R_WOUT))

            pe.wait_ge(s_mn, 1)
            for q in range(2):
                n = N["memt"] + q
                slot_free(n)
                for k in range(4):
                    for t in range(MT):
                        c = k * M + t * P
                        mm = pe.transpose(ps[:, n % 4, c:c + P], memr[:, t, (4 * q + k) * P:(4 * q + k + 1) * P], ident)
                mm.then_inc(s_mm, 1)
            pe.wait_ge(s_evac, N["memt"] + 2)
            units("wkv", 2 * KT, memh, meml, cols=M)
            pe.wait_ge(s_evac, N["wkv"] + 2 * KT)
            for t in range(MT):
                for k in range(KT):
                    mm = pe.transpose(ps[:, 1 + t, k * P:(k + 1) * P], vf[:, k, t * P:(t + 1) * P], ident)
                mm.then_inc(s_mm, 1)

            def xscores(i, par, first):
                pe.wait_ge(s_qc, i + 1)
                if not first:
                    pe.wait_ge(s_xe, i - 1)
                for h in range(H):
                    mm = product(ps[:, 3 * par, h * M:(h + 1) * M], [(qq[:, par, 2 * h + c], kk[:, 2 * h + c]) for c in range(2)
                                                                     for qq, kk in ((qsh, kxh), (qsh, kxl), (qsl, kxh))])
                mm.then_inc(s_xs, 1)

            def xturn(i, par, first):
                pe.wait_ge(s_xn, i + 1)
                if not first:
                    pe.wait_ge(s_xpl, i)
                for b in range(KT):
                    mm = pe.transpose(ps[:, 1, b * P:(b + 1) * P], ex[par][:, b * P:(b + 1) * P], ident)
                mm.then_inc(s_xt, 1)

            def xvalues(i, par, first, slot=2):
                pe.wait_ge(s_xpl, i + 1)
                if not first and slot == 2:
                    pe.wait_ge(s_xyl, i)
                for f in range(KT):
                    h = f // 2
                    mm = product(ps[:, slot, f * P:(f + 1) * P], [(vv[:, t, f * P:(f + 1) * P], pp[:, par, h * MT + t])
                                                               for t in range(MT) for vv, pp in ((vxh, pxh), (vxl, pxh), (vxh, pxl))])
                mm.then_inc(s_xpv, 1)

            xscores(0, 0, True)
            xscores(1, 1, True)
            pe.wait_ge(s_evac, N["vt"] + MT)
            xturn(0, 0, True)
            xscores(2, 0, False)
            xturn(1, 1, False)
            xvalues(0, 0, True)
            xscores(3, 1, False)
            with pe.Fori(1, TT // 2 - 1) as i:
                for par in range(2):
                    xturn(2 * i + par, par, False)
                    xvalues(2 * i + (par - 1), 1 - par, False)
                    xscores(2 * i + (par + 2), par, False)
            xturn(TT - 2, 0, False)
            xvalues(TT - 3, 1, False)
            xturn(TT - 1, 1, False)
            xvalues(TT - 2, 0, False, 0)
            xvalues(TT - 1, 1, False, 3)

            pe.wait_ge(s_xyl, TT)
            units("wo", KT, r1h, r1l)
            ffn("ffn2", r0h, r0l, r1h, r1l, R_WO, FT)
            opening("pool_u", KT, r0h, r0l, [(acc, s_acc, R_FFN2 + KT), (acc2, s_acc2, KT)], (s_alo, R_FFN2))
            for g in range(4):
                n, u = N["pool_g"] + 4 * g, U["pool_g"] + 4 * g
                for j in range(2):
                    unit(n + j, u + j, j, (n + j) % 4, r0h, r0l)
                for j in range(2, 4):
                    unit(n + j, u + j, j % 2, (n + j) % 4, r1h, r1l, kts=range(2 * g, 2 * g + 2), ready=(s_plo, 2 * g))
            n = N["fgain"]
            slot_free(n)
            pe.wait_ge(s_frow, 16)
            for c0, c1 in HALVES:
                mm = pe.matmul(ps[:, n % 4, c0:c1], cst[0:1, C_ONES:C_ONES + P], frow[0:1, c0:c1], start=True, stop=True)
            mm.then_inc(s_mm, 1)
            units("pool_out", KT, r1h, r1l, ready=(s_plo, KT))
            for t in range(TT):
                n = N["final"] + t
                slot_free(n)
                for m in range(KT):
                    pe.wait_ge(s_evac, N["pool_out"] + m + 1)
                    mm = pe.transpose(ps[:, n % 4, m * P:(m + 1) * P], xt[:, m, t * P:(t + 1) * P], ident)
                mm.then_inc(s_mm, 1)

        @block.scalar
        def _(act):
            def step(n, u, j):
                act.wait_ge(s_mm, n + 1)
                if u + 2 < UNITS:
                    act.wait_ge(s_raw[j], landed(u + 2))
                    act.activation(w_hi[:, j], raw[:, j], ACT.Copy).then_inc(s_whi, 1)

            def loop_step(n0, u0, i, j):
                act.wait_ge(s_mm, 4 * i + (n0 + j + 1))
                act.wait_ge(s_raw[j % 2], 32 * i + landed(u0 + j + 2))
                act.activation(w_hi[:, j % 2], raw[:, j % 2], ACT.Copy).then_inc(s_whi, 1)

            def split_residual(n, r, m, xh, g, g_sq2=None):
                act.wait_ge(s_evac, n + 1)
                act.activation(xh[:, m], xt[:, m], ACT.Copy, scale=g[:, m:m + 1]).then_inc(s_ahi, 1)
                if r + m > 0:
                    act.wait_ge(s_acc, r + m)
                act.activation(T2, xt[:, m], ACT.Square).then_inc(s_sq, 1)
                if g_sq2 is not None:
                    if m > 0:
                        act.wait_ge(s_acc2, m)
                    act.activation(T3, xt[:, m], ACT.Square, scale=g_sq2[:, m:m + 1]).then_inc(s_sq2, 1)

            roots = [0]

            def root():
                roots[0] += 1
                act.wait_ge(s_ms, roots[0])
                act.activation(T2, T1, ACT.Sqrt).then_inc(s_sqrt, 1)

            def ffn(f, hh, pairs0, residual):
                pairs = pairs0
                hh_f = hh[:].rearrange("p t n -> p (t n)")
                for c, (t0, k) in enumerate(CHUNKS):
                    n0, u0 = N[f"{f}_up{c}"], U[f"{f}_up{c}"]

                    def up(i, opens=False):
                        for q in range(2):
                            loop_step(n0, u0, i, 2 * q)
                            if opens and q == 0:
                                root()
                            act.wait_ge(s_evac, 4 * i + (n0 + 2 * q + 1))
                            act.activation(T2, T1, ACT.Silu).then_inc(s_silu, 1)
                            loop_step(n0, u0, i, 2 * q + 1)
                            act.wait_ge(s_h, 2 * i + (pairs + q + 1))
                            act.wait_ge(s_rstd, 1)
                            act.activation(hh_f[:, bass.ds(i * (2 * S) + q * S, S)], T1, ACT.Copy).then_inc(s_hhi, 1)

                    if c == 0:
                        up(0, True)
                    with act.Fori(1 if c == 0 else 0, k // 2) as i:
                        up(i)
                    pairs += k
                    n0, u0 = N[f"{f}_down{c}"], U[f"{f}_down{c}"]
                    if c < len(CHUNKS) - 1:
                        with act.Fori(0, 2) as i:
                            for j in range(4):
                                loop_step(n0, u0, i, j)
                    else:
                        for m in range(KT):
                            step(n0 + m, u0 + m, m % 2)
                            residual(n0 + m, m)

            act.wait_ge(s_cst, 16)
            act.activation(ident_r[:], ident, ACT.Copy)
            act.activation(mask_r[:], cst[:, C_MASK:C_MASK + P], ACT.Copy).then_inc(s_setup_act, 1)
            act.wait_ge(s_dve, 2)
            act.activation(small[0:1, 2:4], small[0:1, 0:2], ACT.Exp).then_inc(s_setup_act, 1)
            for u in range(2):
                act.wait_ge(s_raw[u], 16)
                act.activation(w_hi[:, u], raw[:, u], ACT.Copy).then_inc(s_whi, 1)
            act.wait_ge(s_evac, 1)
            for m in range(KT):
                n = N["xt"] + m
                act.wait_ge(s_mm, n + 1)
                act.activation(r0h[:, m], ps[:, n % 4], ACT.Copy, scale=gain[:, G_FFN1 + m:G_FFN1 + m + 1]).then_inc(s_ahi, 1)
                if m >= 2:
                    act.wait_ge(s_acc, m - 1)
                act.activation((T2, T3)[m % 2], ps[:, n % 4], ACT.Square).then_inc(s_sq, 1)
                act.activation(xt[:, m], ps[:, n % 4], ACT.Copy).then_inc(s_evac, 1)
            ffn("ffn1", r1h, 0, lambda n, m: split_residual(n, R_FFN1, m, r0h, gain[:, G_MIX:G_MIX + KT]))
            for j in range(4):
                step(N["win"] + j, U["win"] + j, j % 2)
                if j == 0:
                    root()
            with act.Fori(0, 2) as i:
                for j in range(4):
                    loop_step(N["win"] + 4, U["win"] + 4, i, j)
            act.wait_ge(s_evac, N["win"] + 12)
            act.activation(pa[:, 8:12], pa[:, 8:12], ACT.Silu).then_inc(s_sg, 1)
            with act.Fori(2, 5) as i:
                for j in range(4):
                    loop_step(N["win"] + 4, U["win"] + 4, i, j)

            act.wait_ge(s_evac, N["win"] + 24)

 
            def block_diagonal(dst, src):
                for h in range(H):
                    rows = slice(32 * h, 32 * h + 32)
                    ins = act.activation(dst[rows, :, h], src[rows], ACT.Copy)
                return ins

            def queries(i, par, first):
                act.wait_ge(s_rotd, i + 1)
                if not first:
                    act.wait_ge(s_o, i - 1)
                act.activation(qkh[:, par], qk, ACT.Copy).then_inc(s_qkh, 1)
                act.wait_ge(s_qkh, i + 1)
                block_diagonal(qbh[:, par], qkh[:, par, 0:2])

            def low_queries(i, par):
                act.wait_ge(s_qkl, i + 1)
                block_diagonal(qbl[:, par], qkl[:, par, 0:2]).then_inc(s_qb, 1)

            def values(i, par):
                act.wait_ge(s_vtr, i + 1)
                act.activation(rvh[:, par], bank(4).rearrange("p (h n) -> p h n", h=4), ACT.Copy).then_inc(s_vh, 1)

            def keys(i, first):
                act.wait_ge(s_kz, i + 1)
                if not first:
                    act.wait_ge(s_kv, i)
                act.activation(kzh[:], kz[:], ACT.Copy).then_inc(s_kzh, 1)

            def split_scores(i, first):
                act.wait_ge(s_inf, i + 1)
                if not first:
                    act.wait_ge(s_o, i)
                act.activation(inh[:], inf, ACT.Copy).then_inc(s_inh, 1)

            def square(i, par):
                act.wait_ge(s_o, i + 1)
                act.activation(rsq, bank(1 if par else 6).rearrange("p (h n) -> p h n", h=4), ACT.Square).then_inc(s_rsq, 1)

            def root_square(i):
                act.wait_ge(s_rms, i + 1)
                act.activation(small[:, 8:12], small[:, 4:8], ACT.Sqrt).then_inc(s_rroot, 1)

            def split_state(i):
                act.wait_ge(s_r, i + 1)
                act.wait_ge(s_o, i + 1)
                block_diagonal(rbh[:], rs[:]).then_inc(s_rh, 1)

            def retention_step(i, par):
                split_state(i - 1)
                split_scores(i, False)
                square(i - 1, 1 - par)
                queries(i + 1, 1 - par, False)
                values(i + 1, 1 - par)
                root_square(i - 1)
                low_queries(i + 1, 1 - par)
                keys(i + 1, False)

            act.wait_ge(s_zero2, 1)
            queries(0, 0, True)
            values(0, 0)
            act.wait_ge(s_zero, 1)
            low_queries(0, 0)
            keys(0, True)
            split_scores(0, True)
            act.wait_ge(s_rotd, 2)
            act.activation(qkh[:, 1], qk, ACT.Copy).then_inc(s_qkh, 1)
            act.wait_ge(s_qkh, 2)
            block_diagonal(qbh[:, 1], qkh[:, 1, 0:2])
            values(1, 1)
            low_queries(1, 1)
            keys(1, False)
            act.wait_ge(s_zero, 2)
            retention_step(1, 1)
            retention_step(2, 0)
            with act.Fori(1, 3) as i:
                retention_step(2 * i + 1, 1)
                retention_step(2 * i + 2, 0)
            split_state(TT - 2)
            split_scores(TT - 1, False)
            square(TT - 2, 0)
            root_square(TT - 2)
            square(TT - 1, 1)

            act.sem_inc(s_exp, 2)

            def exps(i, t, c):
                w = (t + 1) * P
                act.wait_ge(s_nm, 2 * (8 * i + t) + c + 1)
                act.wait_ge(s_t, 8 * i + t + 1)
                col = 2 * (t % 2) + c
                act.activation(e[t % 2][c][:, 0:w], ps[:, c, 0:w], ACT.Exp, bias=small[:, 16 + col:17 + col],
                               scale=DIFF_SCALE, accum_out=small[:, 20 + col:21 + col]).then_inc(s_exp, 1)

            def square_output(i):
                act.wait_ge(s_oadd, 8 * i + TT + 2)
                act.activation(turned[:], raw_out[:], ACT.Square).then_inc(s_dsq, 1)

            def root_output(i):
                act.wait_ge(s_dms, i + 1)
                act.activation(small[:, 32:40], small[:, 24:32], ACT.Sqrt).then_inc(s_droot, 1)

            def split_weights(g, t, reused):
                act.wait_ge(s_t, g + 3)
                if reused:
                    act.wait_ge(s_pv, g - 3)
                act.activation(pth[:, t % 4, 0:t + 1].rearrange("p t n -> p (t n)"), ps[:, 2, 0:(t + 1) * P], ACT.Copy).then_inc(s_pth, 1)

            def keep_output(i, half, at):
                act.wait_ge(s_dytr, 2 * i + half + 1)
                act.activation(y_f[:, at], bank(7 - half), ACT.Copy).then_inc(s_dy, 1)

            def split_keys(i, first=False):
                if not first:
                    act.wait_ge(s_s, 16 * i)
                    act.wait_ge(s_o, TT)
                act.activation(dqh[:], pa_f[:, span(i * S + 12 * S, S)], ACT.Copy).then_inc(s_dqh, 1)
                if first:
                    root_square(TT - 1)
                act.activation(dkh[:], pb_f[:, span(i * S, S)], ACT.Copy).then_inc(s_dqh, 1)

            def head(i, first, last=False):
                if first:
                    split_keys(0, True)
                if not first:
                    split_weights(8 * i - 1, TT - 1, True)
                exps(i, 0, 0)
                exps(i, 0, 1)
                exps(i, 1, 0)
                act.wait_ge(s_dvtr, i + 1)
                if not first:
                    act.wait_ge(s_pv, 8 * i)
                act.activation(dv[:, :, 0], ps[:, 2].rearrange("p (t n) -> p t n", t=TT), ACT.Copy).then_inc(s_dvh, 1)
                for t in range(1, TT):
                    if t == TT - 1 and not last:
                        split_keys(i + 1)
                    split_weights(8 * i + t - 1, t - 1, t > 4 or not first)
                    exps(i, t, 1)
                    if t + 1 < TT:
                        exps(i, t + 1, 0)
                    if t == 1 and not first:
                        square_output(i - 1)
                    if t == 2 and not first:
                        root_output(i - 1)
                    if t in (4, 5) and not first:
                        keep_output(i - 1, t - 4, span(i * S + 3 * S + (t - 4) * 512, 512))

            head(0, True)
            with act.Fori(1, H - 1) as i:
                head(i, False)
            head(H - 1, False, True)
            split_weights(8 * H - 1, TT - 1, True)

            def split_mixed(k):
                act.activation(r1h[:, k], y[:, k], ACT.Copy, scale=ygain[:, k:k + 1]).then_inc(s_yhi, 1)

            square_output(H - 1)
            act.wait_ge(s_dy, 2 * H - 2)
            split_mixed(0)
            split_mixed(1)
            root_output(H - 1)
            for k in range(2, KT - 1):
                split_mixed(k)
            for half in range(2):
                keep_output(H - 1, half, slice(7 * S + half * 512, 7 * S + (half + 1) * 512))
            act.wait_ge(s_dy, 2 * H)
            split_mixed(KT - 1)
            act.wait_ge(s_mem, 16)
            for t in range(MT):
                act.activation((T3, T2)[t], memr[:, t], ACT.Square, accum_out=small[:, t:t + 1]).then_inc(s_msq, 1)
            act.wait_ge(s_mms, 1)
            act.activation(small[:, 4:6], small[:, 2:4], ACT.Sqrt).then_inc(s_mroot, 1)
            for m in range(KT):
                step(N["wout"] + m, U["wout"] + m, m % 2)
                split_residual(N["wout"] + m, R_WOUT, m, r0h, gain[:, G_X:G_X + KT])
            def split_memory():
                for q in range(2):
                    n = N["memt"] + q
                    act.wait_ge(s_mm, n + 1)
                    for k in range(4):
                        act.activation(memh[:, 4 * q + k], ps[:, n % 4, k * M:(k + 1) * M], ACT.Copy,
                                       scale=gain[:, G_MEM + 4 * q + k:G_MEM + 4 * q + k + 1]).then_inc(s_mhi, 1)

            for i in range(2):
                for j in range(4):
                    step(N["wq"] + 4 * i + j, U["wq"] + 4 * i + j, j % 2)
                    if i == 0 and j == 0:
                        root()
                    if 4 * i + j == KT - 1:
                        split_memory()
                    act.wait_ge(s_evac, 4 * i + (N["wq"] + j + 1))
                    act.activation(r1h[:, 4 * i + j], T1, ACT.Copy).then_inc(s_qh, 1)

            for m in range(2 * KT):
                n = N["wkv"] + m
                step(n, U["wkv"] + m, m % 2)
                if m < KT:
                    act.activation(kxh[:, m], ps[:, n % 4, 0:M], ACT.Copy).then_inc(s_khi, 1)
            for t in range(MT):
                n = N["vt"] + t
                act.wait_ge(s_mm, n + 1)
                act.activation(vxh[:, t], ps[:, 1 + t], ACT.Copy).then_inc(s_vxh, 1)

            def xexp(i, par, first):
                act.wait_ge(s_xnm, i + 1)
                if not first:
                    act.wait_ge(s_xt, i - 1)
                for h in range(H):
                    ins = act.activation(ex[par][:, h * M:(h + 1) * M], ps[:, 3 * par, h * M:(h + 1) * M], ACT.Exp, scale=XATTN_SCALE,
                                         bias=small[:, 16 + h:17 + h], accum_out=small[:, 20 + h:21 + h])
                ins.then_inc(s_xe, 1)

            def xweights(i, par, first):
                act.wait_ge(s_xt, i + 1)
                if not first:
                    act.wait_ge(s_xpv, i - 1)
                act.activation(pxh[:, par].rearrange("p k n -> p (k n)"), ps[:, 1], ACT.Copy).then_inc(s_xph, 1)

            def xout(i, at, slot=2):
                act.wait_ge(s_xpv, i + 1)
                act.activation(r1h[:, :, at], ps[:, slot].rearrange("p (k n) -> p k n", k=KT), ACT.Copy).then_inc(s_xy, 1)

            act.wait_ge(s_evac, N["vt"] + MT)
            xexp(0, 0, True)
            xweights(0, 0, True)
            xexp(1, 1, True)
            xweights(1, 1, True)
            xexp(2, 0, False)
            xout(0, slice(0, P))
            with act.Fori(1, TT // 2 - 1) as i:
                for par in range(2):
                    xweights(2 * i + par, par, False)
                    xexp(2 * i + (par + 1), 1 - par, False)
                    xout(2 * i + (par - 1), bass.ds(i * (2 * P) + (par - 1) * P, P))
            xweights(TT - 2, 0, False)
            xexp(TT - 1, 1, False)
            xout(TT - 3, slice((TT - 3) * P, (TT - 2) * P))
            xweights(TT - 1, 1, False)
            xout(TT - 2, slice((TT - 2) * P, (TT - 1) * P), 0)
            xout(TT - 1, slice((TT - 1) * P, TT * P), 3)
            for m in range(KT):
                step(N["wo"] + m, U["wo"] + m, m % 2)
                split_residual(N["wo"] + m, R_WO, m, r0h, gain[:, G_FFN2:G_FFN2 + KT])
            ffn("ffn2", r1h, FT, lambda n, m: split_residual(n, R_FFN2, m, r0h, gain2, gain[:, G_FIN:G_FIN + KT]))

            for t in range(KT):
                step(N["pool_u"] + t, U["pool_u"] + t, t % 2)
                if t == 0:
                    act.wait_ge(s_ms2, 1)
                    act.activation(T2, T1, ACT.Sqrt).then_inc(s_sqrt, 1)
                act.wait_ge(s_pd, t + 1)
                act.activation(r1h[:, t], (T3, T2)[t // 2 % 2], ACT.Copy).then_inc(s_phi, 1)
            for g in range(4):
                n, u = N["pool_g"] + 4 * g, U["pool_g"] + 4 * g
                for j in range(2):
                    step(n + j, u + j, j)
                    if j == 1:
                        step(n + 2, u + 2, 0)
                    act.wait_ge(s_evac, n + j + 1)
                    act.activation((T1, T2)[j], (T1, T2)[j], ACT.Silu).then_inc(s_psilu, 1)
                for j in range(2):
                    if j == 1:
                        step(n + 3, u + 3, 1)
                    act.wait_ge(s_yy, 2 * g + j + 1)
                    act.wait_ge(s_mm, n + 4)
                    act.activation(r1h[:, 2 * g + j], T3, ACT.Copy).then_inc(s_phi, 1)
            act.activation(rfin[:], rfin[:], ACT.Sqrt).then_inc(s_sqrt, 1)
            for m in range(KT):
                step(N["pool_out"] + m, U["pool_out"] + m, m % 2)
            def square_row(t):
                n = N["final"] + t
                act.wait_ge(s_mm, n + 1)
                act.activation((T3, acc2[:])[t % 2], ps[:, n % 4], ACT.Square, accum_out=small[:, t:t + 1]).then_inc(s_fsq, 1)

            square_row(0)
            for t in range(TT):
                if t + 1 < TT:
                    square_row(t + 1)
                act.wait_ge(s_fms, t + 1)
                act.activation(small[:, 16 + t:17 + t], small[:, 8 + t:9 + t], ACT.Sqrt).then_inc(s_froot, 1)

        @block.vector
        def _(dve):
            chain = [0]

            def link(ins):
                chain[0] += 1
                ins.then_inc(s_dve, 1)
                dve.wait_ge(s_dve, chain[0])

            def step(n, u, j):
                if u + 2 < UNITS:
                    dve.wait_ge(s_whi, u + 3)
                    dve.tensor_tensor(w_lo[:, j], raw[:, j], w_hi[:, j].bitcast(F32), ALU.subtract).then_inc(s_wlo, 1)
                    dve.wait_ge(s_wlo, u + 3)
                dve.wait_ge(s_mm, n + 1)

            def loop_step(n0, u0, i, j):
                dve.wait_ge(s_whi, 4 * i + (u0 + j + 3))
                dve.tensor_tensor(w_lo[:, j % 2], raw[:, j % 2], w_hi[:, j % 2].bitcast(F32), ALU.subtract).then_inc(s_wlo, 1)
                dve.wait_ge(s_wlo, 4 * i + (u0 + j + 3))
                dve.wait_ge(s_mm, 4 * i + (n0 + j + 1))

            def split_residual(r, m, xh, xl, g, two=False):
                dve.wait_ge(s_ahi, r + m + 1)
                dve.scalar_tensor_tensor(out=xl[:, m], in0=xt[:, m], scalar=g[:, m:m + 1], in1=xh[:, m].bitcast(F32),
                                         op0=ALU.mult, op1=ALU.subtract).then_inc(s_alo, 1)
                for total, part, done, own, r0 in ((acc, T2, s_sq, s_acc, r),) + (((acc2, T3, s_sq2, s_acc2, 0),) if two else ()):
                    dve.wait_ge(done, r0 + m + 1)
                    if m == 0:
                        dve.tensor_copy(total[:], part).then_inc(own, 1)
                    else:
                        dve.wait_ge(own, r0 + m)
                        dve.tensor_tensor(total[:], total[:], part, ALU.add).then_inc(own, 1)

            roots = [0]

            def factors(n0, dst):
                dve.wait_ge(s_stat, roots[0] + 1)
                dve.tensor_scalar(T1, ps[:, (n0 + 3) % 4], 1.0 / D, EPS, ALU.mult, ALU.add).then_inc(s_ms, 1)
                inverse(dst)

            def inverse(dst, root=T2):
                roots[0] += 1
                dve.wait_ge(s_sqrt, roots[0])
                dve.reciprocal(dst[:], root).then_inc(s_rstd, 1)
                dve.wait_ge(s_rstd, roots[0])

            def residual_add(n, m, scale):
                dve.wait_ge(s_evac, n)
                dve.scalar_tensor_tensor(out=xt[:, m], in0=ps[:, n % 4], scalar=scale, in1=xt[:, m],
                                         op0=ALU.mult, op1=ALU.add).then_inc(s_evac, 1)

            def ffn(f, hh, hl, pairs0, split):
                pairs = pairs0
                hh_f, hl_f = (t[:].rearrange("p t n -> p (t n)") for t in (hh, hl))
                xt_f = xt[:].rearrange("p t n -> p (t n)")
                for c, (t0, k) in enumerate(CHUNKS):
                    n0, u0 = N[f"{f}_up{c}"], U[f"{f}_up{c}"]

                    def up(i, opens=False):
                        for q in range(2):
                            loop_step(n0, u0, i, 2 * q)
                            if opens and q == 0:
                                factors(n0, rstd)
                            dve.tensor_tensor(T1, ps[:, (n0 + 2 * q) % 4], rstd[:], ALU.mult).then_inc(s_evac, 1)
                            loop_step(n0, u0, i, 2 * q + 1)
                            dve.tensor_tensor(T3, ps[:, (n0 + 2 * q + 1) % 4], rstd[:], ALU.mult).then_inc(s_evac, 1)
                            dve.wait_ge(s_silu, 2 * i + (pairs + q + 1))
                            dve.wait_ge(s_evac, 4 * i + (n0 + 2 * q + 2))
                            dve.tensor_tensor(T1, T2, T3, ALU.mult).then_inc(s_h, 1)
                            dve.wait_ge(s_hhi, 2 * i + (pairs + q + 1))
                            at_t = bass.ds(i * (2 * S) + q * S, S)
                            dve.tensor_tensor(hl_f[:, at_t], T1, hh_f[:, at_t].bitcast(F32), ALU.subtract).then_inc(s_hlo, 1)

                    if c == 0:
                        up(0, True)
                    with dve.Fori(1 if c == 0 else 0, k // 2) as i:
                        up(i)
                    pairs += k
                    n0, u0 = N[f"{f}_down{c}"], U[f"{f}_down{c}"]
                    if c < len(CHUNKS) - 1:
                        with dve.Fori(0, 2) as i:
                            for j in range(4):
                                loop_step(n0, u0, i, j)
                                at_m = bass.ds(i * (4 * S) + j * S, S)
                                dve.wait_ge(s_evac, 4 * i + (n0 + j))
                                dve.scalar_tensor_tensor(out=xt_f[:, at_m], in0=ps[:, (n0 + j) % 4], scalar=0.5, in1=xt_f[:, at_m],
                                                         op0=ALU.mult, op1=ALU.add).then_inc(s_evac, 1)
                    else:
                        for m in range(KT):
                            step(n0 + m, u0 + m, m % 2)
                            residual_add(n0 + m, m, 0.5)
                            split(m)

            for t in (t1, t2, t3):
                dve.memset(t[:, 0:PAD], 0.0)
            dve.memset(lamv[:, 0:1], 1.0)
            dve.wait_ge(s_lrow, 64)
            prod = T3[0:1, 0:128].rearrange("p (a n) -> p a n", a=2)
            link(dve.tensor_tensor(prod, lrow[0:1, 0::2, :], lrow[0:1, 1::2, :], ALU.mult))
            link(dve.tensor_reduce(small[0:1, 0:2], prod, AX.X, ALU.add))
            dve.wait_ge(s_setup_act, 2)
            link(dve.tensor_tensor(small[0:1, 6:7], small[0:1, 3:4], small[0:1, 2:3], ALU.subtract))
            for c in (4, 5):
                ins = dve.tensor_scalar(small[0:1, c:c + 1], small[0:1, 6:7], -LAMBDA_INIT, None, ALU.add)
                if c == 4:
                    link(ins)
            ins.then_inc(s_lam, 1)
            dve.wait_ge(s_mm, 1)
            link(dve.tensor_copy(gain[:], ps[:, 0, 0:G_ROWS]))
            link(dve.tensor_tensor(gain2[:], gain[:, G_FIN:G_FIN + KT], gain[:, G_NORM2:G_NORM2 + KT], ALU.mult))
            dve.tensor_copy(ygain[:, 0:4], gain[:, G_RET:G_RET + 4])
            dve.tensor_scalar(ygain[:, 4:8], gain[:, G_DIFF:G_DIFF + 4], 1.0 - LAMBDA_INIT, None, ALU.mult)
            dve.tensor_copy(lamv[:, 1:2], ps[:, 0, 512:513]).then_inc(s_evac, 1)
            for u in range(2):
                dve.wait_ge(s_whi, u + 1)
                dve.tensor_tensor(w_lo[:, u], raw[:, u], w_hi[:, u].bitcast(F32), ALU.subtract).then_inc(s_wlo, 1)
            for m in range(KT):
                dve.wait_ge(s_evac, N["xt"] + m + 1)
                dve.scalar_tensor_tensor(out=r0l[:, m], in0=xt[:, m], scalar=gain[:, G_FFN1 + m:G_FFN1 + m + 1],
                                         in1=r0h[:, m].bitcast(F32), op0=ALU.mult, op1=ALU.subtract).then_inc(s_alo, 1)
                if m == 0:
                    dve.tensor_copy(acc[:], T2).then_inc(s_acc, 1)
                else:
                    dve.wait_ge(s_acc, m)
                    dve.tensor_tensor(acc[:], acc[:], (T2, T3)[m % 2], ALU.add).then_inc(s_acc, 1)
            ffn("ffn1", r1h, r1l, 0, lambda m: split_residual(R_FFN1, m, r0h, r0l, gain[:, G_MIX:G_MIX + KT]))

            for j in range(4):
                step(N["win"] + j, U["win"] + j, j % 2)
                if j == 0:
                    factors(N["win"], rstd)
                dve.tensor_tensor(pa[:, j], ps[:, (N["win"] + j) % 4], rstd[:], ALU.mult).then_inc(s_evac, 1)
            for dst, begin, count, first in ((pa_f, 1, 16, 0), (pb_f, 0, 8, 16)):
                if first == 16:
                    dve.wait_ge(s_spill, 16)
                with dve.Fori(begin, count // 4) as i:
                    for j in range(4):
                        loop_step(N["win"] + first, U["win"] + first, i, j)
                        dve.tensor_tensor(dst[:, bass.ds(i * (4 * S) + j * S, S)], ps[:, (N["win"] + first + j) % 4], rstd[:],
                                          ALU.mult).then_inc(s_evac, 1)

            zeta = cst[:, C_ZETA:C_ZETA + P].unsqueeze(1).to_broadcast([P, 2, P])
            decay = cst[:, C_DECAY:C_DECAY + 4 * P].rearrange("p (h n) -> p h n", h=4)

            def low_queries(i, par):
                dve.wait_ge(s_qkh, i + 1)
                dve.tensor_tensor(qkl[:, par], qk, qkh[:, par].bitcast(F32), ALU.subtract).then_inc(s_qkl, 1)

            def low_values(i, par):
                dve.wait_ge(s_vh, i + 1)
                dve.tensor_tensor(rvl[:, par], bank(4).rearrange("p (h n) -> p h n", h=4), rvh[:, par].bitcast(F32),
                                  ALU.subtract).then_inc(s_vl, 1)

            def decayed_keys(i):
                dve.wait_ge(s_ktr, i + 1)
                dve.tensor_tensor(kz[:], bank(5)[:, 0:2 * P].rearrange("p (c n) -> p c n", c=2), zeta, ALU.mult).then_inc(s_kz, 1)

            def low_keys(i):
                dve.wait_ge(s_kzh, i + 1)
                dve.tensor_tensor(kzl[:], kz[:], kzh[:].bitcast(F32), ALU.subtract).then_inc(s_kzl, 1)

            def decayed_scores(i):
                dve.wait_ge(s_inner, i + 1)
                dve.tensor_tensor(inf, bank(0).rearrange("p (h n) -> p h n", h=4), decay, ALU.mult).then_inc(s_inf, 1)

            def low_scores(i):
                dve.wait_ge(s_inh, i + 1)
                dve.tensor_tensor(inl[:], inf, inh[:].bitcast(F32), ALU.subtract).then_inc(s_inl, 1)

            def state(i, first):
                dve.wait_ge(s_kv, i + 1)
                for h in range(H):
                    rows = slice(32 * h, 32 * h + 32)
                    kv = ps[rows, 1].rearrange("p (c h n) -> p c h n", c=2, h=4)[:, :, h]
                    if first:
                        ins = dve.tensor_copy(rs[rows], kv)
                    else:
                        ins = dve.scalar_tensor_tensor(out=rs[rows], in0=rs[rows], scalar=cst[rows, C_GCH:C_GCH + 1],
                                                       in1=kv, op0=ALU.mult, op1=ALU.add)
                ins.then_inc(s_r, 1)

            def low_state(i):
                dve.wait_ge(s_rh, i + 1)
                for h in range(H):
                    rows = slice(32 * h, 32 * h + 32)
                    ins = dve.tensor_tensor(rbl[rows, :, h], rs[rows], rbh[rows, :, h].bitcast(F32), ALU.subtract)
                ins.then_inc(s_rl, 1)

            def mean_squares(i):
                dve.wait_ge(s_rsq, i + 1)
                dve.tensor_reduce(small[:, 12:16], rsq, AX.X, ALU.add).then_inc(s_ra, 1)
                dve.wait_ge(s_ra, 4 * i + 1)
                dve.tensor_tensor(small[:, 56:60], small[:, 12:16], cst[:, C_XI2:C_XI2 + 4], ALU.mult).then_inc(s_ra, 1)
                dve.wait_ge(s_ra, 4 * i + 2)
                dve.tensor_scalar(small[:, 4:8], small[:, 56:60], EPS, None, ALU.add).then_inc(s_rms, 1)

            def normalize(i, par, first=False):
                dve.wait_ge(s_rroot, i + 1)
                dve.reciprocal(small[:, 12:16], small[:, 8:12]).then_inc(s_ra, 1)
                dve.wait_ge(s_ra, 4 * i + 3)
                dve.tensor_tensor(small[:, 60:64], small[:, 12:16], cst[:, C_XI:C_XI + 4], ALU.mult).then_inc(s_ra, 1)
                dve.wait_ge(s_ra, 4 * i + 4)
                if not first:
                    dve.wait_ge(s_ytr, i)
                dve.tensor_tensor(on, bank(1 if par else 6).rearrange("p (h n) -> p h n", h=4),
                                  small[:, 60:64].unsqueeze(2).to_broadcast([P, 4, P]), ALU.mult).then_inc(s_on, 1)

            def retention_gate(i, at):
                dve.wait_ge(s_ytr, i + 1)
                dve.tensor_tensor(y[:, 0:4, at], bank(7).rearrange("p (h n) -> p h n", h=4), pa[:, 8:12, at], ALU.mult).then_inc(s_y, 1)

            def retention_step(i, par, at, second=False):
                decayed_scores(i)
                low_state(i - 1)
                low_scores(i)
                mean_squares(i - 1)
                low_queries(i + 1, 1 - par)
                decayed_keys(i + 1)
                low_values(i + 1, 1 - par)
                normalize(i - 1, 1 - par, second)
                state(i, False)
                low_keys(i + 1)
                retention_gate(i - 1, at)

            dve.wait_ge(s_mm, N["win"] + 24)
            dve.memset(qbh[:].bitcast(F32), 0.0).then_inc(s_zero2, 1)
            dve.wait_ge(s_sg, 1)
            low_queries(0, 0)
            decayed_keys(0)
            low_values(0, 0)
            low_keys(0)
            decayed_scores(0)
            low_scores(0)
            low_queries(1, 1)
            decayed_keys(1)
            low_values(1, 1)
            state(0, True)
            low_keys(1)
            dve.wait_ge(s_zero, 2)
            retention_step(1, 1, slice(0, P), True)
            retention_step(2, 0, slice(P, 2 * P))
            with dve.Fori(1, 3) as i:
                retention_step(2 * i + 1, 1, bass.ds(i * (2 * P), P))
                retention_step(2 * i + 2, 0, bass.ds(i * (2 * P) + P, P))
            decayed_scores(TT - 1)
            low_state(TT - 2)
            low_scores(TT - 1)
            mean_squares(TT - 2)
            normalize(TT - 2, 0)
            retention_gate(TT - 2, slice((TT - 2) * P, (TT - 1) * P))
            mean_squares(TT - 1)

            def maximum(i, t, c):
                k = 2 * (8 * i + t) + c
                col = 2 * (t % 2) + c
                dve.wait_ge(s_s, k + 1)
                dve.tensor_reduce(small[:, 52 + c:53 + c], ps[:, c, 0:(t + 1) * P], AX.X, ALU.max).then_inc(s_mx, 1)
                dve.wait_ge(s_mx, k + 1)
                dve.tensor_scalar(small[:, 16 + col:17 + col], small[:, 52 + c:53 + c], -DIFF_SCALE, None, ALU.mult).then_inc(s_nm, 1)

            def combine(i, t):
                g = 8 * i + t
                e0, e1 = (x[:, 0:(t + 1) * P] for x in e[t % 2])
                sum0 = small[:, 20 + 2 * (t % 2):21 + 2 * (t % 2)]
                dve.wait_ge(s_exp, 2 * g + 4)
                dve.reciprocal(small[:, 48:50], small[:, 20 + 2 * (t % 2):22 + 2 * (t % 2)]).then_inc(s_da, 1)
                dve.wait_ge(s_da, 3 * g + 1)
                dve.scalar_tensor_tensor(out=small[:, 50:51], in0=sum0, scalar=lamv[:, 1:2], in1=small[:, 49:50], op0=ALU.mult,
                                         op1=ALU.mult).then_inc(s_da, 1)
                dve.tensor_copy(small[:, t:t + 1], small[:, 48:49]).then_inc(s_da, 1)
                dve.wait_ge(s_da, 3 * g + 3)
                dve.scalar_tensor_tensor(out=e1, in0=e1, scalar=small[:, 50:51], in1=e0, op0=ALU.mult, op1=ALU.add).then_inc(s_a, 1)

            def keep_sums(i):
                dve.tensor_copy(small[:, 56:64], small[:, 0:8])
                dve.tensor_tensor(small[:, 8:16], small[:, 0:8], small[:, 0:8], ALU.mult).then_inc(s_dn, 1)

            def split_weights(g, t):
                dve.wait_ge(s_pth, g + 1)
                dve.tensor_tensor(ptl[:, t % 4, 0:t + 1].rearrange("p t n -> p (t n)"), ps[:, 2, 0:(t + 1) * P],
                                  pth[:, t % 4, 0:t + 1].rearrange("p t n -> p (t n)").bitcast(F32), ALU.subtract).then_inc(s_ptl, 1)

            def add_output(g, t):
                o = bank(6 + t % 2)
                at_t = slice(t * P, (t + 1) * P)
                dve.wait_ge(s_pv, g + 1)
                dve.tensor_copy(raw_out[:, at_t], o[:, P:2 * P]).then_inc(s_oc, 1)
                dve.wait_ge(s_oc, g + 1)
                dve.tensor_tensor(raw_out[:, at_t], raw_out[:, at_t], o[:, 0:P], ALU.add).then_inc(s_oadd, 1)

            def mean_square(i):
                dve.wait_ge(s_dsq, i + 1)
                dve.tensor_reduce(small[:, 40:48], turned[:].rearrange("p (t n) -> p t n", t=TT), AX.X, ALU.add).then_inc(s_dn, 1)
                dve.wait_ge(s_dn, 5 * i + 2)
                dve.scalar_tensor_tensor(out=small[:, 40:48], in0=small[:, 40:48], scalar=1.0 / P, in1=small[:, 8:16], op0=ALU.mult,
                                         op1=ALU.mult).then_inc(s_dn, 1)
                dve.wait_ge(s_dn, 5 * i + 3)
                dve.tensor_scalar(small[:, 24:32], small[:, 40:48], EPS, None, ALU.add).then_inc(s_dms, 1)

            def normalize_output(i):
                dve.wait_ge(s_droot, i + 1)
                dve.reciprocal(small[:, 40:48], small[:, 32:40]).then_inc(s_dn, 1)
                dve.wait_ge(s_dn, 5 * i + 4)
                dve.tensor_tensor(small[:, 40:48], small[:, 40:48], small[:, 56:64], ALU.mult).then_inc(s_dn, 1)
                dve.wait_ge(s_dn, 5 * i + 5)
                dve.tensor_tensor(turned[:].rearrange("p (t n) -> p t n", t=TT), raw_out[:].rearrange("p (t n) -> p t n", t=TT),
                                  small[:, 40:48].unsqueeze(2).to_broadcast([P, TT, P]), ALU.mult).then_inc(s_don, 1)
                dve.wait_ge(s_don, i + 1)

            def split_keys(i, first=False):
                dve.wait_ge(s_dqh, 2 * i + 1)
                dve.tensor_tensor(dql[:], pa_f[:, span(i * S + 12 * S, S)], dqh[:].bitcast(F32), ALU.subtract)
                if first:
                    normalize(TT - 1, 1)
                dve.wait_ge(s_dqh, 2 * i + 2)
                dve.tensor_tensor(dkl[:], pb_f[:, span(i * S, S)], dkh[:].bitcast(F32), ALU.subtract).then_inc(s_dql, 1)

            def head(i, first, last=False):
                if first:
                    split_keys(0, True)
                if not first:
                    split_weights(8 * i - 1, TT - 1)
                maximum(i, 0, 0)
                maximum(i, 0, 1)
                if first:
                    retention_gate(TT - 1, slice((TT - 1) * P, TT * P))
                else:
                    add_output(8 * i - 2, TT - 2)
                combine(i, 0)
                maximum(i, 1, 0)
                if not first:
                    add_output(8 * i - 1, TT - 1)
                dve.wait_ge(s_dvh, i + 1)
                dve.tensor_tensor(dv[:, :, 1], ps[:, 2].rearrange("p (t n) -> p t n", t=TT), dv[:, :, 0].bitcast(F32),
                                  ALU.subtract).then_inc(s_dvl, 1)
                maximum(i, 1, 1)
                for t in range(1, TT):
                    if t == TT - 1 and not last:
                        split_keys(i + 1)
                    split_weights(8 * i + t - 1, t - 1)
                    if t + 1 < TT:
                        maximum(i, t + 1, 0)
                    combine(i, t)
                    if t + 1 < TT:
                        maximum(i, t + 1, 1)
                    if not first:
                        if t == 1:
                            mean_square(i - 1)
                        if t == 2:
                            normalize_output(i - 1)
                    if t >= 2:
                        add_output(8 * i + t - 2, t - 2)
                dve.wait_ge(s_da, 3 * (8 * i + TT))
                keep_sums(i)

            dve.sem_inc(s_oadd, 2)
            head(0, True)
            with dve.Fori(1, H - 1) as i:
                head(i, False)
            head(H - 1, False, True)
            split_weights(8 * H - 1, TT - 1)
            add_output(8 * H - 2, TT - 2)
            add_output(8 * H - 1, TT - 1)

            def split_mixed(k):
                dve.wait_ge(s_yhi, k + 1)
                dve.scalar_tensor_tensor(out=r1l[:, k], in0=y[:, k], scalar=ygain[:, k:k + 1], in1=r1h[:, k].bitcast(F32),
                                         op0=ALU.mult, op1=ALU.subtract).then_inc(s_ylo, 1)

            mean_square(H - 1)
            split_mixed(0)
            split_mixed(1)
            normalize_output(H - 1)
            for k in range(2, KT - 1):
                split_mixed(k)
            split_mixed(KT - 1)
            dve.wait_ge(s_msq, MT)
            dve.tensor_scalar(small[:, 2:4], small[:, 0:2], 1.0 / D, EPS, ALU.mult, ALU.add).then_inc(s_mms, 1)
            dve.wait_ge(s_mroot, 1)
            link(dve.reciprocal(small[:, 6:8], small[:, 4:6]))
            for t in range(MT):
                ins = dve.tensor_scalar(memr[:, t], memr[:, t], small[:, 6 + t:7 + t], None, ALU.mult)
            ins.then_inc(s_mn, 1)
            dve.wait_ge(s_reload, 16)
            for m in range(KT):
                step(N["wout"] + m, U["wout"] + m, m % 2)
                residual_add(N["wout"] + m, m, 1.0)
                split_residual(R_WOUT, m, r0h, r0l, gain[:, G_X:G_X + KT])
            def split_memory():
                for q in range(2):
                    n = N["memt"] + q
                    for k in range(4):
                        f = 4 * q + k
                        dve.wait_ge(s_mhi, 4 * q + 4)
                        ins = dve.scalar_tensor_tensor(out=meml[:, f], in0=ps[:, n % 4, k * M:(k + 1) * M], scalar=gain[:, G_MEM + f:G_MEM + f + 1],
                                                       in1=memh[:, f].bitcast(F32), op0=ALU.mult, op1=ALU.subtract)
                    ins.then_inc(s_evac, 1)

            for m in range(KT):
                n = N["wq"] + m
                step(n, U["wq"] + m, m % 2)
                if m == 0:
                    factors(N["wq"], rstd)
                dve.tensor_tensor(T1, ps[:, n % 4], rstd[:], ALU.mult).then_inc(s_evac, 1)
                if m == KT - 1:
                    split_memory()
                dve.wait_ge(s_qh, m + 1)
                dve.tensor_tensor(r1l[:, m], T1, r1h[:, m].bitcast(F32), ALU.subtract).then_inc(s_ql, 1)
                dve.wait_ge(s_ql, m + 1)

            for m in range(2 * KT):
                n = N["wkv"] + m
                step(n, U["wkv"] + m, m % 2)
                if m < KT:
                    dve.wait_ge(s_khi, m + 1)
                    dve.tensor_tensor(kxl[:, m], ps[:, n % 4, 0:M], kxh[:, m].bitcast(F32), ALU.subtract).then_inc(s_evac, 1)
                else:
                    dve.tensor_copy(vf[:, m - KT], ps[:, n % 4, 0:M]).then_inc(s_evac, 1)
            for t in range(MT):
                dve.wait_ge(s_vxh, t + 1)
                dve.tensor_tensor(vxl[:, t], ps[:, 1 + t], vxh[:, t].bitcast(F32), ALU.subtract).then_inc(s_evac, 1)

            def xmax(i, par):
                dve.wait_ge(s_xs, i + 1)
                dve.tensor_reduce(small[:, 52:56], ps[:, 3 * par].rearrange("p (h n) -> p h n", h=H), AX.X, ALU.max).then_inc(s_xa, 1)
                dve.wait_ge(s_xa, 2 * i + 1)
                dve.tensor_scalar(small[:, 16:20], small[:, 52:56], -XATTN_SCALE, None, ALU.mult).then_inc(s_xnm, 1)

            def xnorm(i, par):
                dve.wait_ge(s_xe, i + 1)
                dve.reciprocal(small[:, 48:52], small[:, 20:24]).then_inc(s_xa, 1)
                dve.wait_ge(s_xa, 2 * i + 2)
                v = ex[par].rearrange("p (h n) -> p h n", h=H)
                dve.tensor_tensor(v, v, small[:, 48:52].unsqueeze(2).to_broadcast([P, H, M]), ALU.mult).then_inc(s_xn, 1)

            def xweights(i, par):
                dve.wait_ge(s_xph, i + 1)
                dve.tensor_tensor(pxl[:, par].rearrange("p k n -> p (k n)"), ps[:, 1],
                                  pxh[:, par].rearrange("p k n -> p (k n)").bitcast(F32), ALU.subtract).then_inc(s_xpl, 1)

            def xout(i, at, slot=2):
                dve.wait_ge(s_xy, i + 1)
                dve.tensor_tensor(r1l[:, :, at], ps[:, slot].rearrange("p (k n) -> p k n", k=KT), r1h[:, :, at].bitcast(F32),
                                  ALU.subtract).then_inc(s_xyl, 1)

            xmax(0, 0)
            xnorm(0, 0)
            xmax(1, 1)
            xweights(0, 0)
            xnorm(1, 1)
            xmax(2, 0)
            xweights(1, 1)
            xnorm(2, 0)
            xout(0, slice(0, P))
            with dve.Fori(1, TT // 2 - 1) as i:
                for par in range(2):
                    xmax(2 * i + (par + 1), 1 - par)
                    xweights(2 * i + par, par)
                    xnorm(2 * i + (par + 1), 1 - par)
                    xout(2 * i + (par - 1), bass.ds(i * (2 * P) + (par - 1) * P, P))
            xmax(TT - 1, 1)
            xweights(TT - 2, 0)
            xnorm(TT - 1, 1)
            xout(TT - 3, slice((TT - 3) * P, (TT - 2) * P))
            xweights(TT - 1, 1)
            xout(TT - 2, slice((TT - 2) * P, (TT - 1) * P), 0)
            xout(TT - 1, slice((TT - 1) * P, TT * P), 3)
            for m in range(KT):
                step(N["wo"] + m, U["wo"] + m, m % 2)
                residual_add(N["wo"] + m, m, 1.0)
                split_residual(R_WO, m, r0h, r0l, gain[:, G_FFN2:G_FFN2 + KT])
            ffn("ffn2", r1h, r1l, FT, lambda m: split_residual(R_FFN2, m, r0h, r0l, gain2, True))

            def pool_factors():
                n0 = N["pool_u"]
                dve.wait_ge(s_stat, 5)
                dve.tensor_scalar(rfin[:], ps[:, (n0 + 3) % 4], 1.0 / D, EPS, ALU.mult, ALU.add).then_inc(s_ms, 1)
                dve.wait_ge(s_stat, 6)
                dve.tensor_scalar(T3, ps[:, (n0 + 2) % 4], 1.0 / D, None, ALU.mult).then_inc(s_ms, 1)
                dve.wait_ge(s_ms, 6)
                dve.scalar_tensor_tensor(out=T1, in0=rfin[:], scalar=EPS, in1=T3, op0=ALU.mult, op1=ALU.add).then_inc(s_ms2, 1)
                inverse(rstd)

            for t in range(KT):
                n = N["pool_u"] + t
                g = t // 2
                window = 2 << g
                if t == 0:
                    step(n, U["pool_u"], 0)
                    pool_factors()
                else:
                    step(n, U["pool_u"] + t, t % 2)
                dve.tensor_tensor(T1, ps[:, n % 4], rstd[:], ALU.mult).then_inc(s_evac, 1)
                dve.wait_ge(s_evac, n + 1)
                src, dst, other = t1, t2, t3
                for k in range(g + 1):
                    sh = 1 << k
                    link(dve.tensor_tensor(dst[:, PAD:], src[:, PAD:], src[:, PAD - sh:PAD - sh + S], ALU.add))
                    src, dst, other = dst, (t3 if dst is t2 else t2), None
                head = slice(PAD, 2 * PAD)
                rest = slice(2 * PAD, PAD + S)
                dve.scalar_tensor_tensor(out=dst[:, rest], in0=src[:, rest], scalar=1.0 / window, in1=t1[:, rest],
                                         op0=ALU.mult, op1=ALU.subtract)
                link(dve.tensor_tensor(small[:, 0:PAD], src[:, head], cst[:, C_INV + 16 * g:C_INV + 16 * (g + 1)], ALU.mult))
                dve.tensor_tensor(dst[:, head], small[:, 0:PAD], t1[:, head], ALU.subtract).then_inc(s_pd, 1)
                dve.wait_ge(s_phi, t + 1)
                dve.tensor_tensor(r1l[:, t], dst[:, PAD:], r1h[:, t].bitcast(F32), ALU.subtract).then_inc(s_plo, 1)
            for g in range(4):
                n, u = N["pool_g"] + 4 * g, U["pool_g"] + 4 * g
                for j in range(2):
                    step(n + j, u + j, j)
                    dve.tensor_tensor((T1, T2)[j], ps[:, (n + j) % 4], rstd[:], ALU.mult).then_inc(s_evac, 1)
                for j in range(2):
                    f = 2 * g + j
                    step(n + 2 + j, u + 2 + j, j)
                    dve.tensor_scalar(T3, ps[:, (n + 2 + j) % 4], gain[:, G_PB + f:G_PB + f + 1], gain[:, G_PS + f:G_PS + f + 1],
                                      ALU.add, ALU.mult).then_inc(s_evac, 1)
                    dve.wait_ge(s_evac, n + 3 + j)
                    dve.wait_ge(s_psilu, f + 1)
                    dve.tensor_tensor(T3, T3, (T1, T2)[j], ALU.mult).then_inc(s_yy, 1)
                    dve.wait_ge(s_phi, KT + f + 1)
                    dve.tensor_tensor(r1l[:, f], T3, r1h[:, f].bitcast(F32), ALU.subtract).then_inc(s_plo, 1)
            inverse(rfin, rfin[:])
            n = N["fgain"]
            dve.wait_ge(s_mm, n + 1)
            dve.tensor_copy(fgain[:], ps[:, n % 4]).then_inc(s_evac, 1)
            for m in range(KT):
                n = N["pool_out"] + m
                x1 = (T1, T3)[m % 2]
                link(dve.scalar_tensor_tensor(out=x1, in0=xt[:, m], scalar=gain[:, G_FIN + m:G_FIN + m + 1], in1=rfin[:],
                                              op0=ALU.mult, op1=ALU.mult))
                step(n, U["pool_out"] + m, m % 2)
                dve.tensor_tensor(xt[:, m], x1, ps[:, n % 4], ALU.add).then_inc(s_evac, 1)
            def mean_of_row(t):
                dve.wait_ge(s_fsq, t + 1)
                dve.tensor_scalar(small[:, 8 + t:9 + t], small[:, t:t + 1], 1.0 / D, EPS, ALU.mult, ALU.add).then_inc(s_fms, 1)

            for t in range(TT):
                if t == 0:
                    mean_of_row(0)
                if t + 1 < TT:
                    mean_of_row(t + 1)
                n = N["final"] + t
                dve.wait_ge(s_froot, t + 1)
                link(dve.reciprocal(small[:, 24 + t:25 + t], small[:, 16 + t:17 + t]))
                if t >= 4:
                    dve.wait_ge(s_out[t % 4], 16 * (t // 4))
                dve.scalar_tensor_tensor(out=outrow[t % 4], in0=ps[:, n % 4], scalar=small[:, 24 + t:25 + t], in1=fgain[:],
                                         op0=ALU.mult, op1=ALU.mult).then_inc(s_evac, 1)

        @block.gpsimd
        def _(pool):
            cos, sin = (lambda i, t=t: t[:, bass.ds(i * P, P)].unsqueeze(1).to_broadcast([P, 2, P]) for t in (rcos, rsin))

            def retention_chunk(i, first):
                at_i = bass.ds(i * P, P)
                left, right = pa[:, 0:4:2, at_i], pa[:, 1:4:2, at_i]
                if not first:
                    pool.wait_ge(s_qkl, i)
                    pool.wait_ge(s_ktr, i)
                for k, (half, table) in enumerate(((left, cos), (right, sin), (left, sin), (right, cos))):
                    pool.tensor_tensor(rtmp[k], half, table(i), ALU.mult).then_inc(s_pool, 1)
                pool.wait_ge(s_pool, 4 * i + 4)
                pool.tensor_tensor(qk[:, 0:4:2], rtmp[0], rtmp[1], ALU.subtract)
                pool.tensor_tensor(qk[:, 1:4:2], rtmp[2], rtmp[3], ALU.add)
                pool.tensor_copy(vc, pa[:, 4:8, at_i]).then_inc(s_rotd, 1)

            pool.wait_ge(s_rot, 32)
            pool.wait_ge(s_evac, N["win"] + 8)
            retention_chunk(0, True)
            pool.wait_ge(s_mm, N["win"] + 24)
            pool.memset(qbl[:].bitcast(F32), 0.0).then_inc(s_zero, 1)
            pool.memset(rbh[:].bitcast(F32), 0.0)
            pool.memset(rbl[:].bitcast(F32), 0.0).then_inc(s_zero, 1)
            with pool.Fori(1, TT) as i:
                retention_chunk(i, False)

            pool.tensor_copy(T3, pb[:, 4]).then_inc(s_vt, 1)
            with pool.Fori(1, H) as i:
                pool.wait_ge(s_dvtr, i)
                pool.tensor_copy(T3, pb_f[:, bass.ds(i * S + 4 * S, S)]).then_inc(s_vt, 1)

            def query_tile(i, par, at, first):
                if not first:
                    pool.wait_ge(s_xs, i - 1)
                pool.tensor_copy(qsh[:, par], r1h[:, :, at])
                pool.tensor_copy(qsl[:, par], r1l[:, :, at]).then_inc(s_qc, 1)

            pool.wait_ge(s_ql, KT)
            pool.wait_ge(s_mm, N["wq"] + KT)
            query_tile(0, 0, slice(0, P), True)
            query_tile(1, 1, slice(P, 2 * P), True)
            with pool.Fori(1, TT // 2) as i:
                for par in range(2):
                    query_tile(2 * i + par, par, bass.ds(i * (2 * P) + par * P, P), False)


_INS = ["x", "mem", "ffn1_norm", "ffn1_w_gate", "ffn1_w_up", "ffn1_w_down", "mix_norm", "w_in", "ret_out_norm",
        "diff_lq1", "diff_lk1", "diff_lq2", "diff_lk2", "diff_out_norm", "w_out", "xattn_norm", "mem_norm",
        "xattn_wq", "xattn_wkv", "xattn_wo", "ffn2_norm", "ffn2_w_gate", "ffn2_w_up", "ffn2_w_down", "final_norm",
        "norm_w_2", "pool_in_w_2", "pool_group_w_2", "pool_group_b_2", "pool_scale_2", "pool_out_w_2", "final_norm_w_2"]


def kernel(**inputs):
    import concourse.bacc as bacc
    from concourse.bass_utils import run_bass_kernel_spmd

    nc = bacc.Bacc("TRN2", target_bir_lowering=False, num_devices=1, dynamic_dma_scratch_size=1024)
    arrays = {name: np.ascontiguousarray(inputs[name]) for name in _INS}
    arrays["constants"] = constants()
    arrays["rotary"] = rotary_tables()
    aps = {name: nc.dram_tensor("in_" + name, v.shape, mybir.dt.from_np(v.dtype), kind="ExternalInput").ap()
           for name, v in arrays.items()}
    spill = nc.dram_tensor("spill", (P, KT, S), F32, kind="Internal").ap()
    out = nc.dram_tensor("out_0", (1, S, D), F32, kind="ExternalOutput").ap()
    build(nc, aps, aps["constants"], aps["rotary"], spill, out)
    r = run_bass_kernel_spmd(nc, [{"in_" + k: v for k, v in arrays.items()}], core_ids=[0])
    return r.results[0]["out_0"]
```
